# Optimizing a Trainium2 kernel written in Bass

```python
import math
import jax, jax.numpy as jnp
from jax import lax
import numpy as np

D_MODEL = 1024
BATCH = 1
SEQ = 256
DEPTH = 2

ATTN_HEAD_DIM = 64
ATTN_HEADS = D_MODEL // 256
ATTN_V_DIM = 2 * ATTN_HEAD_DIM
ATTN_QK_WIDTH = ATTN_HEADS * 2 * ATTN_HEAD_DIM
ATTN_V_WIDTH = ATTN_HEADS * ATTN_V_DIM
Q_BLOCK = 128
ROPE_THETA = 10000.0

SSM_GROUP_CH = 16
SSM_GROUPS = D_MODEL // 32
SSM_WIDTH = SSM_GROUPS * SSM_GROUP_CH
SSM_STATE = 64
SSM_DT_MIN = 1e-3
SSM_DT_MAX = 1e-1

N_BRANCHES = 2
OFF_K = ATTN_QK_WIDTH
OFF_V = OFF_K + ATTN_QK_WIDTH
OFF_U = OFF_V + ATTN_V_WIDTH
OFF_G = OFF_U + SSM_WIDTH
IN_WIDTH = OFF_G + N_BRANCHES * D_MODEL

D_FF = 256 * ((8 * D_MODEL // 3 + 255) // 256)
N_EXPERTS = 8
TOP_K = 2
MOE_BLOCK = 256
RMS_EPS = 1e-6

kernel_name = "hybrid_diffattn_s5_moe_encoder"

def rms_norm(x, g):
    xf = x.astype(jnp.float32)
    y = xf * lax.rsqrt(jnp.mean(xf * xf, axis=-1, keepdims=True) + RMS_EPS)
    return (y * g.astype(jnp.float32)).astype(x.dtype)

def rotary(x, positions):
    half = ATTN_HEAD_DIM // 2
    inv_freq = 1.0 / (ROPE_THETA ** (jnp.arange(half, dtype=jnp.float32) / half))
    ang = positions.astype(jnp.float32)[:, None] * inv_freq[None, :]
    cos = jnp.cos(ang)[:, None, None, :]
    sin = jnp.sin(ang)[:, None, None, :]
    xf = x.astype(jnp.float32)
    x1, x2 = xf[..., :half], xf[..., half:]
    return jnp.concatenate([x1 * cos - x2 * sin, x2 * cos + x1 * sin], axis=-1).astype(x.dtype)

def diff_attention(q, k, v, lam):
    bsz, seq = q.shape[0], q.shape[1]
    n_blocks = seq // Q_BLOCK
    scale = ATTN_HEAD_DIM ** -0.5
    qb = jnp.moveaxis(q.reshape(bsz, n_blocks, Q_BLOCK, ATTN_HEADS, 2, ATTN_HEAD_DIM), 1, 0)

    def one_block(q_blk):
        s = jnp.einsum('bqhcd,bkhcd->bhcqk', q_blk, k,
                       preferred_element_type=jnp.float32) * scale
        p = jax.nn.softmax(s, axis=-1)
        w = p[:, :, 0] - lam * p[:, :, 1]
        return jnp.einsum('bhqk,bkhe->bqhe', w.astype(v.dtype), v)

    o = lax.map(one_block, qb)
    return jnp.moveaxis(o, 0, 1).reshape(bsz, seq, ATTN_HEADS, ATTN_V_DIM)

def _linear_recurrence_combine(left, right):
    a_l, b_l = left
    a_r, b_r = right
    return a_r * a_l, a_r * b_l + b_r

def s5_bidirectional(u, lam_re, lam_im, log_dt, b_re, b_im, c_re, c_im, d_skip):
    bsz, seq, _ = u.shape
    uf = u.astype(jnp.float32).reshape(bsz, seq, SSM_GROUPS, SSM_GROUP_CH)
    uc = uf.astype(jnp.complex64)
    y = uf * d_skip.astype(jnp.float32).reshape(SSM_GROUPS, SSM_GROUP_CH)
    for direction in range(2):
        lam = lax.complex(lam_re[direction].astype(jnp.float32),
                          lam_im[direction].astype(jnp.float32))
        dt = jnp.exp(log_dt[direction].astype(jnp.float32))[:, None]
        a_bar = jnp.exp(lam * dt)
        b_mat = lax.complex(b_re[direction].astype(jnp.float32),
                            b_im[direction].astype(jnp.float32))
        b_bar = ((a_bar - 1.0) / lam)[..., None] * b_mat
        bu = jnp.einsum('gph,bsgh->bsgp', b_bar, uc)
        a_seq = jnp.broadcast_to(a_bar, bu.shape)
        _, states = lax.associative_scan(_linear_recurrence_combine, (a_seq, bu),
                                         reverse=(direction == 1), axis=1)
        c_mat = lax.complex(c_re[direction].astype(jnp.float32),
                            c_im[direction].astype(jnp.float32))
        y = y + jnp.real(jnp.einsum('ghp,bsgp->bsgh', c_mat, states))
    return y.reshape(bsz, seq, SSM_WIDTH)

def swiglu(h, w1, w3, w2):
    return (jax.nn.silu(h @ w1) * (h @ w3)) @ w2

def moe_swiglu(h, w_router, w1, w3, w2):
    bsz, seq, d = h.shape
    t = h.reshape(-1, d)
    n_tok = t.shape[0]
    logits = jnp.dot(t, w_router, preferred_element_type=jnp.float32)
    top_logit, top_idx = lax.top_k(logits, TOP_K)
    gate = jax.nn.softmax(top_logit, axis=-1)
    n_assign = n_tok * TOP_K
    flat_e = top_idx.reshape(-1)
    order = jnp.argsort(flat_e)
    sorted_e = flat_e[order]
    sorted_tok = order // TOP_K
    sorted_gate = gate.reshape(-1)[order]
    counts = jnp.bincount(flat_e, length=N_EXPERTS)
    padded = (counts + MOE_BLOCK - 1) // MOE_BLOCK * MOE_BLOCK
    pad_end = jnp.cumsum(padded)
    pad_start = pad_end - padded
    grp_start = jnp.cumsum(counts) - counts
    dest = pad_start[sorted_e] + jnp.arange(n_assign) - grp_start[sorted_e]
    n_slots = ((n_assign + MOE_BLOCK - 1) // MOE_BLOCK) * MOE_BLOCK + N_EXPERTS * MOE_BLOCK
    slot_tok = jnp.zeros((n_slots,), jnp.int32).at[dest].set(sorted_tok.astype(jnp.int32))
    slot_gate = jnp.zeros((n_slots,), jnp.float32).at[dest].set(sorted_gate)
    n_blocks = n_slots // MOE_BLOCK
    block_start = jnp.arange(n_blocks) * MOE_BLOCK
    block_exp = jnp.minimum(jnp.searchsorted(pad_end, block_start, side='right'), N_EXPERTS - 1)
    xb = t[slot_tok].reshape(n_blocks, MOE_BLOCK, d)

    def expert_block(args):
        x_blk, e = args
        return (jax.nn.silu(x_blk @ w1[e]) * (x_blk @ w3[e])) @ w2[e]

    yb = lax.map(expert_block, (xb, block_exp)).reshape(n_slots, d)
    y = jnp.zeros_like(t).at[slot_tok].add(yb * slot_gate[:, None].astype(yb.dtype))
    return y.reshape(bsz, seq, d)

def setup_inputs(seed: int = 0) -> dict:
    key = jax.random.key(seed)
    ks = iter(jax.random.split(key, 40))
    f32 = jnp.float32
    n_dense = (DEPTH + 1) // 2
    n_moe = DEPTH // 2

    def nrm(shape, scale):
        return jax.random.normal(next(ks), shape, f32) * scale

    def gain(shape):
        return 1.0 + nrm(shape, 0.02)

    ssm_p = (DEPTH, 2, SSM_GROUPS, SSM_STATE)
    n_idx = jnp.arange(SSM_STATE, dtype=f32)
    return {
        "x": nrm((BATCH, SEQ, D_MODEL), 1.0),
        "norm_mix": gain((DEPTH, D_MODEL)),
        "w_in": nrm((DEPTH, D_MODEL, IN_WIDTH), D_MODEL ** -0.5),
        "attn_lambda": nrm((DEPTH, 4, ATTN_HEAD_DIM), 0.1),
        "attn_subln": gain((DEPTH, ATTN_V_DIM)),
        "ssm_lam_re": -0.5 + nrm(ssm_p, 0.01),
        "ssm_lam_im": math.pi * n_idx + nrm(ssm_p, 0.01),
        "ssm_log_dt": jax.random.uniform(next(ks), (DEPTH, 2, SSM_GROUPS), f32,
                                         math.log(SSM_DT_MIN), math.log(SSM_DT_MAX)),
        "ssm_b_re": nrm((DEPTH, 2, SSM_GROUPS, SSM_STATE, SSM_GROUP_CH), (2 * SSM_GROUP_CH) ** -0.5),
        "ssm_b_im": nrm((DEPTH, 2, SSM_GROUPS, SSM_STATE, SSM_GROUP_CH), (2 * SSM_GROUP_CH) ** -0.5),
        "ssm_c_re": nrm((DEPTH, 2, SSM_GROUPS, SSM_GROUP_CH, SSM_STATE), (2 * SSM_STATE) ** -0.5),
        "ssm_c_im": nrm((DEPTH, 2, SSM_GROUPS, SSM_GROUP_CH, SSM_STATE), (2 * SSM_STATE) ** -0.5),
        "ssm_d": nrm((DEPTH, SSM_WIDTH), 1.0),
        "w_glu": nrm((DEPTH, SSM_WIDTH, SSM_WIDTH), SSM_WIDTH ** -0.5),
        "w_branch": nrm((DEPTH, N_BRANCHES, ATTN_V_WIDTH, D_MODEL), ATTN_V_WIDTH ** -0.5),
        "w_out": nrm((DEPTH, D_MODEL, D_MODEL), D_MODEL ** -0.5),
        "norm_ffn": gain((DEPTH, D_MODEL)),
        "ffn_w1": nrm((n_dense, D_MODEL, D_FF), D_MODEL ** -0.5),
        "ffn_w3": nrm((n_dense, D_MODEL, D_FF), D_MODEL ** -0.5),
        "ffn_w2": nrm((n_dense, D_FF, D_MODEL), D_FF ** -0.5),
        "moe_router": nrm((n_moe, D_MODEL, N_EXPERTS), D_MODEL ** -0.5),
        "moe_w1": nrm((n_moe, N_EXPERTS, D_MODEL, D_FF), D_MODEL ** -0.5),
        "moe_w3": nrm((n_moe, N_EXPERTS, D_MODEL, D_FF), D_MODEL ** -0.5),
        "moe_w2": nrm((n_moe, N_EXPERTS, D_FF, D_MODEL), D_FF ** -0.5),
        "norm_final": gain((D_MODEL,)),
    }

def reference(x, norm_mix, w_in, attn_lambda, attn_subln, ssm_lam_re, ssm_lam_im, ssm_log_dt,
              ssm_b_re, ssm_b_im, ssm_c_re, ssm_c_im, ssm_d, w_glu, w_branch, w_out, norm_ffn,
              ffn_w1, ffn_w3, ffn_w2, moe_router, moe_w1, moe_w3, moe_w2, norm_final):
    bsz, seq, _ = x.shape
    positions = jnp.arange(seq, dtype=jnp.int32)
    for layer in range(DEPTH):
        xn = rms_norm(x, norm_mix[layer])
        proj = xn @ w_in[layer]
        q = proj[..., :OFF_K].reshape(bsz, seq, ATTN_HEADS, 2, ATTN_HEAD_DIM)
        k = proj[..., OFF_K:OFF_V].reshape(bsz, seq, ATTN_HEADS, 2, ATTN_HEAD_DIM)
        v = proj[..., OFF_V:OFF_U].reshape(bsz, seq, ATTN_HEADS, ATTN_V_DIM)
        u = proj[..., OFF_U:OFF_G]
        gates = jax.nn.sigmoid(proj[..., OFF_G:].astype(jnp.float32)).reshape(
            bsz, seq, N_BRANCHES, D_MODEL)

        q = rotary(q, positions)
        k = rotary(k, positions)
        lam_init = 0.8 - 0.6 * math.exp(-0.3 * layer)
        lp = attn_lambda[layer].astype(jnp.float32)
        lam = jnp.exp(jnp.sum(lp[0] * lp[1])) - jnp.exp(jnp.sum(lp[2] * lp[3])) + lam_init
        a = diff_attention(q, k, v, lam)
        a = (rms_norm(a, attn_subln[layer]) * (1.0 - lam_init)).reshape(bsz, seq, ATTN_V_WIDTH)

        s = s5_bidirectional(u, ssm_lam_re[layer], ssm_lam_im[layer], ssm_log_dt[layer],
                             ssm_b_re[layer], ssm_b_im[layer], ssm_c_re[layer], ssm_c_im[layer],
                             ssm_d[layer]).astype(x.dtype)
        s = jax.nn.gelu(s, approximate=False)
        s = s * jax.nn.sigmoid(s @ w_glu[layer])

        merged = (gates[:, :, 0] * (a @ w_branch[layer, 0])
                  + gates[:, :, 1] * (s @ w_branch[layer, 1])).astype(x.dtype)
        x = x + merged @ w_out[layer]

        hn = rms_norm(x, norm_ffn[layer])
        if layer % 2 == 0:
            i = layer // 2
            f = swiglu(hn, ffn_w1[i], ffn_w3[i], ffn_w2[i])
        else:
            i = layer // 2
            f = moe_swiglu(hn, moe_router[i], moe_w1[i], moe_w3[i], moe_w2[i])
        x = x + f.astype(x.dtype)
    return rms_norm(x, norm_final)


_drawn_inputs = setup_inputs


def setup_inputs(seed=0):
    import zlib

    import numpy as np

    out = dict(_drawn_inputs(seed))
    spreads = {}
    factors = {}
    for name, (base, spread) in spreads.items():
        noise = np.random.default_rng([zlib.crc32(name.encode()), seed]).standard_normal(out[name].shape)
        drawn = base * np.exp(spread * noise) if base else spread * noise
        out[name] = __import__('jax').numpy.asarray(drawn.astype(out[name].dtype))
    for name, factor in factors.items():
        out[name] = (out[name] * factor).astype(out[name].dtype)
    return out
```

```python
import math
import concourse.bass as bass
from concourse import mybir
from contextlib import ExitStack

P = 128
SEQ, D = 256, 1024
TH = SEQ // P
KD = D // P
HEADS, HD = 4, 64
WA = HEADS * 2 * HD
NGATE = 2
IN_WIDTH = 4 * WA + NGATE * D
D_FF = 2816
NE = 8
MAXB = NE + 3
PAIRS, GC, NS = 16, 16, 64
EPS = 1e-6
TW = 2048
RAWS, SPLITS = 11, 3
FC = 256
NCH = D_FF // FC
MIX_TILES, FFN_TILES = 25, 3 * NCH
T_FFN0 = MIX_TILES
T_MIX1 = T_FFN0 + FFN_TILES
T_MOE = T_MIX1 + MIX_TILES
T_MIX = (0, T_MIX1)
C_ID, C_TRI, C_ONE, C_IOTA, C_MASK, C_PAT, C_COS, C_SIN = 0, 128, 256, 384, 512, 640, 672, 800
C_END = 928

W_IN_ORDER = [3, 0, 1, 2, 4, 5, 6, 7]


def ffn_order():
    order = [("a", 0), ("b", 0)]
    for c in range(NCH - 1):
        order += [("a", c + 1), ("b", c + 1), ("c", c)]
    return order + [("c", NCH - 1)]


FFN_ORDER = ffn_order()


def mixer_turns():
    names = ["par"]
    for l in range(2):
        names += [(l, "x", g) for g in range(4)] + [(l, "ct", g) for g in range(4)]
        names += [(l, "u", g) for g in range(2)] + [(l, "q", t) for t in range(2)] + [(l, "k", t) for t in range(2)]
        names += [(l, "b", g) for g in range(8)] + [(l, "cb", 0)]
        for s in range(9):
            if s < 8:
                names += [(l, "sc0", s), (l, "sc1", s)]
            if s > 0:
                names.append((l, "o", s - 1))
        names += [(l, "a", t) for t in range(2)] + [(l, "s", t) for t in range(2)] + [(l, "s2", t) for t in range(2)]
        names += [(l, "m", g) for g in range(4)] + [(l, "h", g) for g in range(4)]
    names += ["router", "pos"]
    return {name: n for n, name in enumerate(names)}


TURN = mixer_turns()
AT_ORDER = {name: n for n, name in enumerate(
    [("x", g) for g in range(4)] + [("a", t) for t in range(2)] + [("s", t) for t in range(2)]
    + [("s2", t) for t in range(2)] + [("m", g) for g in range(4)] + [("h", g) for g in range(4)])}
AT_PER_LAYER = len(AT_ORDER)
PJ_PER_LAYER = 15
LOOKAHEAD = 2


class Order:

    def __init__(self, eng, sem):
        self.eng, self.sem, self.n, self.turn, self.per = eng, sem, 0, None, 0

    def step(self, ins):
        ins.then_inc(self.sem, 1)
        self.n += 1
        self.eng.wait_ge(self.sem, self.n if self.turn is None else self.turn * self.per + self.n)

    def loop(self, turn, per):
        self.turn, self.per, self.start = turn, per, self.n

    def end(self, trips=None):
        assert self.n - self.start == self.per, (self.n - self.start, self.per)
        self.turn = None
        if trips is not None:
            self.n = self.start + trips * self.per


def build(nc, x, norm_mix, w_in, attn_lambda, attn_subln, ssm_lam_re, ssm_lam_im, ssm_log_dt, ssm_b_re, ssm_b_im,
          ssm_c_re, ssm_c_im, ssm_d, w_glu, w_branch, w_out, norm_ffn, ffn_w1, ffn_w3, ffn_w2, moe_router,
          moe_w1, moe_w3, moe_w2, norm_final, consts, out):
    f32, f32r, i32, u32 = mybir.dt.float32, mybir.dt.float32r, mybir.dt.int32, mybir.dt.uint32
    ACT, ALU, AX = mybir.ActivationFunctionType, mybir.AluOpType, mybir.AxisListType
    MUL, ADD, SUB = ALU.mult, ALU.add, ALU.subtract
    ctx = ExitStack()
    with ctx:
        def sb(name, shape, dt=f32):
            return ctx.enter_context(nc.sbuf_tensor(name, shape, dt))

        def sem(name):
            return ctx.enter_context(nc.semaphore(name))

        raw = sb("raw", [P, RAWS, TW])
        hi = sb("hi", [P, SPLITS, TW], f32r)
        lo = sb("lo", [P, SPLITS, TW], f32r)
        at_hi = sb("at_hi", [P, KD, SEQ], f32r)
        at_lo = sb("at_lo", [P, KD, SEQ], f32r)
        ht_hi = sb("ht_hi", [P, 2, SEQ], f32r)
        ht_lo = sb("ht_lo", [P, 2, SEQ], f32r)
        xres = sb("xres", [P, TH, D])
        gates = sb("gates", [P, TH, NGATE, D])
        qk = sb("qk", [P, 2, TH, WA])
        vreg = sb("vreg", [P, TH, WA])
        ureg = sb("ureg", [P, TH, WA])
        areg = sb("areg", [P, TH, WA])
        cst = sb("cst", [P, C_END])
        par = sb("par", [P, 7, 64])
        subln = sb("subln", [P, 2, P])
        small = sb("small", [P, 96])
        table = sb("table", [P, 4], i32)

        ident = cst[:, C_ID:C_ID + P]
        xn = qk[:, :, :, :].rearrange("p a t c -> p (a t c)").rearrange("p (t d) -> p t d", t=TH)
        gain = areg[:, :, :].rearrange("p t c -> p (t c)")
        gflat = gates[:, :, :, :].rearrange("p t g d -> p (t g d)")
        ssm = raw[:, 3:RAWS, :].rearrange("p s w -> p (s w)")

        def area(start, size):
            return ssm[:, start:start + size]
        bbt = area(0, 4096).rearrange("p (d r b c) -> p d r b c", d=2, r=2, b=8)
        cblk = area(4096, 4096).rearrange("p (k r d q g h) -> p k r d q g h", k=2, r=2, d=2, q=PAIRS, g=2)
        ut2 = area(8192, 1024).rearrange("p (b c) -> p b c", b=8)
        cbm = area(9216, 256).rearrange("p (b c) -> p b c", b=8)
        w1t = area(9472, 1024).rearrange("p (r j c) -> p r j c", r=2, c=16)
        w16t = area(10496, 512).rearrange("p (r j c) -> p r j c", r=2, c=8)
        TMP = 11008
        wtab = [area(TMP + 512 * i, 512).rearrange("p (r c) -> p r c", r=2) for i in range(2)]
        r2t = area(TMP + 1024, 256)
        rot1 = area(TMP + 1280, 512).rearrange("p (r c) -> p r c", r=2)
        rot2 = area(TMP + 1792, 512).rearrange("p (r c) -> p r c", r=2)
        zs = area(TMP + 2304, 512).rearrange("p (r c) -> p r c", r=2)
        po1 = area(TMP + 2816, 512).rearrange("p (r c) -> p r c", r=2)
        po2 = area(TMP + 3328, 512).rearrange("p (r c) -> p r c", r=2)
        xst = [area(TMP + 3840 + 516 * i, 516).rearrange("p (r d c) -> p r d c", r=2, d=2) for i in range(2)]

        def four(ap):
            return ap.rearrange("p (r j h) -> p r j h", r=2, h=GC)
        braw, bt1, bt2 = four(area(0, 1024)), four(area(1024, 1024)), four(area(2048, 1024))
        bbar, babar, ctr, cabar = [four(area(TMP + 1024 * i, 1024)) for i in range(4)]
        craw = [area(c0, 1024).rearrange("p (i a s) -> p i a s", i=8, a=2) for c0 in (8192, TMP + 4096)]
        bpre = gflat.rearrange("p (d r b q t g h) -> p d r b q t g h", d=2, r=2, b=8, q=2, t=2, g=2)

        banks = [ctx.enter_context(nc.psum_tensor(f"bank{i}", [P, 512], f32)) for i in range(8)]
        PJ, PY, PV, TR = banks[0:2], banks[2:4], banks[4:6], banks[6:8]

        raw_full = [sem(f"raw_full{i}") for i in range(RAWS)]
        hi_ready, lo_ready, tile_used = sem("hi_ready"), sem("lo_ready"), sem("tile_used")
        loads = sem("loads")
        rows_in = sem("rows_in")
        gain_in = sem("gain_in")
        bc_in = sem("bc_in")
        dskip_in = sem("dskip_in")
        sq_ready, var_ready, root_ready, xn_ready = sem("sq_ready"), sem("var_ready"), sem("root_ready"), sem("xn_ready")
        tr_full = sem("tr_full")
        tr_free = [sem("tr_free0"), sem("tr_free1")]
        at_hi_ready, at_lo_ready = sem("at_hi_ready"), sem("at_lo_ready")
        pj0_full = sem("pj0_full")
        pj_free = [sem("pj_free0"), sem("pj_free1")]
        dve_own, pool_own, act_own = sem("dve_own"), sem("pool_own"), sem("act_own")
        act_par, dve_par = sem("act_par"), sem("dve_par")
        rot_ready = sem("rot_ready")
        v_ready = sem("v_ready")
        mats_ready, blocks_ready, bbt_ready, cbm_ready = sem("mats_ready"), sem("blocks_ready"), sem("bbt_ready"), sem("cbm_ready")
        ct_ready, bzero_ready, small_tabs = sem("ct_ready"), sem("bzero_ready"), sem("small_tabs")
        pv_full, pv_free, wtab_ready, r2_ready = sem("pv_full"), sem("pv_free"), sem("wtab_ready"), sem("r2_ready")
        zs_ready, zs_used, states_ready, y_done = sem("zs_ready"), sem("zs_used"), sem("states_ready"), sem("y_done")
        max_ready, exp_ready, w_ready, wt_tr, wt_ready = sem("max_ready"), sem("exp_ready"), sem("w_ready"), sem("wt_tr"), sem("wt_ready")
        o_ready, avar_ready, aroot_ready, a_ready = sem("o_ready"), sem("avar_ready"), sem("aroot_ready"), sem("a_ready")
        s_ready, tg_ready, s2_ready, gate_ready, m_ready, x_added = (sem("s_ready"), sem("tg_ready"), sem("s2_ready"),
                                                                     sem("gate_ready"), sem("m_ready"), sem("x_added"))
        qk_t_ready, u_ready, lam_ready, lam_exp = sem("qk_t_ready"), sem("u_ready"), sem("lam_ready"), sem("lam_exp")
        h_full, g_ready, h_done, ht_tr, ht_hi_ready, ht_lo_ready = (sem("h_full"), sem("g_ready"), sem("h_done"), sem("ht_tr"),
                                                                    sem("ht_hi_ready"), sem("ht_lo_ready"))
        ffn_done = sem("ffn_done")
        sel_ready, pos_full, routed, final_ready, stored = (sem("sel_ready"), sem("pos_full"), sem("routed"),
                                                            sem("final_ready"), sem("stored"))
        gate_exp, router_in, place_ready, pg_full, gt_ready = (sem("gate_exp"), sem("router_in"), sem("place_ready"),
                                                               sem("pg_full"), sem("gt_ready"))
        xe_full, xe_hi_ready, xe_lo_ready, ye_ready, comb_full = (sem("xe_full"), sem("xe_hi_ready"), sem("xe_lo_ready"),
                                                                  sem("ye_ready"), sem("comb_full"))
        out_ready = sem("out_ready")
        def raw_slot(t):
            return t % 3

        def raw_uses(slot, before):
            return sum(1 for t in range(before) if raw_slot(t) == slot)

        def moe_slot(j):
            return (j + 3) % RAWS

        def moe_full_value(j, turn):
            s = moe_slot(j)
            base = raw_uses(s, T_MOE) if s < 3 else 0
            first = min(i for i in range(FFN_TILES) if moe_slot(i) == s)
            return turn * (32 * FFN_TILES // RAWS) + 32 * (base + (j - first) // RAWS + 1)

        SS, VAR, RT, RI, MX, NB, RS, RR, C1 = 0, 2, 4, 6, 8, 10, 12, 14, 16
        AS, AV, AR, AI, LSUM, LEXP, NLAM = 24, 32, 40, 48, 56, 60, 64

        def col(i, n=1):
            return small[:, i:i + n]

        def row(i, n=1):
            return gflat[0:64, i * P:(i + n) * P]
        lamv = gflat[:, 4 * P:8 * P].rearrange("p (l a b c) -> p l a b c", l=2, a=2, b=2)
        lamp = gflat[:, 26 * P:28 * P].rearrange("p (j c) -> p j c", c=HD)
        R_LR, R_LI, R_DT, R_EDT, R_lr, R_li, R_k, R_red, R_er, R_sn, R_sh, R_t, R_u, R_den, R_am = (
            0, 1, 2, 3, 8, 9, 10, 11, 12, 13, 14, 15, 23, 24, 25)
        PACK = 16
        A_RE, A_IM, CO_RE, CO_IM, COS, SIN, RAD2 = range(7)

        kflat = qk[:, 1, :, :].rearrange("p t c -> p (t c)")
        probs = kflat[:, 0:512].rearrange("p (a k) -> p a k", a=2)
        wdiff = kflat[:, 512:768]
        wdiff_t = kflat[:, 768:1024].rearrange("p (t q) -> p t q", t=2)
        u_rows = ureg[:, :, :].rearrange("p t c -> p (t c)").rearrange("p (q t c) -> p q t c", q=PAIRS, t=TH)
        u_flat = ureg[:, :, :].rearrange("p t c -> p (t c)")
        q_t = u_flat.rearrange("p (h s) -> p h s", h=HEADS)
        k_t = qk[:, 0, :, :].rearrange("p t c -> p (t c)").rearrange("p (h s) -> p h s", h=HEADS)
        s_act = ureg
        s_gated = qk[:, 0, :, :]
        a_flat = areg[:, :, :].rearrange("p t c -> p (t c)")
        v_flat = vreg[:, :, :].rearrange("p t c -> p (t c)")

        free_at, seen = {}, [0, 0]
        for name, n in TURN.items():
            if name != "par" and name[1:] in AT_ORDER:
                free_at[name] = (at_lo_ready, name[0] * AT_PER_LAYER + AT_ORDER[name[1:]] + 1)
            else:
                seen[n % 2] += 1
                free_at[name] = (tr_free[n % 2], seen[n % 2])
        NAME = {n: name for name, n in TURN.items()}

        def at_count(l, kind, g):
            return l * AT_PER_LAYER + AT_ORDER[(kind, g)] + 1

        def wait_read(eng, name):
            s, v = free_at[name]
            eng.wait_ge(s, v)

        def wait_turn(eng, name):
            eng.wait_ge(tr_full, TURN[name] + 1)
            return TR[TURN[name] % 2]

        def use(l, i):
            return PJ_PER_LAYER * l + i

        def pj_read(l, i):
            return (PJ_PER_LAYER - 2) * l + i + 1


        def piece(start, size):
            return gflat[:, start:start + size]
        place_gates = piece(0, SEQ)
        cols = piece(256, 48).rearrange("p (a t e) -> p a t e", a=2, t=2)
        column = small[:, 72:76].rearrange("p (a t) -> p a t", a=2)
        r_logit = piece(320, 16).rearrange("p (t e) -> p t e", t=2)
        r_best = piece(336, 16).rearrange("p (t e) -> p t e", t=2)
        r_index = piece(352, 16).rearrange("p (t e) -> p t e", t=2).bitcast(u32)
        r_indexf = piece(368, 4).rearrange("p (t e) -> p t e", t=2)
        r_diff, r_exp, r_g = piece(372, 2), piece(374, 2), piece(376, 2)
        r_hot = piece(384, 32).rearrange("p (i t e) -> p i t e", i=2, t=2)
        sel = piece(416, 16).rearrange("p (t e) -> p t e", t=2)
        r_pos = piece(432, 16).rearrange("p (t e) -> p t e", t=2)
        r_over, r_rank, r_one = piece(448, 8), piece(456, 8), piece(464, 8)
        r_tmp = piece(472, 16).rearrange("p (t e) -> p t e", t=2)
        r_tab = piece(488, 4)
        router = piece(512, 64).rearrange("p (k e) -> p k e", k=KD)
        place = vreg[:, 1, 0:256].rearrange("p (t s) -> p t s", t=2)
        gated_places = vreg[:, 1, 256:512].rearrange("p (t s) -> p t s", t=2)
        dskip = small[:, 76:92].rearrange("p (l b) -> p l b", l=2)
        zero_mark = small[:, 92:93]
        dve_rows, sel_early, inv_ready = sem("dve_rows"), sem("sel_early"), sem("inv_ready")
        BC_LOADS = 16 * 8

        block = ctx.enter_context(nc.Block())

        @block.sync
        def _(sp):
            sp.dma_start(xres[:, :, :], x[0, :, :].rearrange("(p t) d -> p t d", t=TH)).then_inc(loads, 16)
            sp.dma_start(cst[:, :], consts).then_inc(loads, 16)

            def load(slot, parts):
                for dst, src in parts:
                    sp.dma_start(dst, src).then_inc(raw_full[slot], 16)

            def split_k(slot, w, k0, c0, n):
                kk = TW // n
                dst = raw[:, slot, :].rearrange("p (k c) -> p k c", c=n)
                src = w[k0 * P:(k0 + kk) * P, c0:c0 + n].rearrange("(k p) c -> p k c", p=P)
                return [(dst[:, h * kk // 2:(h + 1) * kk // 2, :], src[:, h * kk // 2:(h + 1) * kk // 2, :]) for h in range(2)]

            def ffn_parts(slot, kind, c, w1, w3, w2):
                if kind == "c":
                    return split_k(slot, w2, c * FC // P, 0, D)
                k0 = 0 if kind == "a" else KD // 2
                dst = raw[:, slot, :].rearrange("p (k w c) -> p k w c", w=2, c=FC)
                return [(dst[:, :, i, :],
                         w[k0 * P:(k0 + 4) * P, c * FC:(c + 1) * FC].rearrange("(k p) c -> p k c", p=P))
                        for i, w in enumerate((w1, w3))]

            def static_tile(t, parts):
                slot = raw_slot(t)
                if t >= 3:
                    sp.wait_ge(lo_ready, t - 2)
                load(slot, parts(slot))

            def mixer(l):
                t = T_MIX[l]
                for n in W_IN_ORDER:
                    for kh in range(2):
                        static_tile(t, lambda s: split_k(s, w_in[l, :, :], 4 * kh, 512 * n, 512))
                        t += 1
                for b, n in ((0, 0), (0, 1), (None, 0), (1, 0), (1, 1)):
                    w = w_glu[l, :, :] if b is None else w_branch[l, b, :, :]
                    static_tile(t, lambda s: split_k(s, w, 0, 512 * n, 512))
                    t += 1
                for n in range(2):
                    for kh in range(2):
                        static_tile(t, lambda s: split_k(s, w_out[l, :, :], 4 * kh, 512 * n, 512))
                        t += 1

            mixer(0)
            f1, f3, f2 = ffn_w1[0, :, :], ffn_w3[0, :, :], ffn_w2[0, :, :]
            for i, kind in enumerate("ab"):
                static_tile(T_FFN0 + i, lambda s: ffn_parts(s, kind, 0, f1, f3, f2))
            with sp.Fori(0, NCH - 1) as c:
                for i, (kind, ahead) in enumerate((("a", 1), ("b", 1), ("c", 0))):
                    slot = raw_slot(T_FFN0 + 2 + i)
                    sp.wait_ge(lo_ready, 3 * c + (T_FFN0 + 2 + i - 2))
                    if kind == "c":
                        dst = raw[:, slot, :].rearrange("p (f c) -> p f c", c=D)
                        for f in range(2):
                            sp.dma_start(dst[:, f, :], f2[bass.ds(c * FC + f * P, P), :]).then_inc(raw_full[slot], 16)
                    else:
                        k0 = 0 if kind == "a" else 4
                        dst = raw[:, slot, :].rearrange("p (k w c) -> p k w c", w=2, c=FC)
                        for j, w in enumerate((f1, f3)):
                            src = w[k0 * P:(k0 + 4) * P, bass.ds(c * FC + FC, FC)].rearrange("(k p) c -> p k c", p=P)
                            sp.dma_start(dst[:, :, j, :], src).then_inc(raw_full[slot], 16)
            static_tile(T_MIX1 - 1, lambda s: ffn_parts(s, "c", NCH - 1, f1, f3, f2))
            mixer(1)

            def expert(e, turn):
                m1, m3, m2 = [m[0, bass.ds(e, 1), :, :].rearrange("e a b -> (e a) b") for m in (moe_w1, moe_w3, moe_w2)]
                for j, (kind, c) in enumerate(FFN_ORDER):
                    sp.wait_ge(lo_ready, turn * FFN_TILES + (T_MOE + j - RAWS + 2))
                    load(moe_slot(j), ffn_parts(moe_slot(j), kind, c, m1, m3, m2))

            sp.wait_ge(y_done, 2 * PAIRS)
            with sp.Fori(0, NE) as e:
                expert(e, e)
            sp.wait_ge(routed, 1)
            nb = sp.value_load(table[0:1, 0:1], min_val=NE, max_val=MAXB)
            with sp.If(nb > NE):
                with sp.Fori(NE, nb) as b:
                    e = sp.value_load(table[0:1, bass.ds(b - (NE - 1), 1)], min_val=0, max_val=NE - 1)
                    expert(e, b)
            sp.wait_ge(final_ready, 2)
            sp.dma_start(out[0, :, :].rearrange("(p t) d -> p t d", t=TH), xn).then_inc(stored, 16)
            sp.wait_ge(stored, 16)
        @block.tensor
        def _(pe):
            def mm(o, a, b, start, stop):
                return pe.matmul(o, a, b, start=start, stop=stop)

            def three(o, a_hi, a_lo, b_hi, b_lo, start, stop):
                mm(o, a_hi, b_hi, start, False)
                mm(o, a_hi, b_lo, False, False)
                return mm(o, a_lo, b_hi, False, stop)

            def open_turn(name):
                n = TURN[name]
                if n >= 2:
                    wait_read(pe, NAME[n - 2])
                return TR[n % 2]

            def transposes(name, sources):
                bank = open_turn(name)
                for i, src in enumerate(sources):
                    rows = src.shape[0]
                    last = pe.transpose(bank[:, i * rows:(i + 1) * rows], src, ident[0:rows, 0:rows])
                last.then_inc(tr_full, 1)

            def proj(t, l, i, k0, first, last):
                pe.wait_ge(lo_ready, t + 1)
                s = t % SPLITS
                for th in range(TH):
                    if first and i == PJ_PER_LAYER - 1:
                        pe.wait_ge(x_added, 8 * l + th + 1)
                    elif first and i > 0:
                        pe.wait_ge(pj_free[th], pj_read(l, i - 1))
                    for k in range(4):
                        m = three(PJ[th][:, :], at_hi[:, k0 + k, th * P:(th + 1) * P], at_lo[:, k0 + k, th * P:(th + 1) * P],
                                  hi[:, s, k * 512:(k + 1) * 512], lo[:, s, k * 512:(k + 1) * 512],
                                  first and k == 0, last and k == 3)
                    if last and th == 0:
                        m.then_inc(pj0_full, 1)
                m.then_inc(tile_used, 1)

            def heads_of(region, th):
                return [region[:, th, h * P:(h + 1) * P] for h in range(HEADS)]

            def s5_in(l, q):
                if 16 * l + q >= 2:
                    pe.wait_ge(pv_free, 16 * l + q - 1)
                b, r0 = q // 2, (q % 2) * 64
                v = PV[q % 2][:, :].rearrange("p (r d c) -> p r d c", r=2, d=2)
                for d in range(2):
                    for r in range(2):
                        rhs = ut2[r0:r0 + 64, b, :] if d == 0 else ut2[r0:r0 + 64, b, ::-1]
                        m = mm(v[:, r, d, :], bbt[r0:r0 + 64, d, r, b, :], rhs, True, True)
                m.then_inc(pv_full, 1)

            def s5_out(l, q):
                pe.wait_ge(states_ready, 16 * l + q + 1)
                xs = xst[q % 2]
                b = q // 2
                for th in range(TH):
                    o = PY[th][:, q * 32:(q + 1) * 32]
                    kinds = ((0, 1), (1, 0)) if th == 0 else ((0, 0), (1, 1))
                    n = 0
                    for d, entering in kinds:
                        for r in range(2):
                            states = xs[:, r, d, 0:P] if entering != d else xs[:, r, d, 1:P + 1]
                            mm(o, states, cblk[:, entering, r, d, q, :, :].rearrange("p g h -> p (g h)"), n == 0, False)
                            n += 1
                    if th == 0 and 16 * l + q > 0:
                        pe.wait_ge(y_done, 16 * l + q)
                    r0 = (q % 2) * 64 + th * 32
                    m = mm(o, ut2[r0:r0 + 32, b, :], cbm[r0:r0 + 32, b, :], False, True)
                m.then_inc(y_done, 1)

            def scores(l, j):
                h, th = j // 2, j % 2
                for c in range(2):
                    bank = open_turn((l, f"sc{c}", j))
                    mm(bank[:, 0:SEQ], q_t[c * HD:(c + 1) * HD, h, th * P:(th + 1) * P],
                       k_t[c * HD:(c + 1) * HD, h, :], True, True).then_inc(tr_full, 1)

            def head_out(l, j):
                h = j // 2
                pe.wait_ge(w_ready, 8 * l + j + 1)
                bank = open_turn((l, "o", j))
                for i in range(2):
                    m = pe.transpose(bank[:, i * P:(i + 1) * P], wdiff[:, i * P:(i + 1) * P], ident)
                m.then_inc(wt_tr, 1)
                pe.wait_ge(wt_ready, 8 * l + j + 1)
                for i in range(2):
                    m = mm(bank[:, 2 * P:3 * P], wdiff_t[:, i, :], vreg[:, i, h * P:(h + 1) * P], i == 0, i == 1)
                m.then_inc(tr_full, 1)

            def mixer(l):
                t = T_MIX[l]
                for g in range(4):
                    pe.wait_ge(xn_ready, 4 * l + g // 2 + 1)
                    transposes((l, "x", g), [xn[:, g // 2, (4 * (g % 2) + i) * P:(4 * (g % 2) + i + 1) * P] for i in range(4)])
                pe.wait_ge(bc_in, BC_LOADS * (l + 1))
                for g in range(4):
                    transposes((l, "ct", g), [craw[g // 2][:, 4 * (g % 2) + i, :, :].rearrange("p a s -> p (a s)") for i in range(4)])
                pe.wait_ge(at_lo_ready, at_count(l, "x", 3))
                proj(t, l, 0, 0, True, False)
                proj(t + 1, l, 0, 4, False, True)
                proj(t + 2, l, 1, 0, True, False)
                proj(t + 3, l, 1, 4, False, True)
                pe.wait_ge(pj_free[1], pj_read(l, 0))
                for g in range(2):
                    transposes((l, "u", g), [u_flat[:, (4 * g + i) * P:(4 * g + i + 1) * P] for i in range(4)])
                proj(t + 4, l, 2, 0, True, False)
                proj(t + 5, l, 2, 4, False, True)
                pe.wait_ge(rot_ready, 4 * l + 2)
                for th in range(TH):
                    transposes((l, "q", th), heads_of(qk[:, 0, :, :], th))
                proj(t + 6, l, 3, 0, True, False)
                proj(t + 7, l, 3, 4, False, True)
                pe.wait_ge(rot_ready, 4 * l + 4)
                for th in range(TH):
                    transposes((l, "k", th), heads_of(qk[:, 1, :, :], th))
                pe.wait_ge(blocks_ready, l + 1)
                bp = gflat.rearrange("p (i c) -> p i c", c=P)
                for g in range(8):
                    transposes((l, "b", g), [bp[:, 4 * g + i, :] for i in range(4)])
                bank = open_turn((l, "cb", 0))
                for q in range(PAIRS):
                    b, q2 = q // 2, q % 2
                    for d in range(2):
                        r0 = q2 * 64 + d * 32
                        for r in range(2):
                            m = mm(bank[r0:r0 + 32, b * 32:(b + 1) * 32],
                                   bpre[:, d, r, b, q2, 1 - d, :, :].rearrange("p g h -> p (g h)"),
                                   cblk[:, 0, r, d, q, :, :].rearrange("p g h -> p (g h)"), r == 0, r == 1)
                m.then_inc(tr_full, 1)
                wait_read(pe, (l, "b", 6))
                wait_read(pe, (l, "b", 7))
                wait_read(pe, (l, "u", 0))
                wait_read(pe, (l, "u", 1))
                wait_read(pe, (l, "k", 0))
                wait_read(pe, (l, "k", 1))
                wait_read(pe, (l, "q", 1))
                for s in range(8):
                    s5_in(l, 2 * s)
                    s5_in(l, 2 * s + 1)
                    scores(l, s)
                    proj(t + 8 + s, l, 4 + s // 2, 4 * (s % 2), s % 2 == 0, s % 2 == 1)
                    if s == 0:
                        wait_read(pe, (l, "cb", 0))
                        pe.wait_ge(pj_free[1], pj_read(l, 3))
                    if s > 0:
                        head_out(l, s - 1)
                        s5_out(l, 2 * s - 2)
                        s5_out(l, 2 * s - 1)
                head_out(l, 7)
                s5_out(l, 14)
                s5_out(l, 15)
                pe.wait_ge(a_ready, 2 * l + 2)
                for th in range(TH):
                    transposes((l, "a", th), heads_of(areg, th))
                pe.wait_ge(at_lo_ready, at_count(l, "a", 1))
                proj(t + 16, l, 8, 0, True, True)
                proj(t + 17, l, 9, 0, True, True)
                pe.wait_ge(s_ready, 2 * l + 2)
                for th in range(TH):
                    transposes((l, "s", th), heads_of(s_act, th))
                pe.wait_ge(at_lo_ready, at_count(l, "s", 1))
                proj(t + 18, l, 10, 4, True, True)
                pe.wait_ge(s2_ready, 2 * l + 2)
                for th in range(TH):
                    transposes((l, "s2", th), heads_of(s_gated, th))
                pe.wait_ge(at_lo_ready, at_count(l, "s2", 1))
                proj(t + 19, l, 11, 4, True, True)
                proj(t + 20, l, 12, 4, True, True)
                pe.wait_ge(m_ready, 4 * l + 4)
                for g in range(4):
                    transposes((l, "m", g), [gates[:, g // 2, 0, (4 * (g % 2) + i) * P:(4 * (g % 2) + i + 1) * P] for i in range(4)])
                pe.wait_ge(at_lo_ready, at_count(l, "m", 3))
                for n in range(2):
                    proj(t + 21 + 2 * n, l, 13 + n, 0, True, False)
                    proj(t + 22 + 2 * n, l, 13 + n, 4, False, True)
                for g in range(4):
                    pe.wait_ge(xn_ready, 4 * l + 2 + g // 2 + 1)
                    transposes((l, "h", g), [xn[:, g // 2, (4 * (g % 2) + i) * P:(4 * (g % 2) + i + 1) * P] for i in range(4)])
                pe.wait_ge(at_lo_ready, at_count(l, "h", 3))

            pe.wait_ge(loads, 32)
            pe.wait_ge(dve_par, 1)
            transposes("par", [row(PACK + i) for i in range(7)])
            mixer(0)

            def up2(c, a_tile, a_slot, b_tile, b_slot):
                pe.wait_ge(lo_ready, a_tile + 1)
                if c is not None:
                    pe.wait_ge(h_done, c)
                for th in range(TH):
                    for k in range(4):
                        m = three(PJ[th][:, :], at_hi[:, k, th * P:(th + 1) * P], at_lo[:, k, th * P:(th + 1) * P],
                                  hi[:, a_slot, k * 512:(k + 1) * 512], lo[:, a_slot, k * 512:(k + 1) * 512], k == 0, False)
                m.then_inc(tile_used, 1)
                pe.wait_ge(lo_ready, b_tile + 1)
                for th in range(TH):
                    for k in range(4):
                        m = three(PJ[th][:, :], at_hi[:, 4 + k, th * P:(th + 1) * P], at_lo[:, 4 + k, th * P:(th + 1) * P],
                                  hi[:, b_slot, k * 512:(k + 1) * 512], lo[:, b_slot, k * 512:(k + 1) * 512], False, k == 3)
                    if th == 0:
                        m.then_inc(h_full, 1)
                m.then_inc(tile_used, 1)

            def hidden_t2(done):
                pe.wait_ge(h_done, done)
                for th in range(TH):
                    for f in range(2):
                        m = pe.transpose(TR[0][:, f * SEQ + th * P:f * SEQ + (th + 1) * P],
                                         v_flat[:, (2 + th) * FC + f * P:(2 + th) * FC + (f + 1) * P], ident)
                m.then_inc(ht_tr, 1)

            def down2(tile, slot, parts, start, stop):
                pe.wait_ge(lo_ready, tile + 1)
                pe.wait_ge(ht_lo_ready, parts)
                for th in range(TH):
                    for f in range(2):
                        for n in range(2):
                            m = three(banks[2 + 2 * th + n][:, :], ht_hi[:, f, th * P:(th + 1) * P], ht_lo[:, f, th * P:(th + 1) * P],
                                      hi[:, slot, f * D + n * 512:f * D + (n + 1) * 512],
                                      lo[:, slot, f * D + n * 512:f * D + (n + 1) * 512], start and f == 0, stop and f == 1)
                m.then_inc(tile_used, 1)

            t = T_FFN0
            up2(None, t, t % 3, t + 1, (t + 1) % 3)
            up2(2, t + 2, (t + 2) % 3, t + 3, t % 3)
            hidden_t2(2)
            down2(t + 4, (t + 4) % 3, 1, True, False)
            with pe.Fori(1, NCH - 1) as c:
                up2(c * 2 + 2, c * 3 + (t + 2), (t + 2) % 3, c * 3 + (t + 3), t % 3)
                hidden_t2(c * 2 + 2)
                down2(c * 3 + (t + 4), (t + 4) % 3, c + 1, False, False)
            hidden_t2(2 * NCH)
            down2(T_MIX1 - 1, (T_MIX1 - 1) % 3, NCH, False, True)
            mixer(1)

            pe.wait_ge(router_in, 16)
            bank = open_turn("router")
            for th in range(TH):
                for k in range(KD):
                    for i, a in enumerate((at_hi, at_lo)):
                        m = mm(bank[:, th * 8:(th + 1) * 8], a[:, k, th * P:(th + 1) * P].bitcast(f32), router[:, k, :],
                               k == 0 and i == 0, k == KD - 1 and i == 1)
            m.then_inc(tr_full, 1)
            pe.wait_ge(sel_ready, 1)
            bank = open_turn("pos")
            tri, ones = cst[:, C_TRI:C_TRI + P], cst[:, C_ONE:C_ONE + P]
            mm(bank[:, 0:8], tri, sel[:, 0, :], True, True)
            mm(bank[:, 8:16], tri, sel[:, 1, :], True, False)
            mm(bank[:, 8:16], ones, sel[:, 0, :], False, True)
            mm(bank[:, 16:24], ones, sel[:, 0, :], True, False)
            mm(bank[:, 16:24], ones, sel[:, 1, :], False, True).then_inc(tr_full, 1)

            def gather():
                for k in range(KD):
                    for th in range(TH):
                        m = mm(banks[4 + k // 4][:, (k % 4) * P:(k % 4 + 1) * P], xn[:, th, k * P:(k + 1) * P],
                               place[:, th, :], th == 0, th == 1)
                m.then_inc(xe_full, 1)

            def tile_at(turn, j):
                return turn * FFN_TILES + (T_MOE + j)

            pe.wait_ge(place_ready, 1)
            gather()
            nb = pe.value_load(table[0:1, 0:1], min_val=NE, max_val=MAXB)
            with pe.Fori(0, nb) as b:
                def up(c, ja, jb):
                    for half, j in enumerate((ja, jb)):
                        s = (T_MOE + j) % 3
                        pe.wait_ge(lo_ready, tile_at(b, j) + 1)
                        if half == 0 and c >= 2:
                            pe.wait_ge(h_done, b * NCH + (2 * NCH + c - 1))
                        for k in range(4):
                            m = three(banks[c % 2][:, :], at_hi[:, 4 * half + k, 0:P], at_lo[:, 4 * half + k, 0:P],
                                      hi[:, s, k * 512:(k + 1) * 512], lo[:, s, k * 512:(k + 1) * 512],
                                      half == 0 and k == 0, half == 1 and k == 3)
                        m.then_inc(tile_used, 1)

                def hidden_t(c):
                    pe.wait_ge(h_done, b * NCH + (2 * NCH + c + 1))
                    for f in range(2):
                        m = pe.transpose(TR[0][:, f * P:(f + 1) * P], v_flat[:, FC + f * P:FC + (f + 1) * P], ident)
                    m.then_inc(ht_tr, 1)

                def down(c, j):
                    s = (T_MOE + j) % 3
                    pe.wait_ge(lo_ready, tile_at(b, j) + 1)
                    pe.wait_ge(ht_lo_ready, b * NCH + (NCH + c + 1))
                    for f in range(2):
                        for n in range(2):
                            m = three(banks[2 + n][:, :], ht_hi[:, f, 0:P], ht_lo[:, f, 0:P],
                                      hi[:, s, f * D + n * 512:f * D + (n + 1) * 512],
                                      lo[:, s, f * D + n * 512:f * D + (n + 1) * 512], c == 0 and f == 0, c == NCH - 1 and f == 1)
                    m.then_inc(tile_used, 1)

                pe.wait_ge(xe_lo_ready, b + 1)
                up(0, 0, 1)
                for c in range(NCH - 1):
                    up(c + 1, 3 * c + 2, 3 * c + 3)
                    if c == 0:
                        pe.wait_ge(x_added, b * 4 + 12)
                    hidden_t(c)
                    down(c, 3 * c + 4)
                    if c == 6:
                        pe.wait_ge(place_ready, b + 2)
                        for th in range(TH):
                            m = pe.transpose(TR[1][:, th * P:(th + 1) * P], gated_places[:, th, :], ident)
                        m.then_inc(pg_full, 1)
                gather()
                hidden_t(NCH - 1)
                down(NCH - 1, FFN_TILES - 1)
                pe.wait_ge(gt_ready, b + 1)
                pe.wait_ge(ye_ready, b * 2 + 2)
                for i in range(4):
                    th, n = i // 2, i % 2
                    mm((TR[1], banks[2], banks[3], TR[0])[i][:, :], place_gates[:, th * P:(th + 1) * P],
                       u_flat[:, n * 512:(n + 1) * 512], True, True).then_inc(comb_full, 1)

        @block.scalar
        def _(act):
            own = Order(act, act_own)

            def split(t, full_sem, full, src, slot, after=True):
                act.wait_ge(full_sem, full)
                if after:
                    act.wait_ge(tile_used, t - (SPLITS - 1))
                act.activation(hi[:, slot, :], src, ACT.Copy).then_inc(hi_ready, 1)

            def split_static(t):
                s = raw_slot(t)
                split(t, raw_full[s], 32 * (raw_uses(s, t) + 1), raw[:, s, :], t % SPLITS, t >= SPLITS)

            def at_part(l, kind, g, k0, kn, c0, scale=1.0):
                bank = wait_turn(act, (l, kind, g))
                act.activation(at_hi[:, k0:k0 + kn, c0:c0 + P], bank[:, 0:kn * P].rearrange("p (k c) -> p k c", k=kn),
                               ACT.Copy, scale=scale).then_inc(at_hi_ready, 1)

            def squares(stage):
                for th in range(TH):
                    m = act.activation(xn[:, th, :], xres[:, th, :], ACT.Square, accum_out=col(SS + th))
                m.then_inc(sq_ready, 1)
                act.wait_ge(var_ready, stage + 1)
                act.activation(col(RT, 2), col(VAR, 2), ACT.Sqrt).then_inc(root_ready, 1)

            def load_gain(src):
                act.dma_start(a_flat, src.partition_broadcast(P)).then_inc(gain_in, 16)

            def evac(name, dst, bank_cols=512):
                bank = wait_turn(act, name)
                act.activation(dst, bank[:, 0:bank_cols], ACT.Copy).then_inc(tr_free[TURN[name] % 2], 1)

            def from_pj(l, i, tile, dst, func, scale=1.0, view=None, sig=None):
                for th in range(TH):
                    if th == 0:
                        act.wait_ge(pj0_full, use(l, i) + 1)
                    else:
                        act.wait_ge(tile_used, tile + 1)
                    src = PJ[th][:, :] if view is None else view(PJ[th][:, :])
                    act.activation(dst(th), src, func, scale=scale).then_inc(pj_free[th], 1)

            def probs_of(l, j):
                act.wait_ge(max_ready, 8 * l + j + 1)
                for c in range(2):
                    m = act.activation(probs[:, c, :], TR[TURN[(l, f"sc{c}", j)] % 2][:, 0:SEQ], ACT.Exp, bias=col(NB + c),
                                       scale=HD ** -0.5, accum_out=col(RS + c))
                m.then_inc(exp_ready, 1)

            def head_back(l, j):
                name = (l, "o", j)
                bank = TR[TURN[name] % 2]
                act.wait_ge(wt_tr, 8 * l + j + 1)
                act.activation(wdiff_t, bank[:, 0:2 * P].rearrange("p (t q) -> p t q", t=2), ACT.Copy).then_inc(wt_ready, 1)
                wait_turn(act, name)
                h, th = j // 2, j % 2
                own.step(act.activation(areg[:, th, h * P:(h + 1) * P], bank[:, 2 * P:3 * P], ACT.Copy))
                act.activation(bank[:, 2 * P:3 * P], bank[:, 2 * P:3 * P], ACT.Square,
                               accum_out=col(AS + j)).then_inc(tr_free[TURN[name] % 2], 1)

            def lay_blocks(l):
                act.wait_ge(mats_ready, 2 * l + 1)
                for d in range(2):
                    for kind, src in enumerate((bbar, babar)):
                        t = (1 - d) if kind == 0 else d
                        for g in range(2):
                            for r in range(2):
                                rows = slice(64 * g, 64 * (g + 1))
                                act.activation(bpre[rows, d, r, :, :, t, g, :].rearrange("p b q h -> p (b q) h"),
                                               src[rows, r, d * PAIRS:(d + 1) * PAIRS, :], ACT.Copy)
                act.wait_ge(mats_ready, 2 * l + 2)
                for kind, src in enumerate((ctr, cabar)):
                    for r in range(2):
                        for g in range(2):
                            rows = slice(64 * g, 64 * (g + 1))
                            m = act.activation(cblk[rows, kind, r, :, :, g, :].rearrange("p d q h -> p (d q) h"),
                                               src[rows, r, :, :], ACT.Copy, scale=1.0 if r == 0 else -1.0)
                m.then_inc(blocks_ready, 1)

            def mixer(l):
                t = T_MIX[l]
                if l > 0:
                    act.wait_ge(tile_used, t - 1)
                for g in range(4):
                    at_part(l, "x", g, 4 * (g % 2), 4, (g // 2) * P)
                for g in range(4):
                    bank = wait_turn(act, (l, "ct", g))
                    r, d = g // 2, g % 2
                    for odd in range(2):
                        rows = slice(64 * odd, 64 * (odd + 1))
                        m = act.activation(ctr[rows, r, d * PAIRS:(d + 1) * PAIRS, :],
                                           bank[rows, :].rearrange("p (j g h) -> p j g h", g=2, h=GC)[:, :, odd, :], ACT.Copy)
                    m.then_inc(tr_free[TURN[(l, "ct", g)] % 2], 1)
                for s in range(3):
                    split_static(t + s + 2)
                    if s == 1:
                        from_pj(l, 0, t + 1, lambda th: u_rows[:, :, th, :], ACT.Copy,
                                view=lambda b: b.rearrange("p (q c) -> p q c", q=PAIRS))
                split_static(t + 5)
                for g in range(2):
                    evac((l, "u", g), ut2[:, 4 * g:4 * g + 4, :].rearrange("p b c -> p (b c)"))
                split_static(t + 6)
                split_static(t + 7)
                for th in range(TH):
                    evac_heads(l, "q", th, q_t)
                split_static(t + 8)
                split_static(t + 9)
                from_pj(l, 3, t + 7, lambda th: vreg[:, th, :], ACT.Copy)
                for th in range(TH):
                    evac_heads(l, "k", th, k_t)
                lay_blocks(l)
                bflat = area(0, 4096)
                for g in range(0, 8, 2):
                    evac((l, "b", g), bflat[:, g * 512:(g + 1) * 512])
                for s in range(8):
                    split_static(t + 10 + s)
                    probs_of(l, s)
                    if s % 2 == 1:
                        i = 4 + s // 2
                        g, n = (i - 4) // 2, (i - 4) % 2
                        from_pj(l, i, t + 8 + s, lambda th: gates[:, th, g, n * 512:(n + 1) * 512], ACT.Tanh, scale=0.5)
                    if s > 0:
                        head_back(l, s - 1)
                head_back(l, 7)
                act.wait_ge(avar_ready, l + 1)
                act.activation(col(AR, 8), col(AV, 8), ACT.Sqrt).then_inc(aroot_ready, 1)
                for th in range(TH):
                    at_part(l, "a", th, 0, 4, th * P)
                load_gain(norm_ffn[l, :])
                split_static(t + 18)
                act.wait_ge(y_done, PAIRS * (l + 1))
                for th in range(TH):
                    act.activation(s_act[:, th, :], PY[th][:, :], ACT.Gelu).then_inc(s_ready, 1)
                split_static(t + 19)
                for th in range(TH):
                    at_part(l, "s", th, 4, 4, th * P)
                split_static(t + 20)
                from_pj(l, 10, t + 18, lambda th: s_gated[:, th, :], ACT.Tanh, scale=0.5)
                act.wait_ge(tile_used, t + 19)
                for th in range(TH):
                    at_part(l, "s2", th, 4, 4, th * P, scale=0.5)
                split_static(t + 21)
                split_static(t + 22)
                act.wait_ge(tile_used, t + 21)
                for g in range(4):
                    at_part(l, "m", g, 4 * (g % 2), 4, (g // 2) * P, scale=0.5)
                split_static(t + 23)
                split_static(t + 24)
                if l == 0:
                    split_static(t + 25)
                    split_static(t + 26)
                act.wait_ge(x_added, 8 * l + 4)
                squares(2 * l + 1)
                for g in range(4):
                    at_part(l, "h", g, 4 * (g % 2), 4, (g // 2) * P)
                load_gain(norm_mix[1, :] if l == 0 else norm_final)

            def evac_heads(l, kind, th, dst):
                bank = wait_turn(act, (l, kind, th))
                act.activation(dst[:, :, th * P:(th + 1) * P], bank[:, :].rearrange("p (h s) -> p h s", h=HEADS),
                               ACT.Copy).then_inc(tr_free[TURN[(l, kind, th)] % 2], 1)

            load_gain(norm_mix[0, :])
            act.dma_start(row(R_LR), ssm_lam_re.rearrange("l d (q g) s -> (l d q) (g s)", g=2)).then_inc(rows_in, 16)
            act.dma_start(row(R_LI), ssm_lam_im.rearrange("l d (q g) s -> (l d q) (g s)", g=2)).then_inc(rows_in, 16)
            act.dma_start(row(R_DT)[:, 0:2], ssm_log_dt.rearrange("l d (q g) -> (l d q) g", g=2)).then_inc(rows_in, 16)
            act.dma_start(gflat[:, 4 * P:8 * P], attn_lambda.rearrange("l a c -> (l a c)").partition_broadcast(P)).then_inc(rows_in, 16)
            act.dma_start(subln[:, :, :].rearrange("p l c -> p (l c)"),
                          attn_subln.rearrange("l c -> (l c)").partition_broadcast(P)).then_inc(rows_in, 16)
            act.wait_ge(loads, 32)
            squares(0)
            split_static(0)
            split_static(1)
            act.wait_ge(rows_in, 80)
            act.activation(row(R_EDT)[:, 0:2], row(R_DT)[:, 0:2], ACT.Exp).then_inc(act_par, 1)
            act.wait_ge(dve_rows, 1)
            act.activation(row(R_er), row(R_lr), ACT.Exp)
            act.wait_ge(lam_ready, 1)
            act.activation(col(LEXP, 4), col(LSUM, 4), ACT.Exp).then_inc(lam_exp, 1)
            act.activation(row(R_sn), row(R_red), ACT.Sin)
            act.activation(row(R_sh), row(R_red), ACT.Sin, scale=0.5).then_inc(act_par, 1)
            mixer(0)

            def silu2(full0, used1):
                for th in range(TH):
                    act.wait_ge(h_full if th == 0 else tile_used, full0 if th == 0 else used1)
                    act.activation(v_flat[:, th * FC:(th + 1) * FC], PJ[th][:, 0:FC], ACT.Silu).then_inc(g_ready, 1)

            def hidden_hi(n, cols):
                act.wait_ge(ht_tr, n)
                act.activation(ht_hi[:, :, 0:cols], TR[0][:, 0:2 * cols].rearrange("p (f s) -> p f s", f=2),
                               ACT.Copy).then_inc(ht_hi_ready, 1)

            t = T_FFN0

            def ffn_turn(c, used):
                def split_turn(i):
                    s = raw_slot(t + 2 + i)
                    split(c * 3 + (t + 2 + i), raw_full[s], c * 32 + 32 * (raw_uses(s, t + 2 + i) + 1), raw[:, s, :], (t + 2 + i) % 3)
                split_turn(0)
                silu2(c + 1, used)
                split_turn(1)
                split_turn(2)
                hidden_hi(c + 1, SEQ)
            ffn_turn(0, t + 2)
            with act.Fori(1, NCH - 1) as c:
                ffn_turn(c, c * 3 + (t + 1))
            silu2(NCH, t + 3 * (NCH - 1) + 1)
            split_static(T_MIX1 - 1)
            hidden_hi(NCH, SEQ)
            split_static(T_MIX1)
            split_static(T_MIX1 + 1)
            act.wait_ge(x_added, 8)
            squares(2)
            mixer(1)

            act.dma_start(router, moe_router[0, :, :].rearrange("(k p) e -> p k e", p=P)).then_inc(router_in, 16)
            act.wait_ge(sel_early, 1)
            act.activation(r_exp, r_diff, ACT.Exp).then_inc(gate_exp, 1)

            def gathered(n):
                act.wait_ge(xe_full, n)
                for g in range(2):
                    m = act.activation(at_hi[:, 4 * g:4 * g + 4, 0:P], banks[4 + g][:, :].rearrange("p (k c) -> p k c", k=4), ACT.Copy)
                m.then_inc(xe_hi_ready, 1)

            gathered(1)
            act.wait_ge(routed, 1)
            nb = act.value_load(table[0:1, 0:1], min_val=NE, max_val=MAXB)
            with act.Fori(0, nb) as b:
                def split_moe(j):
                    slot = moe_slot(j)
                    split(b * FFN_TILES + (T_MOE + j), raw_full[slot], moe_full_value(j, b), raw[:, slot, :], (T_MOE + j) % 3)

                def silu(c, j):
                    act.wait_ge(tile_used, b * FFN_TILES + (T_MOE + j + 1))
                    act.activation(v_flat[:, 0:FC], banks[c % 2][:, 0:FC], ACT.Silu).then_inc(g_ready, 1)

                split_moe(0)
                split_moe(1)
                for c in range(NCH - 1):
                    split_moe(3 * c + 2)
                    silu(c, 1 if c == 0 else 3 * c)
                    split_moe(3 * c + 3)
                    split_moe(3 * c + 4)
                    hidden_hi(b * NCH + (NCH + c + 1), P)
                    if c == 6:
                        act.wait_ge(pg_full, b + 1)
                        act.activation(place_gates, TR[1][:, 0:SEQ], ACT.Copy).then_inc(gt_ready, 1)
                silu(NCH - 1, 3 * (NCH - 1))
                split_moe(FFN_TILES - 1)
                gathered(b + 2)
                hidden_hi(b * NCH + 2 * NCH, P)
                act.wait_ge(tile_used, b * FFN_TILES + (T_MOE + FFN_TILES))
                act.activation(u_flat[:, 0:512], banks[2][:, :], ACT.Copy).then_inc(ye_ready, 1)
            act.wait_ge(x_added, nb * 4 + 12)
            squares(4)

        @block.vector
        def _(dve):
            own = Order(dve, dve_own)
            tt, ts, stt = dve.tensor_tensor, dve.tensor_scalar, dve.scalar_tensor_tensor

            def split(t, slot, src):
                dve.wait_ge(hi_ready, t + 1)
                tt(lo[:, slot, :], src, hi[:, slot, :].bitcast(f32), SUB).then_inc(lo_ready, 1)

            def split_static(t):
                split(t, t % SPLITS, raw[:, raw_slot(t), :])

            def at_part(l, kind, g, k0, kn, c0, scale=None):
                bank = TR[TURN[(l, kind, g)] % 2]
                dve.wait_ge(at_hi_ready, at_count(l, kind, g))
                src = bank[:, 0:kn * P].rearrange("p (k c) -> p k c", k=kn)
                dst, first = at_lo[:, k0:k0 + kn, c0:c0 + P], at_hi[:, k0:k0 + kn, c0:c0 + P].bitcast(f32)
                if scale is None:
                    tt(dst, src, first, SUB).then_inc(at_lo_ready, 1)
                else:
                    stt(dst, src, scale, first, MUL, SUB).then_inc(at_lo_ready, 1)

            def norm(stage, done):
                dve.wait_ge(sq_ready, stage + 1)
                ts(col(VAR, 2), col(SS, 2), 1.0 / D, EPS, MUL, ADD).then_inc(var_ready, 1)
                dve.wait_ge(root_ready, stage + 1)
                own.step(dve.reciprocal(col(RI, 2), col(RT, 2)))
                dve.wait_ge(gain_in, 16 * (stage + 1))
                for th in range(TH):
                    stt(xn[:, th, :], xres[:, th, :], col(RI + th), gain, MUL, MUL).then_inc(done, 1)

            def rotary(l, i, tile, dst):
                cos_t, sin_t = (cst[:, c:c + 128].rearrange("p (t c) -> p t c", t=2) for c in (C_COS, C_SIN))
                for th in range(TH):
                    if th == 0:
                        dve.wait_ge(pj0_full, use(l, i) + 1)
                    else:
                        dve.wait_ge(tile_used, tile + 1)
                    src = PJ[th][:, :]
                    own.step(tt(a_flat[:, 0:512].rearrange("p (h c) -> p h c", c=HD), src.rearrange("p (h c) -> p h c", c=HD),
                                cos_t[:, th, :].unsqueeze(1).broadcast_to([P, 8, HD]), MUL))
                    tt(a_flat[:, 512:1024].rearrange("p (h a c) -> p h a c", a=2, c=32),
                       src.rearrange("p (h a c) -> p h a c", a=2, c=32)[:, :, ::-1, :],
                       sin_t[:, th, :].rearrange("p (a c) -> p a c", a=2).unsqueeze(1).broadcast_to([P, 8, 2, 32]),
                       MUL).then_inc(pj_free[th], 1)
                    dve.wait_ge(pj_free[th], pj_read(l, i))
                    tt(dst[:, th, :], a_flat[:, 0:512], a_flat[:, 512:1024], ADD).then_inc(rot_ready, 1)
                    dve.wait_ge(rot_ready, 4 * l + (0 if i == 1 else 2) + th + 1)

            def s5_scan(l, q):
                n = 16 * l + q
                v = PV[q % 2][:, :].rearrange("p (r c) -> p r c", r=2)
                w = wtab[q % 2]
                dve.wait_ge(pv_full, n + 1)
                dve.wait_ge(wtab_ready, n + 1)
                tt(rot1, v, w[:, 0:1, :].broadcast_to([P, 2, 256]), MUL)
                tt(rot2, v[:, ::-1, :], w[:, 1:2, :].broadcast_to([P, 2, 256]), MUL).then_inc(pv_free, 1)
                dve.wait_ge(pv_free, n + 1)
                tt(rot1[:, 0, :], rot1[:, 0, :], rot2[:, 0, :], ADD)
                own.step(tt(rot1[:, 1, :], rot1[:, 1, :], rot2[:, 1, :], SUB))
                dve.wait_ge(r2_ready, n + 1)
                if n > 0:
                    dve.wait_ge(zs_used, n)
                dve.tensor_tensor_scan(zs[:, 0, :], r2t, rot1[:, 0, :], 0.0, MUL, ADD)
                dve.tensor_tensor_scan(zs[:, 1, :], r2t, rot1[:, 1, :], 0.0, MUL, ADD).then_inc(zs_ready, 1)

            def row_max(l, j):
                for c in range(2):
                    bank = wait_turn(dve, (l, f"sc{c}", j))
                    own.step(dve.tensor_reduce(col(MX + c), bank[:, 0:SEQ], AX.X, ALU.max))
                ts(col(NB, 2), col(MX, 2), -(HD ** -0.5), None, MUL).then_inc(max_ready, 1)

            def softmax_difference(l, j):
                names = [(l, f"sc{c}", j) for c in range(2)]
                dve.wait_ge(exp_ready, 8 * l + j + 1)
                dve.reciprocal(col(RR, 2), col(RS, 2)).then_inc(tr_free[TURN[names[0]] % 2], 1)
                wait_read(dve, names[0])
                own.step(tt(col(C1), col(RR + 1), col(NLAM + l), MUL))
                ts(probs[:, 1, :], probs[:, 1, :], col(C1), None, MUL).then_inc(tr_free[TURN[names[1]] % 2], 1)
                wait_read(dve, names[1])
                if 8 * l + j > 0:
                    dve.wait_ge(wt_tr, 8 * l + j)
                stt(wdiff, probs[:, 0, :], col(RR), probs[:, 1, :], MUL, ADD).then_inc(w_ready, 1)

            def gated(l, i, tile, g, n):
                for th in range(TH):
                    if th == 0:
                        dve.wait_ge(pj0_full, use(l, i) + 1)
                    else:
                        dve.wait_ge(tile_used, tile + 1)
                    z = gates[:, th, g, n * 512:(n + 1) * 512]
                    stt(z, z, 1.0, PJ[th][:, :], ADD, MUL).then_inc(pj_free[th], 1)
                    if g == 1:
                        dve.wait_ge(pj_free[th], pj_read(l, i))
                        m = gates[:, th, 0, n * 512:(n + 1) * 512]
                        tt(m, m, z, ADD).then_inc(m_ready, 1)

            def add_out(l, i, tile, n):
                for th in range(TH):
                    if th == 0:
                        dve.wait_ge(pj0_full, use(l, i) + 1)
                    else:
                        dve.wait_ge(tile_used, tile + 1)
                    z = xres[:, th, n * 512:(n + 1) * 512]
                    tt(z, z, PJ[th][:, :], ADD).then_inc(x_added, 1)

            def mixer(l):
                t = T_MIX[l]
                for g in range(4):
                    at_part(l, "x", g, 4 * (g % 2), 4, (g // 2) * P)
                for s in range(4):
                    split_static(t + s + 2)
                rotary(l, 1, t + 3, qk[:, 0, :, :])
                split_static(t + 6)
                split_static(t + 7)
                rotary(l, 2, t + 5, qk[:, 1, :, :])
                split_static(t + 8)
                split_static(t + 9)
                bflat = area(0, 4096)
                for g in range(1, 8, 2):
                    bank = wait_turn(dve, (l, "b", g))
                    dve.tensor_copy(bflat[:, g * 512:(g + 1) * 512], bank[:, :]).then_inc(tr_free[TURN[(l, "b", g)] % 2], 1)
                dve.wait_ge(dskip_in, 16 * 8)
                own.step(tt(cbm, cst[:, C_PAT:C_PAT + 32].unsqueeze(1).broadcast_to([P, 8, 32]),
                            dskip[:, l, :].unsqueeze(2).broadcast_to([P, 8, 32]), MUL))
                bank = wait_turn(dve, (l, "cb", 0))
                tt(cbm, cbm, bank[:, 0:256].rearrange("p (b c) -> p b c", b=8), ADD).then_inc(tr_free[TURN[(l, "cb", 0)] % 2], 1)
                for s in range(8):
                    split_static(t + 10 + s)
                    row_max(l, s)
                    s5_scan(l, 2 * s)
                    softmax_difference(l, s)
                    s5_scan(l, 2 * s + 1)
                wait_read(dve, (l, "o", 6))
                wait_read(dve, (l, "o", 7))
                ts(col(AV, 8), col(AS, 8), 1.0 / P, EPS, MUL, ADD).then_inc(avar_ready, 1)
                dve.wait_ge(aroot_ready, l + 1)
                own.step(dve.reciprocal(col(AI, 8), col(AR, 8)))
                inv = col(AI, 8).rearrange("p (h t) -> p t h", t=2)
                for th in range(TH):
                    z = areg[:, th, :].rearrange("p (h c) -> p h c", h=HEADS)
                    own.step(tt(z, z, inv[:, th, :].unsqueeze(2).broadcast_to([P, HEADS, P]), MUL))
                    tt(z, z, subln[:, l, :].unsqueeze(1).broadcast_to([P, HEADS, P]), MUL).then_inc(a_ready, 1)
                for th in range(TH):
                    at_part(l, "a", th, 0, 4, th * P)
                split_static(t + 18)
                gated(l, 8, t + 16, 0, 0)
                split_static(t + 19)
                gated(l, 9, t + 17, 0, 1)
                for th in range(TH):
                    at_part(l, "s", th, 4, 4, th * P)
                split_static(t + 20)
                for th in range(TH):
                    dve.wait_ge(pj_free[th], pj_read(l, 10))
                    stt(s_gated[:, th, :], s_gated[:, th, :], 1.0, s_act[:, th, :], ADD, MUL).then_inc(s2_ready, 1)
                for th in range(TH):
                    at_part(l, "s2", th, 4, 4, th * P, scale=0.5)
                split_static(t + 21)
                gated(l, 11, t + 19, 1, 0)
                split_static(t + 22)
                gated(l, 12, t + 20, 1, 1)
                for g in range(4):
                    at_part(l, "m", g, 4 * (g % 2), 4, (g // 2) * P, scale=0.5)
                split_static(t + 23)
                split_static(t + 24)
                add_out(l, 13, t + 22, 0)
                if l == 0:
                    split_static(t + 25)
                    split_static(t + 26)
                add_out(l, 14, t + 24, 1)
                norm(2 * l + 1, xn_ready)
                for g in range(4):
                    at_part(l, "h", g, 4 * (g % 2), 4, (g // 2) * P)

            TWO_PI_A = 6.28125
            TWO_PI_B = round((2 * math.pi - TWO_PI_A) * 2 ** 20) / 2 ** 20
            TWO_PI_C = 2 * math.pi - TWO_PI_A - TWO_PI_B
            MAGIC = 1.5 * 2.0 ** 23
            norm(0, xn_ready)
            split_static(0)
            split_static(1)
            dve.wait_ge(act_par, 1)
            dt = row(R_EDT)[:, 0:2].unsqueeze(2).broadcast_to([64, 2, 64])

            def halves(ap):
                return ap.rearrange("p (g s) -> p g s", g=2)
            tt(halves(row(R_lr)), halves(row(R_LR)), dt, MUL).then_inc(dve_rows, 1)
            own.step(tt(halves(row(R_li)), halves(row(R_LI)), dt, MUL))
            own.step(ts(row(R_k), row(R_li), 1.0 / (2 * math.pi), MAGIC, MUL, ADD))
            own.step(ts(row(R_k), row(R_k), -MAGIC, None, ADD))
            own.step(stt(row(R_red), row(R_k), -TWO_PI_A, row(R_li), MUL, ADD))
            own.step(stt(row(R_red), row(R_k), -TWO_PI_B, row(R_red), MUL, ADD))
            own.step(stt(row(R_red), row(R_k), -TWO_PI_C, row(R_red), MUL, ADD))
            own.step(ts(row(R_red), row(R_red), 3.1415925, -3.1415925, ALU.min, ALU.max))
            own.step(tt(lamp.rearrange("p (l a) c -> p l a c", l=2), lamv[:, :, :, 0, :], lamv[:, :, :, 1, :], MUL))
            dve.tensor_reduce(col(LSUM, 4), lamp, AX.X, ADD).then_inc(lam_ready, 1)
            dve.wait_ge(lam_exp, 1)
            le = col(LEXP, 4).rearrange("p (l a) -> p l a", l=2)
            own.step(tt(col(NLAM, 2), le[:, :, 1], le[:, :, 0], SUB))
            for l in range(2):
                lam_init = 0.8 - 0.6 * math.exp(-0.3 * l)
                own.step(ts(col(NLAM + l), col(NLAM + l), -lam_init, None, ADD))
                own.step(ts(subln[:, l, :], subln[:, l, :], 1.0 - lam_init, None, MUL))
            dve.wait_ge(act_par, 2)
            a_re, a_im, co_re, co_im, cos, sin, rad2 = (row(PACK + i) for i in range(7))
            own.step(tt(row(R_t), row(R_sh), row(R_sh), MUL))
            own.step(ts(cos, row(R_t), -2.0, 1.0, MUL, ADD))
            own.step(dve.tensor_copy(sin, row(R_sn)))
            own.step(tt(a_re, row(R_er), cos, MUL))
            own.step(tt(a_im, row(R_er), sin, MUL))
            own.step(tt(rad2, row(R_er), row(R_er), MUL))
            own.step(tt(row(R_t), row(R_LR), row(R_LR), MUL))
            own.step(tt(row(R_u), row(R_LI), row(R_LI), MUL))
            own.step(tt(row(R_t), row(R_t), row(R_u), ADD))
            own.step(dve.reciprocal(row(R_den), row(R_t)))
            own.step(ts(row(R_am), a_re, -1.0, None, ADD))
            own.step(tt(row(R_t), row(R_am), row(R_LR), MUL))
            own.step(tt(row(R_u), a_im, row(R_LI), MUL))
            own.step(tt(row(R_t), row(R_t), row(R_u), ADD))
            own.step(tt(co_re, row(R_t), row(R_den), MUL))
            own.step(tt(row(R_t), a_im, row(R_LR), MUL))
            own.step(tt(row(R_u), row(R_am), row(R_LI), MUL))
            own.step(tt(row(R_t), row(R_t), row(R_u), SUB))
            tt(co_im, row(R_t), row(R_den), MUL).then_inc(dve_par, 1)
            bank = wait_turn(dve, "par")
            dve.tensor_copy(par[:, :, :].rearrange("p i j -> p (i j)"), bank[:, 0:448]).then_inc(tr_free[TURN["par"] % 2], 1)
            mixer(0)

            def hidden2(g, tr, first):
                for th in range(TH):
                    dve.wait_ge(g_ready, g + th)
                    if not first:
                        dve.wait_ge(ht_tr, tr)
                    tt(v_flat[:, (2 + th) * FC:(3 + th) * FC], v_flat[:, th * FC:(th + 1) * FC], PJ[th][:, FC:2 * FC],
                       MUL).then_inc(h_done, 1)

            def hidden_lo(n, cols):
                dve.wait_ge(ht_hi_ready, n)
                tt(ht_lo[:, :, 0:cols], TR[0][:, 0:2 * cols].rearrange("p (f s) -> p f s", f=2),
                   ht_hi[:, :, 0:cols].bitcast(f32), SUB).then_inc(ht_lo_ready, 1)

            t = T_FFN0

            def split_turn(i, tile):
                split(tile, (t + 2 + i) % 3, raw[:, raw_slot(t + 2 + i), :])
            split_turn(0, t + 2)
            hidden2(1, 0, True)
            split_turn(1, t + 3)
            split_turn(2, t + 4)
            hidden_lo(1, SEQ)
            with dve.Fori(1, NCH - 1) as c:
                split_turn(0, c * 3 + (t + 2))
                hidden2(c * 2 + 1, c, False)
                split_turn(1, c * 3 + (t + 3))
                split_turn(2, c * 3 + (t + 4))
                hidden_lo(c + 1, SEQ)
            hidden2(2 * NCH - 1, NCH - 1, False)
            split_static(T_MIX1 - 1)
            hidden_lo(NCH, SEQ)
            split_static(T_MIX1)
            split_static(T_MIX1 + 1)
            dve.wait_ge(tile_used, T_MIX1)
            for i in range(4):
                z = xres[:, i // 2, (i % 2) * 512:(i % 2 + 1) * 512]
                tt(z, z, banks[2 + i][:, :], ADD).then_inc(x_added, 1)
            norm(2, xn_ready)
            mixer(1)

            bank = wait_turn(dve, "router")
            dve.tensor_copy(r_logit, bank[:, 0:16].rearrange("p (t e) -> p t e", t=2)).then_inc(tr_free[TURN["router"] % 2], 1)
            wait_read(dve, "router")
            for th in range(TH):
                own.step(dve.max(r_best[:, th, :], r_logit[:, th, :]))
                own.step(dve.max_index(r_index[:, th, :], r_best[:, th, :], r_logit[:, th, :]))
            tt(r_diff, r_best[:, :, 1], r_best[:, :, 0], SUB).then_inc(sel_early, 1)
            own.step(dve.tensor_copy(r_indexf, r_index[:, :, 0:2]))
            experts_row = cst[:, C_IOTA:C_IOTA + NE]
            for th in range(TH):
                for i in range(2):
                    own.step(ts(r_hot[:, i, th, :], experts_row, r_indexf[:, th, i:i + 1], None, ALU.is_equal))
            tt(sel, r_hot[:, 0, :, :], r_hot[:, 1, :, :], ADD).then_inc(sel_ready, 1)
            own.step(dve.memset(cols, 0.0))
            own.step(dve.memset(cols[:, 0, :, :], -1000.0))
            dve.wait_ge(gate_exp, 1)
            own.step(ts(r_g, r_exp, 1.0, None, ADD))
            own.step(dve.reciprocal(r_g, r_g))
            own.step(tt(r_exp, r_exp, r_g, MUL))
            for i, g in enumerate((r_g, r_exp)):
                own.step(tt(r_hot[:, i, :, :], r_hot[:, i, :, :], g.unsqueeze(2).broadcast_to([P, 2, NE]), MUL))
            own.step(tt(cols[:, 1, :, 0:NE], r_hot[:, 0, :, :], r_hot[:, 1, :, :], ADD))
            bank = wait_turn(dve, "pos")
            pos = bank[:, 0:16].rearrange("p (t e) -> p t e", t=2)
            own.step(stt(r_pos, pos, 1.0, sel, ADD, MUL))
            own.step(ts(cols[:, 0, :, 0:NE], r_pos, -1.0, None, ADD))
            ts(r_over, bank[:, 16:24], float(P), None, ALU.is_gt).then_inc(tr_free[TURN["pos"] % 2], 1)
            wait_read(dve, "pos")
            own.step(dve.tensor_tensor_scan(r_rank, cst[:, C_ONE:C_ONE + NE], r_over, 0.0, MUL, ADD))
            own.step(ts(r_tab[:, 0:1], r_rank[:, NE - 1:NE], float(NE), None, ADD))
            own.step(ts(r_pos, cols[:, 0, :, 0:NE], 1000.0 - P, None, ADD))
            for k in range(MAXB - NE):
                own.step(stt(r_one, r_rank, float(k + 1), r_over, ALU.is_equal, MUL))
                own.step(tt(r_tmp[:, 0, :], r_one, experts_row, MUL))
                own.step(dve.tensor_reduce(r_tab[:, k + 1:k + 2], r_tmp[:, 0, :], AX.X, ADD))
                one = r_one.unsqueeze(1).broadcast_to([P, 2, NE])
                own.step(tt(r_tmp, r_pos, one, MUL))
                own.step(dve.tensor_reduce(cols[:, 0, :, NE + k], r_tmp, AX.X, ADD))
                own.step(ts(cols[:, 0, :, NE + k], cols[:, 0, :, NE + k], -1000.0, None, ADD))
                own.step(tt(r_tmp, cols[:, 1, :, 0:NE], one, MUL))
                own.step(dve.tensor_reduce(cols[:, 1, :, NE + k], r_tmp, AX.X, ADD))
            dve.tensor_copy(table[:, :], r_tab).then_inc(routed, 1)

            def places(dst, scaled):
                for th in range(TH):
                    if scaled:
                        m = ts(dst[:, th, :], cst[:, C_IOTA:C_IOTA + P], column[:, 0, th:th + 1], column[:, 1, th:th + 1],
                               ALU.is_equal, MUL)
                    else:
                        m = ts(dst[:, th, :], cst[:, C_IOTA:C_IOTA + P], column[:, 0, th:th + 1], None, ALU.is_equal)
                return m

            def gathered(n):
                dve.wait_ge(xe_hi_ready, n)
                for g in range(2):
                    m = tt(at_lo[:, 4 * g:4 * g + 4, 0:P], banks[4 + g][:, :].rearrange("p (k c) -> p k c", k=4),
                           at_hi[:, 4 * g:4 * g + 4, 0:P].bitcast(f32), SUB)
                m.then_inc(xe_lo_ready, 1)

            own.step(dve.tensor_copy(column, cols[:, :, :, 0]))
            places(place, False).then_inc(place_ready, 1)
            gathered(1)
            dve.wait_ge(routed, 1)
            nb = dve.value_load(table[0:1, 0:1], min_val=NE, max_val=MAXB)
            with dve.Fori(0, nb) as b:
                own.loop(b, 3)

                def split_moe(j):
                    split(b * FFN_TILES + (T_MOE + j), (T_MOE + j) % 3, raw[:, moe_slot(j), :])

                def hidden(c):
                    dve.wait_ge(g_ready, b * NCH + (2 * NCH + c + 1))
                    dve.wait_ge(ht_tr, b * NCH + (NCH + c))
                    tt(v_flat[:, FC:2 * FC], v_flat[:, 0:FC], banks[c % 2][:, FC:2 * FC], MUL).then_inc(h_done, 1)

                split_moe(0)
                split_moe(1)
                for c in range(NCH - 1):
                    split_moe(3 * c + 2)
                    hidden(c)
                    split_moe(3 * c + 3)
                    split_moe(3 * c + 4)
                    hidden_lo(b * NCH + (NCH + c + 1), P)
                    if c == 4:
                        dve.wait_ge(place_ready, b + 1)
                        own.step(dve.tensor_copy(column, cols[:, :, :, bass.ds(b, 1)].rearrange("p a t o -> p a (t o)")))
                        own.step(places(gated_places, True))
                        own.step(dve.tensor_copy(column, cols[:, :, :, bass.ds(b + 1, 1)].rearrange("p a t o -> p a (t o)")))
                        places(place, False).then_inc(place_ready, 1)
                hidden(NCH - 1)
                split_moe(FFN_TILES - 1)
                gathered(b + 2)
                hidden_lo(b * NCH + 2 * NCH, P)
                dve.wait_ge(tile_used, b * FFN_TILES + (T_MOE + FFN_TILES))
                dve.tensor_copy(u_flat[:, 512:1024], banks[3][:, :]).then_inc(ye_ready, 1)
                for i in range(4):
                    z = xres[:, i // 2, (i % 2) * 512:(i % 2 + 1) * 512]
                    dve.wait_ge(comb_full, b * 4 + (i + 1))
                    tt(z, z, (TR[1], banks[2], banks[3], TR[0])[i][:, :], ADD).then_inc(x_added, 1)
                own.end()
            dve.wait_ge(sq_ready, 5)
            ts(col(VAR, 2), col(SS, 2), 1.0 / D, EPS, MUL, ADD).then_inc(var_ready, 1)
            dve.wait_ge(root_ready, 5)
            dve.reciprocal(col(RI, 2), col(RT, 2)).then_inc(inv_ready, 1)
            dve.wait_ge(inv_ready, 1)
            dve.wait_ge(gain_in, 80)
            for th in range(TH):
                stt(xn[:, th, :], xres[:, th, :], col(RI + th), gain, MUL, MUL).then_inc(final_ready, 1)

        @block.gpsimd
        def _(pool):
            own = Order(pool, pool_own)
            tt = pool.tensor_tensor

            def cmul(out_re, out_im, a, a_swapped, b_re, b_im, t1, t2):
                tt(t1, a, b_re, MUL)
                own.step(tt(t2, a_swapped, b_im, MUL))
                tt(out_re, t1[:, 0], t2[:, 0], SUB)
                own.step(tt(out_im, t1[:, 1], t2[:, 1], ADD))

            def load_matrices(l):
                for r, src in enumerate((ssm_b_re, ssm_b_im)):
                    v = src[l, :, :, :, :].rearrange("d g s h -> (d g) s h").rearrange("(j g) s h -> g s j h", g=2)
                    for g in range(2):
                        pool.dma_start(braw[64 * g:64 * (g + 1), r, :, :], v[g, :, :, :]).then_inc(bc_in, 16)
                for r, src in enumerate((ssm_c_re, ssm_c_im)):
                    for a in range(2):
                        pool.dma_start(craw[r][:, :, a, :], src[l, :, :, :, :].rearrange("d g h s -> (d g h) s")
                                       .rearrange("(i p) s -> p i s", p=P)).then_inc(bc_in, 16)

            def load_dskip(l):
                for q2 in range(2):
                    for t in range(2):
                        r0 = q2 * 64 + t * 32
                        pool.dma_start(dskip[r0:r0 + 32, l, :],
                                       ssm_d[l, :].rearrange("(b q c) -> q c b", b=8, q=2)[q2, :, :],
                                       allow_slow_non_contiguous=True).then_inc(dskip_in, 16)

            def signal_mats():
                pool.memset(zero_mark, 0.0).then_inc(mats_ready, 1)

            def build(l):
                j0 = 32 * l

                def num(i):
                    return par[:, i, j0:j0 + 32]
                sq = [area(TMP + 3072 + 64 * i, 64).rearrange("p (r j) -> p r j", r=2) for i in range(2)]
                def small_t(t, n):
                    return t.rearrange("p r j h -> p (r j h)")[:, 0:64 * n].rearrange("p (r j n) -> p r j n", r=2, j=32)

                def square(dst, src):
                    t1, t2 = (small_t(t, 1)[:, :, :, 0] for t in (bt1, bt2))
                    cmul(dst[:, 0, :], dst[:, 1, :], src, src[:, ::-1, :], src[:, 0:1, :].broadcast_to([P, 2, 32]),
                         src[:, 1:2, :].broadcast_to([P, 2, 32]), t1, t2)
                square(sq[0], par[:, COS:SIN + 1, j0:j0 + 32])
                power = 0
                for tab, n in ((w1t, 16), (w16t, 8)):
                    pool.memset(tab[:, 0, :, 0:1], 1.0)
                    pool.memset(tab[:, 1, :, 0:1], 0.0)
                    own.step(pool.tensor_copy(tab[:, :, :, 1], sq[power % 2]))
                    k = 2
                    while k < n:
                        square(sq[(power + 1) % 2], sq[power % 2])
                        power += 1
                        p = sq[power % 2]
                        t1, t2 = small_t(bt1, k), small_t(bt2, k)
                        a = tab[:, :, :, 0:k]
                        cmul(tab[:, 0, :, k:2 * k], tab[:, 1, :, k:2 * k], a, a[:, ::-1, :, :],
                             p[:, 0:1, :].unsqueeze(3).broadcast_to([P, 2, 32, k]),
                             p[:, 1:2, :].unsqueeze(3).broadcast_to([P, 2, 32, k]), t1, t2)
                        k *= 2
                    square(sq[(power + 1) % 2], sq[power % 2])
                    power += 1

                def times(dst, src, re, im):
                    cmul(dst[:, 0], dst[:, 1], src, src[:, ::-1, :, :],
                         num(re).unsqueeze(1).unsqueeze(3).broadcast_to([P, 2, 32, GC]),
                         num(im).unsqueeze(1).unsqueeze(3).broadcast_to([P, 2, 32, GC]), bt1, bt2)
                pool.memset(gflat, 0.0)
                pool.wait_ge(bc_in, BC_LOADS * (l + 1))
                times(bbar, braw, CO_RE, CO_IM)
                times(babar, bbar, A_RE, A_IM)
                signal_mats()
                wait_read(pool, (l, "ct", 2))
                wait_read(pool, (l, "ct", 3))
                times(cabar, ctr, A_RE, A_IM)
                signal_mats()

            def phases(l, q):
                w = wtab[q % 2]
                n = 16 * l + q
                if q >= 2:
                    pool.wait_ge(pv_free, n - 1)
                    pool.wait_ge(states_ready, n - 1)

                def one(r):
                    return w1t[:, r, q::PAIRS, :].unsqueeze(2).broadcast_to([P, 2, 8, 16])

                def sixteen(r):
                    return w16t[:, r, q::PAIRS, :].unsqueeze(3).broadcast_to([P, 2, 8, 16])

                def quarter(t, i):
                    return t[:, i, :].rearrange("p (d a c) -> p d a c", d=2, a=8)
                tt(quarter(po1, 0), one(0), sixteen(0), MUL)
                tt(quarter(po1, 1), one(1), sixteen(1), MUL)
                tt(quarter(po2, 0), one(0), sixteen(1), MUL)
                own.step(tt(quarter(po2, 1), one(1), sixteen(0), MUL))
                tt(w[:, 0, :], po1[:, 0, :], po1[:, 1, :], SUB)
                tt(w[:, 1, :], po2[:, 0, :], po2[:, 1, :], ADD).then_inc(wtab_ready, 1)
                pool.wait_ge(wtab_ready, n + 1)

            def decay(l, q):
                tt(r2t.rearrange("p (d c) -> p d c", d=2), cst[:, C_MASK:C_MASK + P].unsqueeze(1).broadcast_to([P, 2, P]),
                   par[:, RAD2, 32 * l + q:32 * l + 32:PAIRS].unsqueeze(2).broadcast_to([P, 2, P]), MUL).then_inc(r2_ready, 1)

            def turn_forward(l, q):
                n = 16 * l + q
                w, xs = wtab[q % 2], xst[q % 2]
                pool.wait_ge(zs_ready, n + 1)
                tt(po1, zs, w[:, 0:1, :].broadcast_to([P, 2, 256]), MUL)
                tt(po2, zs[:, ::-1, :], w[:, 1:2, :].broadcast_to([P, 2, 256]), MUL).then_inc(zs_used, 1)
                pool.wait_ge(zs_used, n + 1)
                if n >= 2:
                    pool.wait_ge(y_done, n - 1)
                for r, op in enumerate((SUB, ADD)):
                    for d in range(2):
                        dst = xs[:, r, 0, 1:P + 1] if d == 0 else xs[:, r, 1, P - 1::-1]
                        m = tt(dst, po1[:, r, d * P:(d + 1) * P], po2[:, r, d * P:(d + 1) * P], op)
                m.then_inc(states_ready, 1)

            load_matrices(0)
            load_dskip(0)
            load_dskip(1)
            pool.memset(area(4096, 4096), 0.0)
            wait_read(pool, "par")
            for l in range(2):
                if l == 1:
                    pool.wait_ge(y_done, PAIRS)
                    load_matrices(1)
                    pool.wait_ge(at_lo_ready, at_count(0, "m", 3))
                build(l)
                pool.wait_ge(blocks_ready, l + 1)
                pool.wait_ge(mats_ready, 2 * l + 2)
                for xs in xst:
                    pool.memset(xs[:, :, 0, 0:1], 0.0)
                    pool.memset(xs[:, :, 1, P:P + 1], 0.0)
                phases(l, 0)
                decay(l, 0)
                for q in range(PAIRS):
                    if q + 1 < PAIRS:
                        phases(l, q + 1)
                    turn_forward(l, q)
                    if q + 1 < PAIRS:
                        decay(l, q + 1)


_INS = ["x", "norm_mix", "w_in", "attn_lambda", "attn_subln", "ssm_lam_re", "ssm_lam_im", "ssm_log_dt", "ssm_b_re",
        "ssm_b_im", "ssm_c_re", "ssm_c_im", "ssm_d", "w_glu", "w_branch", "w_out", "norm_ffn", "ffn_w1", "ffn_w3",
        "ffn_w2", "moe_router", "moe_w1", "moe_w3", "moe_w2", "norm_final"]


def shape_constants():
    import numpy as np
    c = np.zeros((P, C_END), np.float32)
    c[:, C_ID:C_ID + P] = np.eye(P)
    c[:, C_TRI:C_TRI + P] = np.triu(np.ones((P, P)), 1)
    c[:, C_ONE:C_ONE + P] = 1.0
    c[:, C_IOTA:C_IOTA + P] = np.arange(P)
    c[:, C_MASK:C_MASK + P] = np.arange(P) > 0
    c[:, C_PAT:C_PAT + 32] = (np.arange(P)[:, None] % 32) == np.arange(32)
    half = HD // 2
    freq = (1.0 / (np.float32(10000.0) ** (np.arange(half, dtype=np.float32) / np.float32(half)))).astype(np.float32)
    pos = (2 * np.arange(P)[:, None] + np.arange(TH)).astype(np.float32)
    ang = (pos[:, :, None] * freq).astype(np.float32).astype(np.float64)
    c[:, C_COS:C_COS + P] = np.concatenate([np.cos(ang), np.cos(ang)], -1).reshape(P, P)
    c[:, C_SIN:C_SIN + P] = np.concatenate([-np.sin(ang), np.sin(ang)], -1).reshape(P, P)
    return c


def kernel(**inputs):
    import numpy as _np
    import concourse.bacc as _bacc
    from concourse import mybir as _mybir
    from concourse.bass_utils import run_bass_kernel_spmd as _run

    nc = _bacc.Bacc("TRN2", target_bir_lowering=False, num_devices=1)
    arrays, args = {}, []
    for name in _INS + ["consts"]:
        a = shape_constants() if name == "consts" else _np.ascontiguousarray(inputs[name])
        arrays[f"in_{name}_dram"] = a
        args.append(nc.dram_tensor(f"in_{name}_dram", a.shape, _mybir.dt.from_np(a.dtype), kind="ExternalInput").ap())
    args.append(nc.dram_tensor("out_0_dram", (1, SEQ, D), _mybir.dt.float32, kind="ExternalOutput").ap())
    build(nc, *args)
    r = _run(nc, [arrays], core_ids=[0])
    return r.results[0]["out_0_dram"]
```

```python
import math
import concourse.bass as bass
from concourse import mybir
from contextlib import ExitStack

P = 128
SEQ, D = 256, 1024
TH = SEQ // P
KD = D // P
HEADS, HD = 4, 64
WA = HEADS * 2 * HD
NGATE = 2
IN_WIDTH = 4 * WA + NGATE * D
D_FF = 2816
NE = 8
MAXB = NE + 3
PAIRS, GC, NS = 16, 16, 64
EPS = 1e-6
TW = 2048
RAWS, SPLITS = 11, 3
FC = 256
NCH = D_FF // FC
MIX_TILES, FFN_TILES = 25, 3 * NCH
T_FFN0 = MIX_TILES
T_MIX1 = T_FFN0 + FFN_TILES
T_MOE = T_MIX1 + MIX_TILES
T_MIX = (0, T_MIX1)
C_ID, C_TRI, C_ONE, C_IOTA, C_MASK, C_PAT, C_COS, C_SIN = 0, 128, 256, 384, 512, 640, 672, 800
C_END = 928

W_IN_ORDER = [3, 0, 1, 2, 4, 5, 6, 7]


def mixer_turns():
    names = ["par"]
    for l in range(2):
        names += [(l, "x", g) for g in range(4)] + [(l, "ct", g) for g in range(4)]
        names += [(l, "u", g) for g in range(2)] + [(l, "q", t) for t in range(2)] + [(l, "k", t) for t in range(2)]
        names += [(l, "b", g) for g in range(8)] + [(l, "cb", 0)]
        for s in range(9):
            if s < 8:
                names.append((l, "sc", s))
            if s > 0:
                names.append((l, "o", s - 1))
        names += [(l, "a", t) for t in range(2)] + [(l, "s", t) for t in range(2)] + [(l, "s2", t) for t in range(2)]
        names += [(l, "m", g) for g in range(4)] + [(l, "h", g) for g in range(4)]
    names += ["router", "pos"]
    return {name: n for n, name in enumerate(names)}


TURN = mixer_turns()
AT_ORDER = {name: n for n, name in enumerate(
    [("x", g) for g in range(4)] + [("a", t) for t in range(2)] + [("sa", i) for i in range(2)]
    + [("s2", t) for t in range(2)] + [("m", g) for g in range(4)] + [("h", g) for g in range(4)])}
AT_PER_LAYER = len(AT_ORDER)
AHEAD = 8
PJ_PER_LAYER = 15


class Order:

    def __init__(self, eng, sem):
        self.eng, self.sem, self.n, self.turn, self.per = eng, sem, 0, None, 0

    def step(self, ins):
        ins.then_inc(self.sem, 1)
        self.n += 1
        self.eng.wait_ge(self.sem, self.n if self.turn is None else self.turn * self.per + self.n)

    def loop(self, turn, per):
        self.turn, self.per, self.start = turn, per, self.n

    def end(self, trips=None):
        assert self.n - self.start == self.per, (self.n - self.start, self.per)
        self.turn = None
        if trips is not None:
            self.n = self.start + trips * self.per


def build(nc, x, norm_mix, w_in, attn_lambda, attn_subln, ssm_lam_re, ssm_lam_im, ssm_log_dt, ssm_b_re, ssm_b_im,
          ssm_c_re, ssm_c_im, ssm_d, w_glu, w_branch, w_out, norm_ffn, ffn_w1, ffn_w3, ffn_w2, moe_router,
          moe_w1, moe_w3, moe_w2, norm_final, consts, out):
    f32, f32r, i32, u32 = mybir.dt.float32, mybir.dt.float32r, mybir.dt.int32, mybir.dt.uint32
    ACT, ALU, AX = mybir.ActivationFunctionType, mybir.AluOpType, mybir.AxisListType
    MUL, ADD, SUB = ALU.mult, ALU.add, ALU.subtract
    ctx = ExitStack()
    with ctx:
        def sb(name, shape, dt=f32):
            return ctx.enter_context(nc.sbuf_tensor(name, shape, dt))

        def sem(name):
            return ctx.enter_context(nc.semaphore(name))

        raw = sb("raw", [P, RAWS, TW])
        hi = sb("hi", [P, SPLITS, TW], f32r)
        lo = sb("lo", [P, SPLITS, TW], f32r)
        at_hi = sb("at_hi", [P, KD, SEQ], f32r)
        at_lo = sb("at_lo", [P, KD, SEQ], f32r)
        ht_hi = sb("ht_hi", [P, 2, SEQ], f32r)
        ht_lo = sb("ht_lo", [P, 2, SEQ], f32r)
        xres = sb("xres", [P, TH, D])
        gates = sb("gates", [P, TH, NGATE, D])
        qk = sb("qk", [P, 2, TH, WA])
        vreg = sb("vreg", [P, TH, WA])
        ureg = sb("ureg", [P, TH, WA])
        areg = sb("areg", [P, TH, WA])
        cst = sb("cst", [P, C_END])
        par = sb("par", [P, 7, 64])
        subln = sb("subln", [P, 2, P])
        small = sb("small", [P, 96])
        php_last = sb("php_last", [P, 256])
        sum_ready = sem("sum_ready")
        half_scores, b_laid = sem("half_scores"), sem("b_laid")
        table = sb("table", [P, 5], i32)

        ident = cst[:, C_ID:C_ID + P]
        xn = qk[:, :, :, :].rearrange("p a t c -> p (a t c)").rearrange("p (t d) -> p t d", t=TH)
        gain = areg[:, :, :].rearrange("p t c -> p (t c)")
        gflat = gates[:, :, :, :].rearrange("p t g d -> p (t g d)")
        ssm = raw[:, 3:RAWS, :].rearrange("p s w -> p (s w)")

        def area(start, size):
            return ssm[:, start:start + size]
        bbt = area(0, 4096).rearrange("p (d r b c) -> p d r b c", d=2, r=2, b=8)
        cblk = area(4096, 4096).rearrange("p (k r d q g h) -> p k r d q g h", k=2, r=2, d=2, q=PAIRS, g=2)
        ut2 = area(8192, 1024).rearrange("p (b c) -> p b c", b=8)
        cbm = area(9216, 256).rearrange("p (b c) -> p b c", b=8)
        w1t = area(9472, 1024).rearrange("p (r j c) -> p r j c", r=2, c=16)
        w16t = area(10496, 512).rearrange("p (r j c) -> p r j c", r=2, c=8)
        TMP = 11008
        wtab = [area(TMP + 512 * i, 512).rearrange("p (r c) -> p r c", r=2) for i in range(2)]
        rot1 = area(TMP + 1280, 512).rearrange("p (r c) -> p r c", r=2)
        rot2 = area(TMP + 1792, 512).rearrange("p (r c) -> p r c", r=2)
        zs = area(TMP + 2304, 512).rearrange("p (r c) -> p r c", r=2)
        po1 = area(TMP + 2816, 512).rearrange("p (r c) -> p r c", r=2)
        po2 = area(TMP + 3328, 512).rearrange("p (r c) -> p r c", r=2)
        xst_flat = [area(TMP + 3840 + 516 * i, 516).rearrange("p (r c) -> p r c", r=2) for i in range(2)]
        xst = [x2.rearrange("p r (d c) -> p r d c", d=2) for x2 in xst_flat]
        php = [area(TMP + 1024, 256), area(TMP + 4872, 256), php_last[:, :]]

        def four(ap):
            return ap.rearrange("p (r j h) -> p r j h", r=2, h=GC)
        braw, bt1, bt2 = four(area(0, 1024)), four(area(1024, 1024)), four(area(2048, 1024))
        bbar, babar, ctr, cabar = [four(area(TMP + 1024 * i, 1024)) for i in range(4)]
        craw = [area(c0, 1024).rearrange("p (i a s) -> p i a s", i=8, a=2) for c0 in (8192, TMP + 4096)]
        bpre = gflat.rearrange("p (d r b q t g h) -> p d r b q t g h", d=2, r=2, b=8, q=2, t=2, g=2)

        banks = [ctx.enter_context(nc.psum_tensor(f"bank{i}", [P, 512], f32)) for i in range(8)]
        PJ, PY, PV, TR = banks[0:2], banks[2:4], banks[4:6], banks[6:8]

        raw_full = [sem(f"raw_full{i}") for i in range(RAWS)]
        hi_ready, lo_ready, tile_used = sem("hi_ready"), sem("lo_ready"), sem("tile_used")
        loads = sem("loads")
        rows_in, lam_in = sem("rows_in"), sem("lam_in")
        router_hi_ready, router_ready = sem("router_hi_ready"), sem("router_ready")
        gain_in = sem("gain_in")
        bc_in = sem("bc_in")
        dskip_in = sem("dskip_in")
        sq_ready, var_ready, root_ready, xn_ready = sem("sq_ready"), sem("var_ready"), sem("root_ready"), sem("xn_ready")
        tr_full = sem("tr_full")
        tr_free = [sem("tr_free0"), sem("tr_free1")]
        at_hi_ready, at_lo_ready = sem("at_hi_ready"), sem("at_lo_ready")
        pj0_full = sem("pj0_full")
        pj_free = [sem("pj_free0"), sem("pj_free1")]
        dve_own, pool_own, act_own = sem("dve_own"), sem("pool_own"), sem("act_own")
        act_par, dve_par = sem("act_par"), sem("dve_par")
        rot_ready = sem("rot_ready")
        v_ready = sem("v_ready")
        mats_ready, blocks_ready, bbt_ready, cbm_ready = sem("mats_ready"), sem("blocks_ready"), sem("bbt_ready"), sem("cbm_ready")
        ct_ready, bzero_ready, small_tabs = sem("ct_ready"), sem("bzero_ready"), sem("small_tabs")
        pv_full, pv_free, wtab_ready, php_ready = sem("pv_full"), sem("pv_free"), sem("wtab_ready"), sem("php_ready")
        zs_ready, zs_used, states_ready, y_done = sem("zs_ready"), sem("zs_used"), sem("states_ready"), sem("y_done")
        max_ready, exp_ready, w_ready, wt_tr, wt_ready = sem("max_ready"), sem("exp_ready"), sem("w_ready"), sem("wt_tr"), sem("wt_ready")
        o_ready, avar_ready, aroot_ready, a_ready = sem("o_ready"), sem("avar_ready"), sem("aroot_ready"), sem("a_ready")
        s_ready, tg_ready, s2_ready, gate_ready, m_ready, x_added = (sem("s_ready"), sem("tg_ready"), sem("s2_ready"),
                                                                     sem("gate_ready"), sem("m_ready"), sem("x_added"))
        qk_t_ready, u_ready, lam_ready, lam_exp = sem("qk_t_ready"), sem("u_ready"), sem("lam_ready"), sem("lam_exp")
        h_full, g_ready, h_done, ht_tr, ht_hi_ready, ht_lo_ready = (sem("h_full"), sem("g_ready"), sem("h_done"), sem("ht_tr"),
                                                                    sem("ht_hi_ready"), sem("ht_lo_ready"))
        ffn_done = sem("ffn_done")
        sel_ready, pos_full, routed, final_ready, stored = (sem("sel_ready"), sem("pos_full"), sem("routed"),
                                                            sem("final_ready"), sem("stored"))
        gate_exp, router_in, place_ready, pg_full, gt_ready = (sem("gate_exp"), sem("router_in"), sem("place_ready"),
                                                               sem("pg_full"), sem("gt_ready"))
        ye_hi_ready = sem("ye_hi_ready")
        xe_full, xe_hi_ready, xe_lo_ready, ye_ready, comb_full = (sem("xe_full"), sem("xe_hi_ready"), sem("xe_lo_ready"),
                                                                  sem("ye_ready"), sem("comb_full"))
        out_ready = sem("out_ready")
        def raw_slot(t):
            return t % 3

        def raw_uses(slot, before):
            return sum(1 for t in range(before) if raw_slot(t) == slot)

        def moe_slot(j):
            return (list(range(3, RAWS)) + [raw_slot(T_MOE - 3 + i) for i in range(3)])[j % RAWS]

        def moe_tile(j):
            if j < 2:
                return "ab"[j], 0, 0
            c, i = (j - 2) // 3, (j - 2) % 3
            g = c if i == 2 else c + 1
            return "abc"[i], g % NCH, g // NCH

        def moe_full_value(j, turn):
            s = moe_slot(j)
            base = raw_uses(s, T_MOE) if s < 3 else 0
            first = min(i for i in range(FFN_TILES) if moe_slot(i) == s)
            return turn * (32 * FFN_TILES // RAWS) + 32 * (base + (j - first) // RAWS + 1)

        SS, VAR, RT, RI, MX, NB, RS, RR, C1 = 0, 2, 4, 6, 8, 10, 12, 14, 16
        SS2 = 94
        AS, AV, AR, AI, LSUM, LEXP, NLAM = 24, 32, 40, 48, 56, 60, 64

        def col(i, n=1):
            return small[:, i:i + n]

        def row(i, n=1):
            return gflat[0:64, i * P:(i + n) * P]
        lamv = gflat[:, 4 * P:8 * P].rearrange("p (l a b c) -> p l a b c", l=2, a=2, b=2)
        lamp = gflat[:, 26 * P:28 * P].rearrange("p (j c) -> p j c", c=HD)
        R_LR, R_LI, R_DT, R_EDT, R_lr, R_li, R_k, R_red, R_er, R_sn, R_sh, R_t, R_u, R_den, R_am = (
            0, 1, 2, 3, 8, 9, 10, 11, 12, 13, 14, 15, 23, 24, 25)
        PACK = 16
        A_RE, A_IM, CO_RE, CO_IM, COS, SIN, RAD2 = range(7)

        kflat = qk[:, 1, :, :].rearrange("p t c -> p (t c)")
        probs = kflat[:, 0:512].rearrange("p (a k) -> p a k", a=2)
        wdiff = kflat[:, 512:768]
        wdiff_t = kflat[:, 768:1024].rearrange("p (t q) -> p t q", t=2)
        u_rows = ureg[:, :, :].rearrange("p t c -> p (t c)").rearrange("p (q t c) -> p q t c", q=PAIRS, t=TH)
        u_flat = ureg[:, :, :].rearrange("p t c -> p (t c)")
        q_t = u_flat.rearrange("p (h s) -> p h s", h=HEADS)
        k_t = qk[:, 0, :, :].rearrange("p t c -> p (t c)").rearrange("p (h s) -> p h s", h=HEADS)
        s_t = u_flat.rearrange("p (k s) -> p k s", k=4)
        s_gated = qk[:, 0, :, :]
        a_flat = areg[:, :, :].rearrange("p t c -> p (t c)")
        v_flat = vreg[:, :, :].rearrange("p t c -> p (t c)")

        free_at, seen = {}, [0, 0]
        for name, n in TURN.items():
            if name != "par" and name[1:] in AT_ORDER:
                free_at[name] = (at_lo_ready, name[0] * AT_PER_LAYER + AT_ORDER[name[1:]] + 1)
            else:
                seen[n % 2] += 1
                free_at[name] = (tr_free[n % 2], seen[n % 2])
        NAME = {n: name for name, n in TURN.items()}

        def at_count(l, kind, g):
            return l * AT_PER_LAYER + AT_ORDER[(kind, g)] + 1

        def wait_read(eng, name):
            s, v = free_at[name]
            eng.wait_ge(s, v)

        def wait_turn(eng, name):
            eng.wait_ge(tr_full, TURN[name] + 1)
            return TR[TURN[name] % 2]

        def use(l, i):
            return PJ_PER_LAYER * l + i

        def pj_read(l, i):
            return (PJ_PER_LAYER - 2) * l + i + 1


        def piece(start, size):
            return gflat[:, start:start + size]
        cols = piece(256, 48).rearrange("p (a t e) -> p a t e", a=2, t=2)
        column = small[:, 72:76].rearrange("p (a t) -> p a t", a=2)
        r_logit = piece(320, 16).rearrange("p (t e) -> p t e", t=2)
        r_best = piece(336, 16).rearrange("p (t e) -> p t e", t=2)
        r_index = piece(352, 16).rearrange("p (t e) -> p t e", t=2).bitcast(u32)
        r_indexf = piece(368, 4).rearrange("p (t e) -> p t e", t=2)
        r_diff, r_exp, r_g = piece(372, 2), piece(374, 2), piece(376, 2)
        r_hot = piece(384, 32).rearrange("p (i t e) -> p i t e", i=2, t=2)
        sel = piece(416, 16).rearrange("p (t e) -> p t e", t=2)
        r_pos = piece(432, 16).rearrange("p (t e) -> p t e", t=2)
        r_over, r_rank, r_one = piece(448, 8), piece(456, 8), piece(464, 8)
        r_tmp = piece(472, 16).rearrange("p (t e) -> p t e", t=2)
        r_tab = piece(488, 5)
        router = piece(512, 64).rearrange("p (k e) -> p k e", k=KD)
        router_parts = ht_hi[:, 0, 0:KD * 2 * NE].rearrange("p (k c) -> p k c", k=KD)
        place = vreg[:, 1, 0:256].rearrange("p (t s) -> p t s", t=2)
        dskip = small[:, 76:92].rearrange("p (l b) -> p l b", l=2)
        zero_mark = small[:, 92:93]
        dve_rows, sel_early, inv_ready = sem("dve_rows"), sem("sel_early"), sem("inv_ready")
        BC_LOADS = 16 * 8
        place_gate = small[:, 93:94]
        comb_banks = (TR[0], TR[1], PV[0], PV[1])

        def phase_product(tt, dst, l, q, r1, r16):
            return tt(dst.rearrange("p (d a c) -> p d a c", d=2, a=8),
                      w1t[:, r1, q::PAIRS, :].unsqueeze(2).broadcast_to([P, 2, 8, 16]),
                      w16t[:, r16, q::PAIRS, :].unsqueeze(3).broadcast_to([P, 2, 8, 16]), MUL)

        def h_bank(c):
            return TR[1] if c % NCH == NCH - 1 else PJ[c % NCH % 2]

        block = ctx.enter_context(nc.Block())

        @block.sync
        def _(sp):
            sp.dma_start(xres[:, :, :], x[0, :, :].rearrange("(p t) d -> p t d", t=TH)).then_inc(loads, 16)
            sp.dma_start(cst[:, :], consts).then_inc(loads, 16)
            sp.wait_ge(rows_in, 48)

            def load(slot, parts):
                for dst, src in parts:
                    sp.dma_start(dst, src).then_inc(raw_full[slot], 16)

            def split_k(slot, w, k0, c0, n):
                kk = TW // n
                dst = raw[:, slot, :].rearrange("p (k c) -> p k c", c=n)
                src = w[k0 * P:(k0 + kk) * P, c0:c0 + n].rearrange("(k p) c -> p k c", p=P)
                return [(dst[:, h * kk // 2:(h + 1) * kk // 2, :], src[:, h * kk // 2:(h + 1) * kk // 2, :]) for h in range(2)]

            def ffn_parts(slot, kind, c, w1, w3, w2):
                if kind == "c":
                    return split_k(slot, w2, c * FC // P, 0, D)
                k0 = 0 if kind == "a" else KD // 2
                dst = raw[:, slot, :].rearrange("p (k w c) -> p k w c", w=2, c=FC)
                return [(dst[:, :, i, :],
                         w[k0 * P:(k0 + 4) * P, c * FC:(c + 1) * FC].rearrange("(k p) c -> p k c", p=P))
                        for i, w in enumerate((w1, w3))]

            def static_tile(t, parts):
                slot = raw_slot(t)
                if t >= 3:
                    sp.wait_ge(lo_ready, t - 2)
                load(slot, parts(slot))

            def expert_tile(j, here, after):
                kind, c, which = moe_tile(j)
                m1, m3, m2 = [m[0, bass.ds(after if which else here, 1), :, :].rearrange("e a b -> (e a) b")
                              for m in (moe_w1, moe_w3, moe_w2)]
                load(moe_slot(j), ffn_parts(moe_slot(j), kind, c, m1, m3, m2))

            def mixer(l):
                t = T_MIX[l]
                for n in W_IN_ORDER:
                    for kh in range(2):
                        static_tile(t, lambda s: split_k(s, w_in[l, :, :], 4 * kh, 512 * n, 512))
                        t += 1
                for b, n in ((0, 0), (0, 1), (None, 0), (1, 0), (1, 1)):
                    if l == 1 and (b, n) == (1, 1):
                        sp.wait_ge(y_done, 2 * PAIRS)
                    w = w_glu[l, :, :] if b is None else w_branch[l, b, :, :]
                    static_tile(t, lambda s: split_k(s, w, 0, 512 * n, 512))
                    t += 1
                for n in range(2):
                    for kh in range(2):
                        static_tile(t, lambda s: split_k(s, w_out[l, :, :], 4 * kh, 512 * n, 512))
                        t += 1
                        if l == 1:
                            for j in (4 * n + 2 * kh, 4 * n + 2 * kh + 1):
                                expert_tile(j, 0, 0)

            mixer(0)
            f1, f3, f2 = ffn_w1[0, :, :], ffn_w3[0, :, :], ffn_w2[0, :, :]
            for i, kind in enumerate("ab"):
                static_tile(T_FFN0 + i, lambda s: ffn_parts(s, kind, 0, f1, f3, f2))
            with sp.Fori(0, NCH - 1) as c:
                for i, (kind, ahead) in enumerate((("a", 1), ("b", 1), ("c", 0))):
                    slot = raw_slot(T_FFN0 + 2 + i)
                    sp.wait_ge(lo_ready, 3 * c + (T_FFN0 + 2 + i - 2))
                    if kind == "c":
                        dst = raw[:, slot, :].rearrange("p (f c) -> p f c", c=D)
                        for f in range(2):
                            sp.dma_start(dst[:, f, :], f2[bass.ds(c * FC + f * P, P), :]).then_inc(raw_full[slot], 16)
                    else:
                        k0 = 0 if kind == "a" else 4
                        dst = raw[:, slot, :].rearrange("p (k w c) -> p k w c", w=2, c=FC)
                        for j, w in enumerate((f1, f3)):
                            src = w[k0 * P:(k0 + 4) * P, bass.ds(c * FC + FC, FC)].rearrange("(k p) c -> p k c", p=P)
                            sp.dma_start(dst[:, :, j, :], src).then_inc(raw_full[slot], 16)
            static_tile(T_MIX1 - 1, lambda s: ffn_parts(s, "c", NCH - 1, f1, f3, f2))
            mixer(1)

            def expert(turn, here, after):
                for j in range(AHEAD, FFN_TILES + AHEAD):
                    kind, c, which = moe_tile(j)
                    if after is None:
                        if which:
                            continue
                        j = min(j, FFN_TILES - 1)
                    sp.wait_ge(lo_ready, turn * FFN_TILES + (T_MOE + j - RAWS + 1))
                    if after is None and j == FFN_TILES - 1:
                        m2 = moe_w2[0, bass.ds(here, 1), :, :].rearrange("e a b -> (e a) b")
                        load(moe_slot(j), split_k(moe_slot(j), m2, (NCH - 1) * FC // P, 0, D))
                    else:
                        expert_tile(j, here, after)

            with sp.Fori(0, NE - 1) as e:
                expert(e, e, e + 1)
            sp.wait_ge(routed, 1)
            last = sp.value_load(table[0:1, 0:1], min_val=NE - 1, max_val=MAXB - 1)

            def expert_of(b):
                return sp.value_load(table[0:1, bass.ds(b - (NE - 2), 1)], min_val=0, max_val=NE - 1)
            with sp.If(last > NE - 1):
                with sp.Fori(NE - 1, last) as b:
                    expert(b, expert_of(b), expert_of(b + 1))
            expert(last, expert_of(last), None)
            for th in range(TH):
                sp.wait_ge(final_ready, th + 1)
                sp.dma_start(out[0, :, :].rearrange("(p t) d -> p t d", t=TH)[:, th, :], xn[:, th, :]).then_inc(stored, 16)
            sp.wait_ge(stored, 32)
        @block.tensor
        def _(pe):
            def mm(o, a, b, start, stop):
                return pe.matmul(o, a, b, start=start, stop=stop)

            def three(o, a_hi, a_lo, b_hi, b_lo, start, stop):
                mm(o, a_hi, b_hi, start, False)
                mm(o, a_hi, b_lo, False, False)
                return mm(o, a_lo, b_hi, False, stop)

            def open_turn(name):
                n = TURN[name]
                if n >= 2:
                    wait_read(pe, NAME[n - 2])
                return TR[n % 2]

            def transposes(name, sources):
                bank = open_turn(name)
                for i, src in enumerate(sources):
                    rows = src.shape[0]
                    last = pe.transpose(bank[:, i * rows:(i + 1) * rows], src, ident[0:rows, 0:rows])
                last.then_inc(tr_full, 1)

            def proj(t, l, i, k0, first, last):
                pe.wait_ge(lo_ready, t + 1)
                s = t % SPLITS
                for th in range(TH):
                    if first and i == PJ_PER_LAYER - 1:
                        pe.wait_ge(x_added, 8 * l + th + 1)
                    elif first and i > 0:
                        pe.wait_ge(pj_free[th], pj_read(l, i - 1))
                    for k in range(4):
                        m = three(PJ[th][:, :], at_hi[:, k0 + k, th * P:(th + 1) * P], at_lo[:, k0 + k, th * P:(th + 1) * P],
                                  hi[:, s, k * 512:(k + 1) * 512], lo[:, s, k * 512:(k + 1) * 512],
                                  first and k == 0, last and k == 3)
                    if last and th == 0:
                        m.then_inc(pj0_full, 1)
                m.then_inc(tile_used, 1)

            def heads_of(region, th):
                return [region[:, th, h * P:(h + 1) * P] for h in range(HEADS)]

            def s5_in(l, q):
                if 16 * l + q >= 2:
                    pe.wait_ge(pv_free, 16 * l + q - 1)
                b, r0 = q // 2, (q % 2) * 64
                v = PV[q % 2][:, :].rearrange("p (r d c) -> p r d c", r=2, d=2)
                for d in range(2):
                    for r in range(2):
                        rhs = ut2[r0:r0 + 64, b, :] if d == 0 else ut2[r0:r0 + 64, b, ::-1]
                        m = mm(v[:, r, d, :], bbt[r0:r0 + 64, d, r, b, :], rhs, True, True)
                m.then_inc(pv_full, 1)

            def s5_out(l, q):
                pe.wait_ge(states_ready, 16 * l + q + 1)
                xs = xst[q % 2]
                b, k, c0 = q // 2, q // 4, (q % 4) * 32
                for th in range(TH):
                    o = PY[th][c0:c0 + 32, k * P:(k + 1) * P]
                    kinds = ((0, 1), (1, 0)) if th == 0 else ((0, 0), (1, 1))
                    n = 0
                    for d, entering in kinds:
                        for r in range(2):
                            states = xs[:, r, d, 0:P] if entering != d else xs[:, r, d, 1:P + 1]
                            mm(o, cblk[:, entering, r, d, q, :, :].rearrange("p g h -> p (g h)"), states, n == 0, False)
                            n += 1
                    if th == 0 and 16 * l + q > 0:
                        pe.wait_ge(y_done, 16 * l + q)
                    r0 = (q % 2) * 64 + th * 32
                    m = mm(o, cbm[r0:r0 + 32, b, :], ut2[r0:r0 + 32, b, :], False, True)
                m.then_inc(y_done, 1)

            def scores(l, j, c):
                h, th = j // 2, j % 2
                bank = TR[TURN[(l, "sc", j)] % 2]
                if c == 0:
                    open_turn((l, "sc", j))
                else:
                    pe.wait_ge(half_scores, 8 * l + j + 1)
                mm(bank[:, c * SEQ:(c + 1) * SEQ], q_t[c * HD:(c + 1) * HD, h, th * P:(th + 1) * P],
                   k_t[c * HD:(c + 1) * HD, h, :], True, True).then_inc(tr_full if c else half_scores, 1)

            def weights_t(l, j):
                pe.wait_ge(w_ready, 8 * l + j + 1)
                bank = open_turn((l, "o", j))
                for i in range(2):
                    m = pe.transpose(bank[:, i * P:(i + 1) * P], wdiff[:, i * P:(i + 1) * P], ident)
                m.then_inc(wt_tr, 1)

            def head_out(l, j):
                bank, h = TR[TURN[(l, "o", j)] % 2], j // 2
                pe.wait_ge(wt_ready, 8 * l + j + 1)
                for i in range(2):
                    m = mm(bank[:, 2 * P:3 * P], wdiff_t[:, i, :], vreg[:, i, h * P:(h + 1) * P], i == 0, i == 1)
                m.then_inc(tr_full, 1)

            def mixer(l):
                t = T_MIX[l]
                for g in range(4):
                    pe.wait_ge(xn_ready, 4 * l + g // 2 + 1)
                    transposes((l, "x", g), [xn[:, g // 2, (4 * (g % 2) + i) * P:(4 * (g % 2) + i + 1) * P] for i in range(4)])
                pe.wait_ge(bc_in, BC_LOADS * (l + 1))
                for g in range(4):
                    transposes((l, "ct", g), [craw[g // 2][:, 4 * (g % 2) + i, :, :].rearrange("p a s -> p (a s)") for i in range(4)])
                pe.wait_ge(at_lo_ready, at_count(l, "x", 3))
                proj(t, l, 0, 0, True, False)
                proj(t + 1, l, 0, 4, False, True)
                proj(t + 2, l, 1, 0, True, False)
                proj(t + 3, l, 1, 4, False, True)
                pe.wait_ge(pj_free[1], pj_read(l, 0))
                for g in range(2):
                    transposes((l, "u", g), [u_flat[:, (4 * g + i) * P:(4 * g + i + 1) * P] for i in range(4)])
                proj(t + 4, l, 2, 0, True, False)
                proj(t + 5, l, 2, 4, False, True)
                pe.wait_ge(rot_ready, 4 * l + 2)
                for th in range(TH):
                    transposes((l, "q", th), heads_of(qk[:, 0, :, :], th))
                proj(t + 6, l, 3, 0, True, False)
                proj(t + 7, l, 3, 4, False, True)
                pe.wait_ge(rot_ready, 4 * l + 4)
                for th in range(TH):
                    transposes((l, "k", th), heads_of(qk[:, 1, :, :], th))
                pe.wait_ge(b_laid, l + 1)
                bp = gflat.rearrange("p (i c) -> p i c", c=P)
                for g in range(8):
                    transposes((l, "b", g), [bp[:, 4 * g + i, :] for i in range(4)])
                pe.wait_ge(blocks_ready, l + 1)
                bank = open_turn((l, "cb", 0))
                for q in range(PAIRS):
                    b, q2 = q // 2, q % 2
                    for d in range(2):
                        r0 = q2 * 64 + d * 32
                        for r in range(2):
                            m = mm(bank[r0:r0 + 32, b * 32:(b + 1) * 32],
                                   bpre[:, d, r, b, q2, 1 - d, :, :].rearrange("p g h -> p (g h)"),
                                   cblk[:, 0, r, d, q, :, :].rearrange("p g h -> p (g h)"), r == 0, r == 1)
                m.then_inc(tr_full, 1)
                wait_read(pe, (l, "b", 6))
                wait_read(pe, (l, "b", 7))
                wait_read(pe, (l, "u", 0))
                wait_read(pe, (l, "u", 1))
                wait_read(pe, (l, "k", 0))
                wait_read(pe, (l, "k", 1))
                wait_read(pe, (l, "q", 1))
                for s in range(8):
                    if s > 0:
                        weights_t(l, s - 1)
                    s5_in(l, 2 * s)
                    scores(l, s, 0)
                    s5_in(l, 2 * s + 1)
                    scores(l, s, 1)
                    proj(t + 8 + s, l, 4 + s // 2, 4 * (s % 2), s % 2 == 0, s % 2 == 1)
                    if s == 0:
                        wait_read(pe, (l, "cb", 0))
                        pe.wait_ge(pj_free[1], pj_read(l, 3))
                    if s > 0:
                        head_out(l, s - 1)
                        s5_out(l, 2 * s - 2)
                        s5_out(l, 2 * s - 1)
                weights_t(l, 7)
                s5_out(l, 14)
                head_out(l, 7)
                s5_out(l, 15)
                pe.wait_ge(a_ready, 2 * l + 2)
                for th in range(TH):
                    transposes((l, "a", th), heads_of(areg, th))
                pe.wait_ge(at_lo_ready, at_count(l, "a", 1))
                proj(t + 16, l, 8, 0, True, True)
                proj(t + 17, l, 9, 0, True, True)
                pe.wait_ge(s_ready, 2 * l + 2)
                for th in range(TH):
                    transposes((l, "s", th), [s_t[:, k, th * P:(th + 1) * P] for k in range(4)])
                pe.wait_ge(at_lo_ready, at_count(l, "sa", 1))
                proj(t + 18, l, 10, 4, True, True)
                for th in range(TH):
                    wait_read(pe, (l, "s", th))
                for th in range(TH):
                    transposes((l, "s2", th), heads_of(s_gated, th))
                pe.wait_ge(at_lo_ready, at_count(l, "s2", 1))
                proj(t + 19, l, 11, 4, True, True)
                proj(t + 20, l, 12, 4, True, True)
                pe.wait_ge(m_ready, 4 * l + 4)
                for g in range(4):
                    transposes((l, "m", g), [gates[:, g // 2, 0, (4 * (g % 2) + i) * P:(4 * (g % 2) + i + 1) * P] for i in range(4)])
                pe.wait_ge(at_lo_ready, at_count(l, "m", 3))
                for n in range(2):
                    proj(t + 21 + 2 * n, l, 13 + n, 0, True, False)
                    proj(t + 22 + 2 * n, l, 13 + n, 4, False, True)
                for g in range(4):
                    pe.wait_ge(xn_ready, 4 * l + 2 + g // 2 + 1)
                    transposes((l, "h", g), [xn[:, g // 2, (4 * (g % 2) + i) * P:(4 * (g % 2) + i + 1) * P] for i in range(4)])
                pe.wait_ge(at_lo_ready, at_count(l, "h", 3))

            pe.wait_ge(loads, 32)
            pe.wait_ge(dve_par, 1)
            transposes("par", [row(PACK + i) for i in range(7)])
            mixer(0)

            def up2(c, a_tile, a_slot, b_tile, b_slot):
                pe.wait_ge(lo_ready, a_tile + 1)
                if c is not None:
                    pe.wait_ge(h_done, c)
                for th in range(TH):
                    for k in range(4):
                        m = three(PJ[th][:, :], at_hi[:, k, th * P:(th + 1) * P], at_lo[:, k, th * P:(th + 1) * P],
                                  hi[:, a_slot, k * 512:(k + 1) * 512], lo[:, a_slot, k * 512:(k + 1) * 512], k == 0, False)
                m.then_inc(tile_used, 1)
                if c is not None:
                    hidden_t2(c)
                pe.wait_ge(lo_ready, b_tile + 1)
                for th in range(TH):
                    for k in range(4):
                        m = three(PJ[th][:, :], at_hi[:, 4 + k, th * P:(th + 1) * P], at_lo[:, 4 + k, th * P:(th + 1) * P],
                                  hi[:, b_slot, k * 512:(k + 1) * 512], lo[:, b_slot, k * 512:(k + 1) * 512], False, k == 3)
                    if th == 0:
                        m.then_inc(h_full, 1)
                m.then_inc(tile_used, 1)

            def hidden_t2(done):
                pe.wait_ge(h_done, done)
                for th in range(TH):
                    for f in range(2):
                        m = pe.transpose(TR[0][:, f * SEQ + th * P:f * SEQ + (th + 1) * P],
                                         v_flat[:, (2 + th) * FC + f * P:(2 + th) * FC + (f + 1) * P], ident)
                m.then_inc(ht_tr, 1)

            def down2(tile, slot, parts, start, stop):
                pe.wait_ge(lo_ready, tile + 1)
                pe.wait_ge(ht_lo_ready, parts)
                for th in range(TH):
                    for f in range(2):
                        for n in range(2):
                            m = three(banks[2 + 2 * th + n][:, :], ht_hi[:, f, th * P:(th + 1) * P], ht_lo[:, f, th * P:(th + 1) * P],
                                      hi[:, slot, f * D + n * 512:f * D + (n + 1) * 512],
                                      lo[:, slot, f * D + n * 512:f * D + (n + 1) * 512], start and f == 0, stop and f == 1)
                m.then_inc(tile_used, 1)

            t = T_FFN0
            up2(None, t, t % 3, t + 1, (t + 1) % 3)
            up2(2, t + 2, (t + 2) % 3, t + 3, t % 3)
            down2(t + 4, (t + 4) % 3, 1, True, False)
            with pe.Fori(1, NCH - 1) as c:
                up2(c * 2 + 2, c * 3 + (t + 2), (t + 2) % 3, c * 3 + (t + 3), t % 3)
                down2(c * 3 + (t + 4), (t + 4) % 3, c + 1, False, False)
            hidden_t2(2 * NCH)
            down2(T_MIX1 - 1, (T_MIX1 - 1) % 3, NCH, False, True)
            mixer(1)

            pe.wait_ge(router_ready, 1)
            bank = open_turn("router")
            for th in range(TH):
                for k in range(KD):
                    for i, a in enumerate((at_hi, at_lo)):
                        m = mm(bank[:, th * 16:(th + 1) * 16], a[:, k, th * P:(th + 1) * P], router_parts[:, k, :],
                               k == 0 and i == 0, k == KD - 1 and i == 1)
            m.then_inc(tr_full, 1)
            pe.wait_ge(sel_ready, 1)
            bank = open_turn("pos")
            tri, ones = cst[:, C_TRI:C_TRI + P], cst[:, C_ONE:C_ONE + P]
            mm(bank[:, 0:8], tri, sel[:, 0, :], True, True)
            mm(bank[:, 8:16], tri, sel[:, 1, :], True, False)
            mm(bank[:, 8:16], ones, sel[:, 0, :], False, True)
            mm(bank[:, 16:24], ones, sel[:, 0, :], True, False)
            mm(bank[:, 16:24], ones, sel[:, 1, :], False, True).then_inc(tr_full, 1)

            def gather():
                for k in range(KD):
                    for th in range(TH):
                        m = mm(banks[4 + k // 4][:, (k % 4) * P:(k % 4 + 1) * P], xn[:, th, k * P:(k + 1) * P],
                               place[:, th, :], th == 0, th == 1)
                m.then_inc(xe_full, 1)

            def up(b, c, half):
                j = 3 * c - 1 + half if c > 0 else half
                s = (T_MOE + j) % SPLITS
                pe.wait_ge(lo_ready, b * FFN_TILES + (T_MOE + j + 1))
                if half == 0 and c == NCH - 1:
                    pe.wait_ge(gt_ready, b + 1)
                if half == 0 and c == NCH:
                    pe.wait_ge(xe_lo_ready, b + 2)
                for k in range(4):
                    m = three(h_bank(c)[:, :], at_hi[:, 4 * half + k, 0:P], at_lo[:, 4 * half + k, 0:P],
                              hi[:, s, k * 512:(k + 1) * 512], lo[:, s, k * 512:(k + 1) * 512],
                              half == 0 and k == 0, half == 1 and k == 3)
                m.then_inc(tile_used, 1)

            def hidden_t(b, c):
                pe.wait_ge(h_done, b * NCH + (2 * NCH + c + 1))
                if c == 1:
                    pe.wait_ge(x_added, b * 4 + 12)
                for f in range(2):
                    m = pe.transpose(TR[0][:, f * P:(f + 1) * P], v_flat[:, FC + f * P:FC + (f + 1) * P], ident)
                m.then_inc(ht_tr, 1)

            def down(b, c, j):
                s = (T_MOE + j) % SPLITS
                pe.wait_ge(lo_ready, b * FFN_TILES + (T_MOE + j + 1))
                pe.wait_ge(ht_lo_ready, b * NCH + (NCH + c + 1))
                if c == NCH:
                    pe.wait_ge(ye_ready, b + 1)
                for f in range(2):
                    for n in range(2):
                        m = three(banks[2 + n][:, :], ht_hi[:, f, 0:P], ht_lo[:, f, 0:P],
                                  hi[:, s, f * D + n * 512:f * D + (n + 1) * 512],
                                  lo[:, s, f * D + n * 512:f * D + (n + 1) * 512],
                                  c % NCH == 0 and f == 0, c == NCH - 1 and f == 1)
                m.then_inc(tile_used, 1)

            def combine(b):
                pe.wait_ge(gt_ready, b + 1)
                pe.wait_ge(ye_ready, b + 1)
                for i, bank in enumerate(comb_banks):
                    th, n = i // 2, i % 2
                    mm(bank[:, :], ht_hi[:, th, P:2 * P], at_hi[:, 4 * n:4 * n + 4, P:2 * P], True, False)
                    mm(bank[:, :], ht_hi[:, th, P:2 * P], at_lo[:, 4 * n:4 * n + 4, P:2 * P], False, True).then_inc(comb_full, 1)

            def expert_step(b, c, final=False):
                ahead = not (final and c == NCH - 1)
                if ahead:
                    up(b, c + 1, 0)
                hidden_t(b, c)
                if ahead:
                    up(b, c + 1, 1)
                down(b, c, FFN_TILES - 1 if final and c == NCH - 1 else 3 * c + 4)
                if c == 3:
                    for th in range(TH):
                        pe.transpose(TR[1][:, th * P:(th + 1) * P], place[:, th, :], ident)
                    for th in range(TH):
                        m = mm(TR[1][:, TH * P:TH * P + 1], place[:, th, :], column[:, 1, th:th + 1], th == 0, th == 1)
                    m.then_inc(pg_full, 1)
                if c == 8 and not final:
                    pe.wait_ge(place_ready, b + 2)
                    gather()
                if c == NCH:
                    combine(b)

            pe.wait_ge(place_ready, 1)
            gather()
            pe.wait_ge(xe_lo_ready, 1)
            for half in range(2):
                up(0, 0, half)
            expert_step(0, 0)
            last = pe.value_load(table[0:1, 0:1], min_val=NE - 1, max_val=MAXB - 1)
            with pe.Fori(0, last) as b:
                for c in range(1, NCH + 1):
                    expert_step(b, c)
            for c in range(1, NCH):
                expert_step(last, c, True)
            combine(last)

        @block.scalar
        def _(act):
            own = Order(act, act_own)

            def split(t, full_sem, full, src, slot, after=True):
                act.wait_ge(full_sem, full)
                if after:
                    act.wait_ge(tile_used, t - (SPLITS - 1))
                act.activation(hi[:, slot, :], src, ACT.Copy).then_inc(hi_ready, 1)

            def split_moe(b, j):
                slot = moe_slot(j)
                split(b * FFN_TILES + (T_MOE + j), raw_full[slot], moe_full_value(j, b), raw[:, slot, :], (T_MOE + j) % SPLITS)

            def split_static(t):
                s = raw_slot(t)
                split(t, raw_full[s], 32 * (raw_uses(s, t) + 1), raw[:, s, :], t % SPLITS, t >= SPLITS)

            def at_part(l, kind, g, k0, kn, c0, scale=1.0):
                bank = wait_turn(act, (l, kind, g))
                act.activation(at_hi[:, k0:k0 + kn, c0:c0 + P], bank[:, 0:kn * P].rearrange("p (k c) -> p k c", k=kn),
                               ACT.Copy, scale=scale).then_inc(at_hi_ready, 1)

            def squares(stage, quarters):
                for th, n, added in quarters:
                    if added is not None:
                        act.wait_ge(x_added, added)
                    half = slice(n * 512, (n + 1) * 512)
                    m = act.activation(xn[:, th, half], xres[:, th, half], ACT.Square, accum_out=col((SS, SS2)[n] + th))
                m.then_inc(sq_ready, 1)
                act.wait_ge(var_ready, stage + 1)
                act.activation(col(RT, 2), col(VAR, 2), ACT.Sqrt).then_inc(root_ready, 1)

            def load_gain(src):
                act.dma_start(a_flat, src.partition_broadcast(P)).then_inc(gain_in, 16)

            def evac(name, dst, bank_cols=512):
                bank = wait_turn(act, name)
                act.activation(dst, bank[:, 0:bank_cols], ACT.Copy).then_inc(tr_free[TURN[name] % 2], 1)

            def from_pj(l, i, tile, dst, func, scale=1.0, view=None, sig=None):
                for th in range(TH):
                    if th == 0:
                        act.wait_ge(pj0_full, use(l, i) + 1)
                    else:
                        act.wait_ge(tile_used, tile + 1)
                    src = PJ[th][:, :] if view is None else view(PJ[th][:, :])
                    act.activation(dst(th), src, func, scale=scale).then_inc(pj_free[th], 1)

            def probs_of(l, j):
                act.wait_ge(max_ready, 8 * l + j + 1)
                for c in range(2):
                    m = act.activation(probs[:, c, :], TR[TURN[(l, "sc", j)] % 2][:, c * SEQ:(c + 1) * SEQ], ACT.Exp, bias=col(NB + c),
                                       scale=HD ** -0.5, accum_out=col(RS + c))
                m.then_inc(exp_ready, 1)

            def head_back(l, j):
                name = (l, "o", j)
                bank = TR[TURN[name] % 2]
                act.wait_ge(wt_tr, 8 * l + j + 1)
                act.activation(wdiff_t, bank[:, 0:2 * P].rearrange("p (t q) -> p t q", t=2), ACT.Copy).then_inc(wt_ready, 1)
                wait_turn(act, name)
                h, th = j // 2, j % 2
                own.step(act.activation(areg[:, th, h * P:(h + 1) * P], bank[:, 2 * P:3 * P], ACT.Copy))
                act.activation(bank[:, 2 * P:3 * P], bank[:, 2 * P:3 * P], ACT.Square,
                               accum_out=col(AS + j)).then_inc(tr_free[TURN[name] % 2], 1)

            def lay_b(l):
                if l == 0:
                    act.wait_ge(bzero_ready, 2)
                act.wait_ge(mats_ready, 2 * l + 1)
                for d in range(2):
                    for kind, src in enumerate((bbar, babar)):
                        t = (1 - d) if kind == 0 else d
                        for g in range(2):
                            for r in range(2):
                                rows = slice(64 * g, 64 * (g + 1))
                                m = act.activation(bpre[rows, d, r, :, :, t, g, :].rearrange("p b q h -> p (b q) h"),
                                                   src[rows, r, d * PAIRS:(d + 1) * PAIRS, :], ACT.Copy)
                m.then_inc(b_laid, 1)

            def lay_c(l):
                act.wait_ge(mats_ready, 2 * l + 2)
                for kind, src in enumerate((ctr, cabar)):
                    for r in range(2):
                        for g in range(2):
                            rows = slice(64 * g, 64 * (g + 1))
                            m = act.activation(cblk[rows, kind, r, :, :, g, :].rearrange("p d q h -> p (d q) h"),
                                               src[rows, r, :, :], ACT.Copy, scale=1.0 if r == 0 else -1.0)
                m.then_inc(blocks_ready, 1)

            def mixer(l):
                t = T_MIX[l]
                if l > 0:
                    act.wait_ge(tile_used, t - 1)
                for g in range(4):
                    at_part(l, "x", g, 4 * (g % 2), 4, (g // 2) * P)
                for g in range(4):
                    bank = wait_turn(act, (l, "ct", g))
                    r, d = g // 2, g % 2
                    for odd in range(2):
                        rows = slice(64 * odd, 64 * (odd + 1))
                        m = act.activation(ctr[rows, r, d * PAIRS:(d + 1) * PAIRS, :],
                                           bank[rows, :].rearrange("p (j g h) -> p j g h", g=2, h=GC)[:, :, odd, :], ACT.Copy)
                    m.then_inc(tr_free[TURN[(l, "ct", g)] % 2], 1)
                for s in range(3):
                    split_static(t + s + 2)
                    if s == 1:
                        from_pj(l, 0, t + 1, lambda th: u_rows[:, :, th, :], ACT.Copy,
                                view=lambda b: b.rearrange("p (q c) -> p q c", q=PAIRS))
                split_static(t + 5)
                for g in range(2):
                    evac((l, "u", g), ut2[:, 4 * g:4 * g + 4, :].rearrange("p b c -> p (b c)"))
                split_static(t + 6)
                if l == 0:
                    lay_b(0)
                split_static(t + 7)
                for th in range(TH):
                    evac_heads(l, "q", th, q_t)
                split_static(t + 8)
                lay_c(l)
                split_static(t + 9)
                from_pj(l, 3, t + 7, lambda th: vreg[:, th, :], ACT.Copy)
                for th in range(TH):
                    evac_heads(l, "k", th, k_t)
                bflat = area(0, 4096)
                for g in range(0, 8, 2):
                    evac((l, "b", g), bflat[:, g * 512:(g + 1) * 512])
                for s in range(8):
                    split_static(t + 10 + s)
                    probs_of(l, s)
                    if s % 2 == 1:
                        i = 4 + s // 2
                        g, n = (i - 4) // 2, (i - 4) % 2
                        from_pj(l, i, t + 8 + s, lambda th: gates[:, th, g, n * 512:(n + 1) * 512], ACT.Tanh, scale=0.5)
                    if s > 0:
                        head_back(l, s - 1)
                head_back(l, 7)
                act.wait_ge(avar_ready, l + 1)
                act.activation(col(AR, 8), col(AV, 8), ACT.Sqrt).then_inc(aroot_ready, 1)
                for th in range(TH):
                    at_part(l, "a", th, 0, 4, th * P)
                load_gain(norm_ffn[l, :])
                split_static(t + 18)
                act.wait_ge(y_done, PAIRS * (l + 1))
                for th in range(TH):
                    act.activation(s_t[:, :, th * P:(th + 1) * P], PY[th][:, :].rearrange("p (k s) -> p k s", k=4),
                                   ACT.Gelu).then_inc(s_ready, 1)
                for th in range(TH):
                    act.wait_ge(s_ready, 2 * l + th + 1)
                    act.activation(at_hi[:, 4:8, th * P:(th + 1) * P], s_t[:, :, th * P:(th + 1) * P],
                                   ACT.Copy).then_inc(at_hi_ready, 1)
                split_static(t + 19)
                split_static(t + 20)
                from_pj(l, 10, t + 18, lambda th: s_gated[:, th, :], ACT.Tanh, scale=0.5)
                act.wait_ge(tile_used, t + 19)
                for th in range(TH):
                    at_part(l, "s2", th, 4, 4, th * P, scale=0.5)
                split_static(t + 21)
                split_static(t + 22)
                act.wait_ge(tile_used, t + 21)
                for g in range(4):
                    at_part(l, "m", g, 4 * (g % 2), 4, (g // 2) * P, scale=0.5)
                split_static(t + 23)
                split_static(t + 24)
                if l == 1:
                    act.wait_ge(at_lo_ready, at_count(l, "m", 3))
                    act.dma_start(router, moe_router[0, :, :].rearrange("(k p) e -> p k e", p=P)).then_inc(router_in, 16)
                for i in range(2):
                    if l == 0:
                        split_static(t + 25 + i)
                    else:
                        split_moe(0, i)
                if l == 1:
                    act.wait_ge(router_in, 16)
                    act.activation(router_parts[:, :, 0:NE], router, ACT.Copy).then_inc(router_hi_ready, 1)
                squares(2 * l + 1, [(th, n, 8 * l + 2 * n + th + 1) for n in range(2) for th in range(TH)])
                for g in range(4):
                    at_part(l, "h", g, 4 * (g % 2), 4, (g // 2) * P)
                load_gain(norm_mix[1, :] if l == 0 else norm_final)

            def evac_heads(l, kind, th, dst):
                bank = wait_turn(act, (l, kind, th))
                act.activation(dst[:, :, th * P:(th + 1) * P], bank[:, :].rearrange("p (h s) -> p h s", h=HEADS),
                               ACT.Copy).then_inc(tr_free[TURN[(l, kind, th)] % 2], 1)

            act.dma_start(row(R_LR), ssm_lam_re.rearrange("l d (q g) s -> (l d q) (g s)", g=2)).then_inc(rows_in, 16)
            act.dma_start(row(R_LI), ssm_lam_im.rearrange("l d (q g) s -> (l d q) (g s)", g=2)).then_inc(rows_in, 16)
            act.dma_start(row(R_DT)[:, 0:2], ssm_log_dt.rearrange("l d (q g) -> (l d q) g", g=2)).then_inc(rows_in, 16)
            act.dma_start(gflat[:, 4 * P:8 * P], attn_lambda.rearrange("l a c -> (l a c)").partition_broadcast(P)).then_inc(lam_in, 16)
            act.dma_start(subln[:, :, :].rearrange("p l c -> p (l c)"),
                          attn_subln.rearrange("l c -> (l c)").partition_broadcast(P)).then_inc(lam_in, 16)
            load_gain(norm_mix[0, :])
            act.wait_ge(rows_in, 48)
            act.activation(row(R_EDT)[:, 0:2], row(R_DT)[:, 0:2], ACT.Exp).then_inc(act_par, 1)
            act.wait_ge(dve_rows, 1)
            act.activation(row(R_er), row(R_lr), ACT.Exp)
            act.wait_ge(lam_ready, 1)
            act.activation(col(LEXP, 4), col(LSUM, 4), ACT.Exp).then_inc(lam_exp, 1)
            act.activation(row(R_sn), row(R_red), ACT.Sin)
            act.activation(row(R_sh), row(R_red), ACT.Sin, scale=0.5).then_inc(act_par, 1)
            act.wait_ge(loads, 32)
            squares(0, [(th, n, None) for th in range(TH) for n in range(2)])
            split_static(0)
            split_static(1)
            mixer(0)

            def silu2(full0, used1):
                for th in range(TH):
                    act.wait_ge(h_full if th == 0 else tile_used, full0 if th == 0 else used1)
                    act.activation(v_flat[:, th * FC:(th + 1) * FC], PJ[th][:, 0:FC], ACT.Silu).then_inc(g_ready, 1)

            def hidden_hi(n, cols):
                act.wait_ge(ht_tr, n)
                act.activation(ht_hi[:, :, 0:cols], TR[0][:, 0:2 * cols].rearrange("p (f s) -> p f s", f=2),
                               ACT.Copy).then_inc(ht_hi_ready, 1)

            t = T_FFN0

            def ffn_turn(c, used):
                def split_turn(i):
                    s = raw_slot(t + 2 + i)
                    split(c * 3 + (t + 2 + i), raw_full[s], c * 32 + 32 * (raw_uses(s, t + 2 + i) + 1), raw[:, s, :], (t + 2 + i) % 3)
                split_turn(0)
                silu2(c + 1, used)
                split_turn(1)
                split_turn(2)
                hidden_hi(c + 1, SEQ)
            ffn_turn(0, t + 2)
            with act.Fori(1, NCH - 1) as c:
                ffn_turn(c, c * 3 + (t + 1))
            silu2(NCH, t + 3 * (NCH - 1) + 1)
            lay_b(1)
            split_static(T_MIX1 - 1)
            hidden_hi(NCH, SEQ)
            split_static(T_MIX1)
            split_static(T_MIX1 + 1)
            squares(2, [(th, n, 5 + 2 * th + n) for th in range(TH) for n in range(2)])
            mixer(1)

            act.wait_ge(sel_early, 1)
            act.activation(r_exp, r_diff, ACT.Exp).then_inc(gate_exp, 1)

            def gathered(n):
                act.wait_ge(xe_full, n)
                for g in range(2):
                    m = act.activation(at_hi[:, 4 * g:4 * g + 4, 0:P], banks[4 + g][:, :].rearrange("p (k c) -> p k c", k=4), ACT.Copy)
                m.then_inc(xe_hi_ready, 1)

            def silu(b, c):
                act.wait_ge(tile_used, b * FFN_TILES + (T_MOE + (3 * c if c > 0 else 1) + 1))
                act.activation(v_flat[:, 0:FC], h_bank(c)[:, 0:FC], ACT.Silu).then_inc(g_ready, 1)

            def result_hi(b, used):
                act.wait_ge(tile_used, used)
                for n in range(2):
                    m = act.activation(at_hi[:, 4 * n:4 * n + 4, P:2 * P], PY[n][:, :].rearrange("p (k c) -> p k c", k=4),
                                       ACT.Copy, scale=place_gate)
                m.then_inc(ye_hi_ready, 1)

            def expert_step(b, c, final=False):
                if c == NCH:
                    result_hi(b, b * FFN_TILES + (T_MOE + FFN_TILES + 2))
                if c == 4:
                    act.wait_ge(pg_full, b + 1)
                    act.activation(ht_hi[:, :, P:2 * P], TR[1][:, 0:SEQ].rearrange("p (t c) -> p t c", t=TH), ACT.Copy)
                    act.activation(place_gate, TR[1][:, SEQ:SEQ + 1], ACT.Copy).then_inc(gt_ready, 1)
                if c >= 0:
                    split_moe(b, FFN_TILES - 1 if final and c == NCH - 1 else 3 * c + 4)
                    hidden_hi(b * NCH + (NCH + c + 1), P)
                if not (final and c + 2 >= NCH):
                    split_moe(b, 3 * c + 5)
                if not (final and c + 1 >= NCH):
                    silu(b, c + 1)
                if c == NCH - 2 and not final:
                    gathered(b + 2)
                if not (final and c + 2 >= NCH):
                    split_moe(b, 3 * c + 6)

            gathered(1)
            expert_step(0, -1)
            expert_step(0, 0)
            act.wait_ge(routed, 1)
            last = act.value_load(table[0:1, 0:1], min_val=NE - 1, max_val=MAXB - 1)
            with act.Fori(0, last) as b:
                for c in range(1, NCH + 1):
                    expert_step(b, c)
            for c in range(1, NCH):
                expert_step(last, c, True)
            result_hi(last, last * FFN_TILES + (T_MOE + FFN_TILES))
            squares(4, [(th, n, last * 4 + (13 + 2 * th + n)) for th in range(TH) for n in range(2)])

        @block.vector
        def _(dve):
            own = Order(dve, dve_own)
            tt, ts, stt = dve.tensor_tensor, dve.tensor_scalar, dve.scalar_tensor_tensor

            def split(t, slot, src):
                dve.wait_ge(hi_ready, t + 1)
                tt(lo[:, slot, :], src, hi[:, slot, :].bitcast(f32), SUB).then_inc(lo_ready, 1)

            def split_moe(b, j):
                split(b * FFN_TILES + (T_MOE + j), (T_MOE + j) % SPLITS, raw[:, moe_slot(j), :])

            def split_static(t):
                split(t, t % SPLITS, raw[:, raw_slot(t), :])

            def at_part(l, kind, g, k0, kn, c0, scale=None):
                bank = TR[TURN[(l, kind, g)] % 2]
                dve.wait_ge(at_hi_ready, at_count(l, kind, g))
                src = bank[:, 0:kn * P].rearrange("p (k c) -> p k c", k=kn)
                dst, first = at_lo[:, k0:k0 + kn, c0:c0 + P], at_hi[:, k0:k0 + kn, c0:c0 + P].bitcast(f32)
                if scale is None:
                    tt(dst, src, first, SUB).then_inc(at_lo_ready, 1)
                else:
                    stt(dst, src, scale, first, MUL, SUB).then_inc(at_lo_ready, 1)

            def norm(stage, done):
                dve.wait_ge(sq_ready, stage + 1)
                tt(col(SS, 2), col(SS, 2), col(SS2, 2), ADD).then_inc(sum_ready, 1)
                dve.wait_ge(sum_ready, stage + 1)
                ts(col(VAR, 2), col(SS, 2), 1.0 / D, EPS, MUL, ADD).then_inc(var_ready, 1)
                dve.wait_ge(root_ready, stage + 1)
                dve.reciprocal(col(RI, 2), col(RT, 2)).then_inc(inv_ready, 1)
                dve.wait_ge(inv_ready, stage + 1)
                dve.wait_ge(gain_in, 16 * (stage + 1))
                for th in range(TH):
                    stt(xn[:, th, :], xres[:, th, :], col(RI + th), gain, MUL, MUL).then_inc(done, 1)

            def rotary(l, i, tile, dst):
                cos_t, sin_t = (cst[:, c:c + 128].rearrange("p (t c) -> p t c", t=2) for c in (C_COS, C_SIN))
                for th in range(TH):
                    if th == 0:
                        dve.wait_ge(pj0_full, use(l, i) + 1)
                    else:
                        dve.wait_ge(tile_used, tile + 1)
                    src = PJ[th][:, :]
                    own.step(tt(a_flat[:, 0:512].rearrange("p (h c) -> p h c", c=HD), src.rearrange("p (h c) -> p h c", c=HD),
                                cos_t[:, th, :].unsqueeze(1).broadcast_to([P, 8, HD]), MUL))
                    tt(a_flat[:, 512:1024].rearrange("p (h a c) -> p h a c", a=2, c=32),
                       src.rearrange("p (h a c) -> p h a c", a=2, c=32)[:, :, ::-1, :],
                       sin_t[:, th, :].rearrange("p (a c) -> p a c", a=2).unsqueeze(1).broadcast_to([P, 8, 2, 32]),
                       MUL).then_inc(pj_free[th], 1)
                    dve.wait_ge(pj_free[th], pj_read(l, i))
                    tt(dst[:, th, :], a_flat[:, 0:512], a_flat[:, 512:1024], ADD).then_inc(rot_ready, 1)
                    dve.wait_ge(rot_ready, 4 * l + (0 if i == 1 else 2) + th + 1)

            def phases(l, q):
                n = 16 * l + q
                if n >= 2:
                    dve.wait_ge(zs_used, n - 1)
                w = wtab[q % 2]
                dve.wait_ge(php_ready, n + 1)
                own.step(phase_product(tt, w[:, 0, :], l, q, 0, 0))
                tt(w[:, 0, :], w[:, 0, :], php[0], SUB)
                tt(w[:, 1, :], php[1], php[2], ADD).then_inc(wtab_ready, 1)

            def s5_scan(l, q):
                n = 16 * l + q
                v = PV[q % 2][:, :].rearrange("p (r c) -> p r c", r=2)
                w = wtab[q % 2]
                dve.wait_ge(pv_full, n + 1)
                dve.wait_ge(wtab_ready, n + 1)
                tt(rot1, v, w[:, 0:1, :].broadcast_to([P, 2, 256]), MUL)
                tt(rot2, v[:, ::-1, :], w[:, 1:2, :].broadcast_to([P, 2, 256]), MUL).then_inc(pv_free, 1)
                dve.wait_ge(pv_free, n + 1)
                tt(rot1[:, 0, :], rot1[:, 0, :], rot2[:, 0, :], ADD)
                own.step(tt(rot1[:, 1, :], rot1[:, 1, :], rot2[:, 1, :], SUB))
                if n > 0:
                    dve.wait_ge(zs_used, n)
                for r in range(2):
                    for d in range(2):
                        half = slice(d * P, (d + 1) * P)
                        j = 32 * l + d * PAIRS + q
                        m = dve.tensor_tensor_scan(zs[:, r, half], par[:, RAD2, j:j + 1].broadcast_to([P, P]),
                                                   rot1[:, r, half], 0.0, MUL, ADD)
                m.then_inc(zs_ready, 1)

            def row_max(l, j):
                bank = wait_turn(dve, (l, "sc", j))
                own.step(dve.tensor_reduce(col(MX, 2), bank[:, :].rearrange("p (c s) -> p c s", c=2), AX.X, ALU.max))
                ts(col(NB, 2), col(MX, 2), -(HD ** -0.5), None, MUL).then_inc(max_ready, 1)

            def softmax_difference(l, j):
                dve.wait_ge(exp_ready, 8 * l + j + 1)
                dve.reciprocal(col(RR, 2), col(RS, 2)).then_inc(tr_free[TURN[(l, "sc", j)] % 2], 1)
                wait_read(dve, (l, "sc", j))
                own.step(tt(col(C1), col(RR + 1), col(NLAM + l), MUL))
                own.step(ts(probs[:, 1, :], probs[:, 1, :], col(C1), None, MUL))
                if 8 * l + j > 0:
                    dve.wait_ge(wt_tr, 8 * l + j)
                stt(wdiff, probs[:, 0, :], col(RR), probs[:, 1, :], MUL, ADD).then_inc(w_ready, 1)

            def gated(l, i, tile, g, n):
                for th in range(TH):
                    if th == 0:
                        dve.wait_ge(pj0_full, use(l, i) + 1)
                    else:
                        dve.wait_ge(tile_used, tile + 1)
                    z = gates[:, th, g, n * 512:(n + 1) * 512]
                    stt(z, z, 1.0, PJ[th][:, :], ADD, MUL).then_inc(pj_free[th], 1)
                    if g == 1:
                        dve.wait_ge(pj_free[th], pj_read(l, i))
                        m = gates[:, th, 0, n * 512:(n + 1) * 512]
                        tt(m, m, z, ADD).then_inc(m_ready, 1)

            def add_out(l, i, tile, n):
                for th in range(TH):
                    if th == 0:
                        dve.wait_ge(pj0_full, use(l, i) + 1)
                    else:
                        dve.wait_ge(tile_used, tile + 1)
                    z = xres[:, th, n * 512:(n + 1) * 512]
                    tt(z, z, PJ[th][:, :], ADD).then_inc(x_added, 1)

            def mixer(l):
                t = T_MIX[l]
                for g in range(4):
                    at_part(l, "x", g, 4 * (g % 2), 4, (g // 2) * P)
                for s in range(4):
                    split_static(t + s + 2)
                    if l == 0 and s < 2:
                        if s == 0:
                            wait_read(dve, "par")
                        dve.memset(gflat[:, s * 2048:(s + 1) * 2048], 0.0).then_inc(bzero_ready, 1)
                rotary(l, 1, t + 3, qk[:, 0, :, :])
                split_static(t + 6)
                split_static(t + 7)
                rotary(l, 2, t + 5, qk[:, 1, :, :])
                split_static(t + 8)
                split_static(t + 9)
                bflat = area(0, 4096)
                for g in range(1, 8, 2):
                    bank = wait_turn(dve, (l, "b", g))
                    dve.tensor_copy(bflat[:, g * 512:(g + 1) * 512], bank[:, :]).then_inc(tr_free[TURN[(l, "b", g)] % 2], 1)
                dve.wait_ge(dskip_in, 16 * 8)
                own.step(tt(cbm, cst[:, C_PAT:C_PAT + 32].unsqueeze(1).broadcast_to([P, 8, 32]),
                            dskip[:, l, :].unsqueeze(2).broadcast_to([P, 8, 32]), MUL))
                bank = wait_turn(dve, (l, "cb", 0))
                tt(cbm, cbm, bank[:, 0:256].rearrange("p (b c) -> p b c", b=8), ADD).then_inc(tr_free[TURN[(l, "cb", 0)] % 2], 1)
                phases(l, 0)
                for s in range(8):
                    split_static(t + 10 + s)
                    row_max(l, s)
                    s5_scan(l, 2 * s)
                    phases(l, 2 * s + 1)
                    softmax_difference(l, s)
                    s5_scan(l, 2 * s + 1)
                    if s < 7:
                        phases(l, 2 * s + 2)
                wait_read(dve, (l, "o", 6))
                wait_read(dve, (l, "o", 7))
                ts(col(AV, 8), col(AS, 8), 1.0 / P, EPS, MUL, ADD).then_inc(avar_ready, 1)
                dve.wait_ge(aroot_ready, l + 1)
                own.step(dve.reciprocal(col(AI, 8), col(AR, 8)))
                inv = col(AI, 8).rearrange("p (h t) -> p t h", t=2)
                for th in range(TH):
                    z = areg[:, th, :].rearrange("p (h c) -> p h c", h=HEADS)
                    own.step(tt(z, z, inv[:, th, :].unsqueeze(2).broadcast_to([P, HEADS, P]), MUL))
                    tt(z, z, subln[:, l, :].unsqueeze(1).broadcast_to([P, HEADS, P]), MUL).then_inc(a_ready, 1)
                for th in range(TH):
                    at_part(l, "a", th, 0, 4, th * P)
                split_static(t + 18)
                gated(l, 8, t + 16, 0, 0)
                split_static(t + 19)
                gated(l, 9, t + 17, 0, 1)
                for th in range(TH):
                    half = slice(th * P, (th + 1) * P)
                    dve.wait_ge(at_hi_ready, at_count(l, "sa", th))
                    tt(at_lo[:, 4:8, half], s_t[:, :, half], at_hi[:, 4:8, half].bitcast(f32), SUB).then_inc(at_lo_ready, 1)
                split_static(t + 20)
                for th in range(TH):
                    dve.wait_ge(pj_free[th], pj_read(l, 10))
                    bank = wait_turn(dve, (l, "s", th))
                    stt(s_gated[:, th, :], s_gated[:, th, :], 1.0, bank[:, :], ADD,
                        MUL).then_inc(tr_free[TURN[(l, "s", th)] % 2], 1)
                for th in range(TH):
                    at_part(l, "s2", th, 4, 4, th * P, scale=0.5)
                split_static(t + 21)
                gated(l, 11, t + 19, 1, 0)
                split_static(t + 22)
                gated(l, 12, t + 20, 1, 1)
                for g in range(4):
                    at_part(l, "m", g, 4 * (g % 2), 4, (g // 2) * P, scale=0.5)
                split_static(t + 23)
                split_static(t + 24)
                add_out(l, 13, t + 22, 0)
                for i in range(2):
                    if l == 0:
                        split_static(t + 25 + i)
                    else:
                        split_moe(0, i)
                add_out(l, 14, t + 24, 1)
                if l == 1:
                    dve.wait_ge(router_hi_ready, 1)
                    tt(router_parts[:, :, NE:2 * NE], router, router_parts[:, :, 0:NE].bitcast(f32), SUB).then_inc(router_ready, 1)
                norm(2 * l + 1, xn_ready)
                for g in range(4):
                    at_part(l, "h", g, 4 * (g % 2), 4, (g // 2) * P)

            TWO_PI_A = 6.28125
            TWO_PI_B = round((2 * math.pi - TWO_PI_A) * 2 ** 20) / 2 ** 20
            TWO_PI_C = 2 * math.pi - TWO_PI_A - TWO_PI_B
            MAGIC = 1.5 * 2.0 ** 23
            dve.wait_ge(rows_in, 48)
            dve.wait_ge(act_par, 1)
            dt = row(R_EDT)[:, 0:2].unsqueeze(2).broadcast_to([64, 2, 64])

            def halves(ap):
                return ap.rearrange("p (g s) -> p g s", g=2)
            tt(halves(row(R_lr)), halves(row(R_LR)), dt, MUL).then_inc(dve_rows, 1)
            own.step(tt(halves(row(R_li)), halves(row(R_LI)), dt, MUL))
            own.step(ts(row(R_k), row(R_li), 1.0 / (2 * math.pi), MAGIC, MUL, ADD))
            own.step(ts(row(R_k), row(R_k), -MAGIC, None, ADD))
            own.step(stt(row(R_red), row(R_k), -TWO_PI_A, row(R_li), MUL, ADD))
            own.step(stt(row(R_red), row(R_k), -TWO_PI_B, row(R_red), MUL, ADD))
            own.step(stt(row(R_red), row(R_k), -TWO_PI_C, row(R_red), MUL, ADD))
            own.step(ts(row(R_red), row(R_red), 3.1415925, -3.1415925, ALU.min, ALU.max))
            dve.wait_ge(lam_in, 32)
            own.step(tt(lamp.rearrange("p (l a) c -> p l a c", l=2), lamv[:, :, :, 0, :], lamv[:, :, :, 1, :], MUL))
            dve.tensor_reduce(col(LSUM, 4), lamp, AX.X, ADD).then_inc(lam_ready, 1)
            dve.wait_ge(lam_exp, 1)
            le = col(LEXP, 4).rearrange("p (l a) -> p l a", l=2)
            own.step(tt(col(NLAM, 2), le[:, :, 1], le[:, :, 0], SUB))
            for l in range(2):
                lam_init = 0.8 - 0.6 * math.exp(-0.3 * l)
                own.step(ts(col(NLAM + l), col(NLAM + l), -lam_init, None, ADD))
                own.step(ts(subln[:, l, :], subln[:, l, :], 1.0 - lam_init, None, MUL))
            dve.wait_ge(act_par, 2)
            a_re, a_im, co_re, co_im, cos, sin, rad2 = (row(PACK + i) for i in range(7))
            own.step(tt(row(R_t), row(R_sh), row(R_sh), MUL))
            own.step(ts(cos, row(R_t), -2.0, 1.0, MUL, ADD))
            own.step(dve.tensor_copy(sin, row(R_sn)))
            own.step(tt(a_re, row(R_er), cos, MUL))
            own.step(tt(a_im, row(R_er), sin, MUL))
            own.step(tt(rad2, row(R_er), row(R_er), MUL))
            own.step(tt(row(R_t), row(R_LR), row(R_LR), MUL))
            own.step(tt(row(R_u), row(R_LI), row(R_LI), MUL))
            own.step(tt(row(R_t), row(R_t), row(R_u), ADD))
            own.step(dve.reciprocal(row(R_den), row(R_t)))
            own.step(ts(row(R_am), a_re, -1.0, None, ADD))
            own.step(tt(row(R_t), row(R_am), row(R_LR), MUL))
            own.step(tt(row(R_u), a_im, row(R_LI), MUL))
            own.step(tt(row(R_t), row(R_t), row(R_u), ADD))
            own.step(tt(co_re, row(R_t), row(R_den), MUL))
            own.step(tt(row(R_t), a_im, row(R_LR), MUL))
            own.step(tt(row(R_u), row(R_am), row(R_LI), MUL))
            own.step(tt(row(R_t), row(R_t), row(R_u), SUB))
            tt(co_im, row(R_t), row(R_den), MUL).then_inc(dve_par, 1)
            bank = wait_turn(dve, "par")
            dve.tensor_copy(par[:, :, :].rearrange("p i j -> p (i j)"), bank[:, 0:448]).then_inc(tr_free[TURN["par"] % 2], 1)
            norm(0, xn_ready)
            split_static(0)
            split_static(1)
            mixer(0)

            def hidden2(g, tr, first):
                for th in range(TH):
                    dve.wait_ge(g_ready, g + th)
                    if not first:
                        dve.wait_ge(ht_tr, tr)
                    tt(v_flat[:, (2 + th) * FC:(3 + th) * FC], v_flat[:, th * FC:(th + 1) * FC], PJ[th][:, FC:2 * FC],
                       MUL).then_inc(h_done, 1)

            def hidden_lo(n, cols):
                dve.wait_ge(ht_hi_ready, n)
                tt(ht_lo[:, :, 0:cols], TR[0][:, 0:2 * cols].rearrange("p (f s) -> p f s", f=2),
                   ht_hi[:, :, 0:cols].bitcast(f32), SUB).then_inc(ht_lo_ready, 1)

            t = T_FFN0

            def split_turn(i, tile):
                split(tile, (t + 2 + i) % 3, raw[:, raw_slot(t + 2 + i), :])
            split_turn(0, t + 2)
            hidden2(1, 0, True)
            split_turn(1, t + 3)
            split_turn(2, t + 4)
            hidden_lo(1, SEQ)
            with dve.Fori(1, NCH - 1) as c:
                split_turn(0, c * 3 + (t + 2))
                hidden2(c * 2 + 1, c, False)
                split_turn(1, c * 3 + (t + 3))
                split_turn(2, c * 3 + (t + 4))
                hidden_lo(c + 1, SEQ)
            hidden2(2 * NCH - 1, NCH - 1, False)
            split_static(T_MIX1 - 1)
            hidden_lo(NCH, SEQ)
            split_static(T_MIX1)
            split_static(T_MIX1 + 1)
            dve.wait_ge(tile_used, T_MIX1)
            for i in range(4):
                z = xres[:, i // 2, (i % 2) * 512:(i % 2 + 1) * 512]
                tt(z, z, banks[2 + i][:, :], ADD).then_inc(x_added, 1)
            norm(2, xn_ready)
            mixer(1)

            bank = wait_turn(dve, "router")
            sums = bank[:, 0:32].rearrange("p (t i e) -> p t i e", t=2, i=2)
            own.step(dve.tensor_copy(r_tmp, sums[:, :, 0, :]))
            tt(r_logit, r_tmp, sums[:, :, 1, :], ADD).then_inc(tr_free[TURN["router"] % 2], 1)
            wait_read(dve, "router")
            for th in range(TH):
                own.step(dve.max(r_best[:, th, :], r_logit[:, th, :]))
                own.step(dve.max_index(r_index[:, th, :], r_best[:, th, :], r_logit[:, th, :]))
            tt(r_diff, r_best[:, :, 1], r_best[:, :, 0], SUB).then_inc(sel_early, 1)
            own.step(dve.tensor_copy(r_indexf, r_index[:, :, 0:2]))
            experts_row = cst[:, C_IOTA:C_IOTA + NE]
            for th in range(TH):
                for i in range(2):
                    own.step(ts(r_hot[:, i, th, :], experts_row, r_indexf[:, th, i:i + 1], None, ALU.is_equal))
            tt(sel, r_hot[:, 0, :, :], r_hot[:, 1, :, :], ADD).then_inc(sel_ready, 1)
            own.step(dve.memset(cols, 0.0))
            own.step(dve.memset(cols[:, 0, :, :], -1000.0))
            dve.wait_ge(gate_exp, 1)
            own.step(ts(r_g, r_exp, 1.0, None, ADD))
            own.step(dve.reciprocal(r_g, r_g))
            own.step(tt(r_exp, r_exp, r_g, MUL))
            for i, g in enumerate((r_g, r_exp)):
                own.step(tt(r_hot[:, i, :, :], r_hot[:, i, :, :], g.unsqueeze(2).broadcast_to([P, 2, NE]), MUL))
            own.step(tt(cols[:, 1, :, 0:NE], r_hot[:, 0, :, :], r_hot[:, 1, :, :], ADD))
            bank = wait_turn(dve, "pos")
            pos = bank[:, 0:16].rearrange("p (t e) -> p t e", t=2)
            own.step(stt(r_pos, pos, 1.0, sel, ADD, MUL))
            own.step(ts(cols[:, 0, :, 0:NE], r_pos, -1.0, None, ADD))
            ts(r_over, bank[:, 16:24], float(P), None, ALU.is_gt).then_inc(tr_free[TURN["pos"] % 2], 1)
            wait_read(dve, "pos")
            def places():
                for th in range(TH):
                    m = ts(place[:, th, :], cst[:, C_IOTA:C_IOTA + P], column[:, 0, th:th + 1], None, ALU.is_equal)
                return m

            def gathered(n):
                dve.wait_ge(xe_hi_ready, n)
                for g in range(2):
                    m = tt(at_lo[:, 4 * g:4 * g + 4, 0:P], banks[4 + g][:, :].rearrange("p (k c) -> p k c", k=4),
                           at_hi[:, 4 * g:4 * g + 4, 0:P].bitcast(f32), SUB)
                m.then_inc(xe_lo_ready, 1)

            own.step(dve.tensor_copy(column, cols[:, :, :, 0]))
            places().then_inc(place_ready, 1)
            own.step(dve.tensor_tensor_scan(r_rank, cst[:, C_ONE:C_ONE + NE], r_over, 0.0, MUL, ADD))
            own.step(ts(r_tab[:, 0:1], r_rank[:, NE - 1:NE], float(NE - 1), None, ADD))
            own.step(dve.memset(r_tab[:, 1:2], float(NE - 1)))
            own.step(ts(r_pos, cols[:, 0, :, 0:NE], 1000.0 - P, None, ADD))
            for k in range(MAXB - NE):
                own.step(stt(r_one, r_rank, float(k + 1), r_over, ALU.is_equal, MUL))
                own.step(tt(r_tmp[:, 0, :], r_one, experts_row, MUL))
                own.step(dve.tensor_reduce(r_tab[:, k + 2:k + 3], r_tmp[:, 0, :], AX.X, ADD))
                one = r_one.unsqueeze(1).broadcast_to([P, 2, NE])
                own.step(tt(r_tmp, r_pos, one, MUL))
                own.step(dve.tensor_reduce(cols[:, 0, :, NE + k], r_tmp, AX.X, ADD))
                own.step(ts(cols[:, 0, :, NE + k], cols[:, 0, :, NE + k], -1000.0, None, ADD))
                own.step(tt(r_tmp, cols[:, 1, :, 0:NE], one, MUL))
                own.step(dve.tensor_reduce(cols[:, 1, :, NE + k], r_tmp, AX.X, ADD))
            dve.tensor_copy(table[:, :], r_tab).then_inc(routed, 1)
            gathered(1)

            def hidden(b, c):
                dve.wait_ge(g_ready, b * NCH + (2 * NCH + c + 1))
                dve.wait_ge(ht_tr, b * NCH + (NCH + c))
                tt(v_flat[:, FC:2 * FC], v_flat[:, 0:FC], h_bank(c)[:, FC:2 * FC], MUL).then_inc(h_done, 1)

            def result_lo(b):
                dve.wait_ge(ye_hi_ready, b + 1)
                for n in range(2):
                    m = stt(at_lo[:, 4 * n:4 * n + 4, P:2 * P], PY[n][:, :].rearrange("p (k c) -> p k c", k=4), place_gate,
                            at_hi[:, 4 * n:4 * n + 4, P:2 * P].bitcast(f32), MUL, SUB)
                m.then_inc(ye_ready, 1)

            def add_block(b):
                for i, bank in enumerate(comb_banks):
                    z = xres[:, i // 2, (i % 2) * 512:(i % 2 + 1) * 512]
                    dve.wait_ge(comb_full, b * 4 + (i + 1))
                    tt(z, z, bank[:, :], ADD).then_inc(x_added, 1)

            def expert_step(b, c, final=False):
                if c == NCH:
                    result_lo(b)
                if c >= 0:
                    split_moe(b, FFN_TILES - 1 if final and c == NCH - 1 else 3 * c + 4)
                    hidden_lo(b * NCH + (NCH + c + 1), P)
                if not (final and c + 2 >= NCH):
                    split_moe(b, 3 * c + 5)
                if not (final and c + 1 >= NCH):
                    hidden(b, c + 1)
                if c == 5 and not final:
                    dve.wait_ge(gt_ready, b + 1)
                    own.step(dve.tensor_copy(column, cols[:, :, :, bass.ds(b + 1, 1)].rearrange("p a t o -> p a (t o)")))
                    places().then_inc(place_ready, 1)
                if c == NCH - 2 and not final:
                    gathered(b + 2)
                if not (final and c + 2 >= NCH):
                    split_moe(b, 3 * c + 6)
                if c == NCH:
                    add_block(b)

            expert_step(0, -1)
            expert_step(0, 0)
            dve.wait_ge(routed, 1)
            last = dve.value_load(table[0:1, 0:1], min_val=NE - 1, max_val=MAXB - 1)
            with dve.Fori(0, last) as b:
                own.loop(b, 1)
                for c in range(1, NCH + 1):
                    expert_step(b, c)
                own.end()
            for c in range(1, NCH):
                expert_step(last, c, True)
            result_lo(last)
            add_block(last)
            norm(4, final_ready)

        @block.gpsimd
        def _(pool):
            own = Order(pool, pool_own)
            tt = pool.tensor_tensor

            def cmul(out_re, out_im, a, a_swapped, b_re, b_im, t1, t2):
                tt(t1, a, b_re, MUL)
                own.step(tt(t2, a_swapped, b_im, MUL))
                tt(out_re, t1[:, 0], t2[:, 0], SUB)
                own.step(tt(out_im, t1[:, 1], t2[:, 1], ADD))

            def load_matrices(l):
                for r, src in enumerate((ssm_b_re, ssm_b_im)):
                    v = src[l, :, :, :, :].rearrange("d g s h -> (d g) s h").rearrange("(j g) s h -> g s j h", g=2)
                    for g in range(2):
                        pool.dma_start(braw[64 * g:64 * (g + 1), r, :, :], v[g, :, :, :]).then_inc(bc_in, 16)
                for r, src in enumerate((ssm_c_re, ssm_c_im)):
                    for a in range(2):
                        pool.dma_start(craw[r][:, :, a, :], src[l, :, :, :, :].rearrange("d g h s -> (d g h) s")
                                       .rearrange("(i p) s -> p i s", p=P)).then_inc(bc_in, 16)

            def load_dskip(l):
                for q2 in range(2):
                    for t in range(2):
                        r0 = q2 * 64 + t * 32
                        pool.dma_start(dskip[r0:r0 + 32, l, :],
                                       ssm_d[l, :].rearrange("(b q c) -> q c b", b=8, q=2)[q2, :, :],
                                       allow_slow_non_contiguous=True).then_inc(dskip_in, 16)

            def signal_mats():
                pool.memset(zero_mark, 0.0).then_inc(mats_ready, 1)

            def phasors(l):
                j0 = 32 * l
                t1, t2 = area(TMP, 512), area(TMP + 512, 512)
                sq = [area(TMP + 1024 + 64 * i, 64).rearrange("p (r j) -> p r j", r=2) for i in range(2)]

                def small_t(t, n):
                    return t[:, 0:64 * n].rearrange("p (r j n) -> p r j n", r=2, j=32)

                def square(dst, src):
                    s1, s2 = (small_t(t, 1)[:, :, :, 0] for t in (t1, t2))
                    cmul(dst[:, 0, :], dst[:, 1, :], src, src[:, ::-1, :], src[:, 0:1, :].broadcast_to([P, 2, 32]),
                         src[:, 1:2, :].broadcast_to([P, 2, 32]), s1, s2)
                square(sq[0], par[:, COS:SIN + 1, j0:j0 + 32])
                power = 0
                for tab, n in ((w1t, 16), (w16t, 8)):
                    pool.memset(tab[:, 0, :, 0:1], 1.0)
                    pool.memset(tab[:, 1, :, 0:1], 0.0)
                    own.step(pool.tensor_copy(tab[:, :, :, 1], sq[power % 2]))
                    k = 2
                    while k < n:
                        square(sq[(power + 1) % 2], sq[power % 2])
                        power += 1
                        p = sq[power % 2]
                        a = tab[:, :, :, 0:k]
                        cmul(tab[:, 0, :, k:2 * k], tab[:, 1, :, k:2 * k], a, a[:, ::-1, :, :],
                             p[:, 0:1, :].unsqueeze(3).broadcast_to([P, 2, 32, k]),
                             p[:, 1:2, :].unsqueeze(3).broadcast_to([P, 2, 32, k]), small_t(t1, k), small_t(t2, k))
                        k *= 2
                    square(sq[(power + 1) % 2], sq[power % 2])
                    power += 1

            def build(l):
                j0 = 32 * l

                def num(i):
                    return par[:, i, j0:j0 + 32]

                def times(dst, src, re, im):
                    cmul(dst[:, 0], dst[:, 1], src, src[:, ::-1, :, :],
                         num(re).unsqueeze(1).unsqueeze(3).broadcast_to([P, 2, 32, GC]),
                         num(im).unsqueeze(1).unsqueeze(3).broadcast_to([P, 2, 32, GC]), bt1, bt2)
                if l == 1:
                    pool.memset(gflat, 0.0)
                pool.wait_ge(bc_in, BC_LOADS * (l + 1))
                times(bbar, braw, CO_RE, CO_IM)
                times(babar, bbar, A_RE, A_IM)
                signal_mats()
                wait_read(pool, (l, "ct", 2))
                wait_read(pool, (l, "ct", 3))
                times(cabar, ctr, A_RE, A_IM)
                signal_mats()

            def phase_products(l, q):
                if 16 * l + q > 0:
                    pool.wait_ge(wtab_ready, 16 * l + q)
                for dst, (r1, r16) in zip(php, ((1, 1), (0, 1), (1, 0))):
                    m = phase_product(tt, dst, l, q, r1, r16)
                m.then_inc(php_ready, 1)

            def turn_forward(l, q):
                n = 16 * l + q
                w, xs = wtab[q % 2], xst_flat[q % 2]
                pool.wait_ge(wtab_ready, n + 1)
                pool.wait_ge(zs_ready, n + 1)
                if n > 0:
                    pool.wait_ge(states_ready, n)
                for po, z, r in ((po1, zs, 0), (po2, zs[:, ::-1, :], 1)):
                    for d in range(2):
                        half = slice(d * P, (d + 1) * P)
                        dst = po[:, :, 0:P] if d == 0 else po[:, :, 2 * P - 1:P - 1:-1]
                        m = tt(dst, z[:, :, half], w[:, r:r + 1, half].broadcast_to([P, 2, P]), MUL)
                m.then_inc(zs_used, 1)
                pool.wait_ge(zs_used, n + 1)
                if n >= 2:
                    pool.wait_ge(y_done, n - 1)
                tt(xs[:, 0, 1:2 * P + 1], po1[:, 0, :], po2[:, 0, :], SUB)
                tt(xs[:, 1, 1:2 * P + 1], po1[:, 1, :], po2[:, 1, :], ADD).then_inc(states_ready, 1)

            load_matrices(0)
            load_dskip(0)
            load_dskip(1)
            pool.memset(area(4096, 4096), 0.0)
            wait_read(pool, "par")
            for l in range(2):
                if l == 1:
                    pool.wait_ge(y_done, PAIRS)
                    load_matrices(1)
                    pool.wait_ge(at_lo_ready, at_count(0, "m", 3))
                    phasors(1)
                build(l)
                if l == 0:
                    pool.wait_ge(b_laid, 1)
                    phasors(0)
                pool.wait_ge(blocks_ready, l + 1)
                pool.wait_ge(mats_ready, 2 * l + 2)
                for xs in xst:
                    pool.memset(xs[:, :, 0, 0:1], 0.0)
                    pool.memset(xs[:, :, 1, P:P + 1], 0.0)
                phase_products(l, 0)
                for q in range(PAIRS):
                    if q + 1 < PAIRS:
                        phase_products(l, q + 1)
                    turn_forward(l, q)


_INS = ["x", "norm_mix", "w_in", "attn_lambda", "attn_subln", "ssm_lam_re", "ssm_lam_im", "ssm_log_dt", "ssm_b_re",
        "ssm_b_im", "ssm_c_re", "ssm_c_im", "ssm_d", "w_glu", "w_branch", "w_out", "norm_ffn", "ffn_w1", "ffn_w3",
        "ffn_w2", "moe_router", "moe_w1", "moe_w3", "moe_w2", "norm_final"]


def shape_constants():
    import numpy as np
    c = np.zeros((P, C_END), np.float32)
    c[:, C_ID:C_ID + P] = np.eye(P)
    c[:, C_TRI:C_TRI + P] = np.triu(np.ones((P, P)), 1)
    c[:, C_ONE:C_ONE + P] = 1.0
    c[:, C_IOTA:C_IOTA + P] = np.arange(P)
    c[:, C_MASK:C_MASK + P] = np.arange(P) > 0
    c[:, C_PAT:C_PAT + 32] = (np.arange(P)[:, None] % 32) == np.arange(32)
    half = HD // 2
    freq = (1.0 / (np.float32(10000.0) ** (np.arange(half, dtype=np.float32) / np.float32(half)))).astype(np.float32)
    pos = (2 * np.arange(P)[:, None] + np.arange(TH)).astype(np.float32)
    ang = (pos[:, :, None] * freq).astype(np.float32).astype(np.float64)
    c[:, C_COS:C_COS + P] = np.concatenate([np.cos(ang), np.cos(ang)], -1).reshape(P, P)
    c[:, C_SIN:C_SIN + P] = np.concatenate([-np.sin(ang), np.sin(ang)], -1).reshape(P, P)
    return c


def kernel(**inputs):
    import numpy as _np
    import concourse.bacc as _bacc
    from concourse import mybir as _mybir
    from concourse.bass_utils import run_bass_kernel_spmd as _run

    nc = _bacc.Bacc("TRN2", target_bir_lowering=False, num_devices=1)
    arrays, args = {}, []
    for name in _INS + ["consts"]:
        a = shape_constants() if name == "consts" else _np.ascontiguousarray(inputs[name])
        arrays[f"in_{name}_dram"] = a
        args.append(nc.dram_tensor(f"in_{name}_dram", a.shape, _mybir.dt.from_np(a.dtype), kind="ExternalInput").ap())
    args.append(nc.dram_tensor("out_0_dram", (1, SEQ, D), _mybir.dt.float32, kind="ExternalOutput").ap())
    build(nc, *args)
    r = _run(nc, [arrays], core_ids=[0])
    return r.results[0]["out_0_dram"]
```

```python
import math
import concourse.bass as bass
from concourse import mybir
from contextlib import ExitStack

P = 128
SEQ, D = 256, 1024
TH = SEQ // P
KD = D // P
HEADS, HD = 4, 64
WA = HEADS * 2 * HD
NGATE = 2
IN_WIDTH = 4 * WA + NGATE * D
D_FF = 2816
NE = 8
MAXB = NE + 3
PAIRS, GC, NS = 16, 16, 64
EPS = 1e-6
TW = 2048
RAWS, SPLITS = 11, 3
FC = 256
NCH = D_FF // FC
MIX_TILES, FFN_TILES = 25, 3 * NCH
T_FFN0 = MIX_TILES
T_MIX1 = T_FFN0 + FFN_TILES
T_MOE = T_MIX1 + MIX_TILES
T_MIX = (0, T_MIX1)
C_ID, C_TRI, C_ONE, C_IOTA, C_MASK, C_PAT, C_COS, C_SIN = 0, 128, 256, 384, 512, 640, 672, 800
C_END = 928

GROUPS = (0, 2, 1, 3)
W_IN_ORDER = [3, 0, 1, 2, 4, 5, 6, 7]


def mixer_turns():
    names = []
    for l in range(2):
        names += [(l, "x", g) for g in GROUPS] + (["par"] if l == 0 else []) + [(l, "ct", g) for g in range(4)]
        names += [(l, "u", g) for g in range(2)] + [(l, "q", t) for t in range(2)] + [(l, "k", t) for t in range(2)]
        names += [(l, "b", g) for g in range(8)] + [(l, "cb", 0)]
        for s in range(9):
            if s < 8:
                names.append((l, "sc", s))
            if s > 0:
                names.append((l, "o", s - 1))
        names += [(l, "a", t) for t in range(2)] + [(l, "s", t) for t in range(2)] + [(l, "s2", t) for t in range(2)]
        names += [(l, "m", g) for g in GROUPS] + [(l, "h", g) for g in GROUPS]
    names += ["router", "pos"]
    return {name: n for n, name in enumerate(names)}


TURN = mixer_turns()
AT_ORDER = {name: n for n, name in enumerate(
    [("x", g) for g in GROUPS] + [("sa", t) for t in range(2)] + [("a", t) for t in range(2)]
    + [("s2", t) for t in range(2)] + [("m", g) for g in GROUPS] + [("h", g) for g in GROUPS])}
AT_PER_LAYER = len(AT_ORDER)
AHEAD = 8
PJ_PER_LAYER = 15


class Order:

    def __init__(self, eng, sem):
        self.eng, self.sem, self.n, self.turn, self.per = eng, sem, 0, None, 0

    def step(self, ins):
        ins.then_inc(self.sem, 1)
        self.n += 1
        self.eng.wait_ge(self.sem, self.n if self.turn is None else self.turn * self.per + self.n)

    def loop(self, turn, per):
        self.turn, self.per, self.start = turn, per, self.n

    def end(self, trips=None):
        assert self.n - self.start == self.per, (self.n - self.start, self.per)
        self.turn = None
        if trips is not None:
            self.n = self.start + trips * self.per


def build(nc, x, norm_mix, w_in, attn_lambda, attn_subln, ssm_lam_re, ssm_lam_im, ssm_log_dt, ssm_b_re, ssm_b_im,
          ssm_c_re, ssm_c_im, ssm_d, w_glu, w_branch, w_out, norm_ffn, ffn_w1, ffn_w3, ffn_w2, moe_router,
          moe_w1, moe_w3, moe_w2, norm_final, consts, out):
    f32, f32r, i32, u32 = mybir.dt.float32, mybir.dt.float32r, mybir.dt.int32, mybir.dt.uint32
    ACT, ALU, AX = mybir.ActivationFunctionType, mybir.AluOpType, mybir.AxisListType
    MUL, ADD, SUB = ALU.mult, ALU.add, ALU.subtract
    ctx = ExitStack()
    with ctx:
        def sb(name, shape, dt=f32):
            return ctx.enter_context(nc.sbuf_tensor(name, shape, dt))

        def sem(name):
            return ctx.enter_context(nc.semaphore(name))

        raw = sb("raw", [P, RAWS, TW])
        hi = sb("hi", [P, SPLITS, TW], f32r)
        lo = sb("lo", [P, SPLITS, TW], f32r)
        at_hi = sb("at_hi", [P, KD, SEQ], f32r)
        at_lo = sb("at_lo", [P, KD, SEQ], f32r)
        ht_hi = sb("ht_hi", [P, 2, SEQ], f32r)
        ht_lo = sb("ht_lo", [P, 2, SEQ], f32r)
        xres = sb("xres", [P, TH, D])
        gates = sb("gates", [P, TH, NGATE, D])
        qk = sb("qk", [P, 2, TH, WA])
        vreg = sb("vreg", [P, TH, WA])
        ureg = sb("ureg", [P, TH, WA])
        areg = sb("areg", [P, TH, WA])
        cst = sb("cst", [P, C_END])
        par = sb("par", [P, 7, 64])
        subln = sb("subln", [P, 2, P])
        small = sb("small", [P, 96])
        php_last = sb("php_last", [P, 256])
        sum_ready, y_half, xn_scaled, whole_inv = sem("sum_ready"), sem("y_half"), sem("xn_scaled"), sem("whole_inv")
        factor_ready, second_scaled = sem("factor_ready"), sem("second_scaled")
        half_scores, b_laid = sem("half_scores"), sem("b_laid")
        table = sb("table", [P, 5], i32)

        ident = cst[:, C_ID:C_ID + P]
        xn = qk[:, :, :, :].rearrange("p a t c -> p (a t c)").rearrange("p (t d) -> p t d", t=TH)
        gain = areg[:, :, :].rearrange("p t c -> p (t c)")
        gflat = gates[:, :, :, :].rearrange("p t g d -> p (t g d)")
        ssm = raw[:, 3:RAWS, :].rearrange("p s w -> p (s w)")

        def area(start, size):
            return ssm[:, start:start + size]
        bbt = area(0, 4096).rearrange("p (d r b c) -> p d r b c", d=2, r=2, b=8)
        cblk = area(4096, 4096).rearrange("p (k r d q g h) -> p k r d q g h", k=2, r=2, d=2, q=PAIRS, g=2)
        ut2 = area(8192, 1024).rearrange("p (b c) -> p b c", b=8)
        cbm = area(9216, 256).rearrange("p (b c) -> p b c", b=8)
        w1t = area(9472, 1024).rearrange("p (r j c) -> p r j c", r=2, c=16)
        w16t = area(10496, 512).rearrange("p (r j c) -> p r j c", r=2, c=8)
        TMP = 11008
        wtab = [area(TMP + 512 * i, 512).rearrange("p (r c) -> p r c", r=2) for i in range(2)]
        rot1 = area(TMP + 1280, 512).rearrange("p (r c) -> p r c", r=2)
        rot2 = area(TMP + 1792, 512).rearrange("p (r c) -> p r c", r=2)
        zs = area(TMP + 2304, 512).rearrange("p (r c) -> p r c", r=2)
        po1 = area(TMP + 2816, 512).rearrange("p (r c) -> p r c", r=2)
        po2 = area(TMP + 3328, 512).rearrange("p (r c) -> p r c", r=2)
        xst_flat = [area(TMP + 3840 + 516 * i, 516).rearrange("p (r c) -> p r c", r=2) for i in range(2)]
        xst = [x2.rearrange("p r (d c) -> p r d c", d=2) for x2 in xst_flat]
        php = [area(TMP + 1024, 256), area(TMP + 4872, 256), php_last[:, :]]

        def four(ap):
            return ap.rearrange("p (r j h) -> p r j h", r=2, h=GC)
        braw, bt1, bt2 = four(area(0, 1024)), four(area(1024, 1024)), four(area(2048, 1024))
        bbar, babar, ctr, cabar = [four(area(TMP + 1024 * i, 1024)) for i in range(4)]
        craw = [area(c0, 1024).rearrange("p (i a s) -> p i a s", i=8, a=2) for c0 in (8192, TMP + 4096)]
        bpre = gflat.rearrange("p (d r b q t g h) -> p d r b q t g h", d=2, r=2, b=8, q=2, t=2, g=2)

        banks = [ctx.enter_context(nc.psum_tensor(f"bank{i}", [P, 512], f32)) for i in range(8)]
        PJ, PY, PV, TR = banks[0:2], banks[2:4], banks[4:6], banks[6:8]

        raw_full = [sem(f"raw_full{i}") for i in range(RAWS)]
        hi_ready, lo_ready, tile_used = sem("hi_ready"), sem("lo_ready"), sem("tile_used")
        loads = sem("loads")
        rows_in, lam_in = sem("rows_in"), sem("lam_in")
        router_hi_ready, router_ready = sem("router_hi_ready"), sem("router_ready")
        gain_in = sem("gain_in")
        bc_in = sem("bc_in")
        dskip_in = sem("dskip_in")
        sq_ready, var_ready, root_ready, xn_ready = sem("sq_ready"), sem("var_ready"), sem("root_ready"), sem("xn_ready")
        tr_full = sem("tr_full")
        tr_free = [sem("tr_free0"), sem("tr_free1")]
        at_hi_ready, at_lo_ready = sem("at_hi_ready"), sem("at_lo_ready")
        pj0_full = sem("pj0_full")
        pj_free = [sem("pj_free0"), sem("pj_free1")]
        dve_own, pool_own, act_own = sem("dve_own"), sem("pool_own"), sem("act_own")
        act_par, dve_par = sem("act_par"), sem("dve_par")
        rot_ready = sem("rot_ready")
        mats_ready, blocks_ready = sem("mats_ready"), sem("blocks_ready")
        bzero_ready = sem("bzero_ready")
        pv_full, pv_free, wtab_ready, php_ready = sem("pv_full"), sem("pv_free"), sem("wtab_ready"), sem("php_ready")
        zs_ready, zs_used, states_ready, y_done = sem("zs_ready"), sem("zs_used"), sem("states_ready"), sem("y_done")
        max_ready, exp_ready, w_ready, wt_tr, wt_ready = sem("max_ready"), sem("exp_ready"), sem("w_ready"), sem("wt_tr"), sem("wt_ready")
        avar_ready, aroot_ready, a_ready = sem("avar_ready"), sem("aroot_ready"), sem("a_ready")
        s_ready, m_ready, x_added = sem("s_ready"), sem("m_ready"), sem("x_added")
        lam_ready, lam_exp = sem("lam_ready"), sem("lam_exp")
        h_full, g_ready, h_done, ht_tr, ht_hi_ready, ht_lo_ready = (sem("h_full"), sem("g_ready"), sem("h_done"), sem("ht_tr"),
                                                                    sem("ht_hi_ready"), sem("ht_lo_ready"))
        sel_ready, routed, final_ready = sem("sel_ready"), sem("routed"), sem("final_ready")
        stored = sem("stored")
        gate_exp, router_in, place_ready, pg_full, gt_ready = (sem("gate_exp"), sem("router_in"), sem("place_ready"),
                                                               sem("pg_full"), sem("gt_ready"))
        ye_hi_ready = sem("ye_hi_ready")
        xe_full, xe_hi_ready, xe_lo_ready, ye_ready, comb_full = (sem("xe_full"), sem("xe_hi_ready"), sem("xe_lo_ready"),
                                                                  sem("ye_ready"), sem("comb_full"))
        def raw_slot(t):
            return t % 3

        def raw_uses(slot, before):
            return sum(1 for t in range(before) if raw_slot(t) == slot)

        def moe_slot(j):
            return (list(range(3, RAWS)) + [raw_slot(T_MOE - 3 + i) for i in range(3)])[j % RAWS]

        def moe_tile(j):
            if j < 2:
                return "ab"[j], 0, 0
            c, i = (j - 2) // 3, (j - 2) % 3
            g = c if i == 2 else c + 1
            return "abc"[i], g % NCH, g // NCH

        def moe_full_value(j, turn):
            s = moe_slot(j)
            base = raw_uses(s, T_MOE) if s < 3 else 0
            first = min(i for i in range(FFN_TILES) if moe_slot(i) == s)
            return turn * (32 * FFN_TILES // RAWS) + 32 * (base + (j - first) // RAWS + 1)

        SS, VAR, RT, RI, MX, NB, RS, RR, C1 = 0, 2, 4, 6, 8, 10, 12, 14, 16
        SS2, RH = 94, 66
        AS, AV, AR, AI, LSUM, LEXP, NLAM = 24, 32, 40, 48, 56, 60, 64

        def col(i, n=1):
            return small[:, i:i + n]

        def row(i, n=1):
            return gflat[0:64, i * P:(i + n) * P]
        lamv = gflat[:, 4 * P:8 * P].rearrange("p (l a b c) -> p l a b c", l=2, a=2, b=2)
        lamp = gflat[:, 26 * P:28 * P].rearrange("p (j c) -> p j c", c=HD)
        R_LR, R_LI, R_DT, R_EDT, R_lr, R_li, R_k, R_red, R_er, R_sn, R_sh, R_t, R_u, R_den, R_am = (
            0, 1, 2, 3, 8, 9, 10, 11, 12, 13, 14, 15, 23, 24, 25)
        PACK = 16
        A_RE, A_IM, CO_RE, CO_IM, COS, SIN, RAD2 = range(7)

        kflat = qk[:, 1, :, :].rearrange("p t c -> p (t c)")
        probs = kflat[:, 0:512].rearrange("p (a k) -> p a k", a=2)
        wdiff = kflat[:, 512:768]
        wdiff_t = kflat[:, 768:1024].rearrange("p (t q) -> p t q", t=2)
        u_rows = ureg[:, :, :].rearrange("p t c -> p (t c)").rearrange("p (q t c) -> p q t c", q=PAIRS, t=TH)
        u_flat = ureg[:, :, :].rearrange("p t c -> p (t c)")
        q_t = u_flat.rearrange("p (h s) -> p h s", h=HEADS)
        k_t = qk[:, 0, :, :].rearrange("p t c -> p (t c)").rearrange("p (h s) -> p h s", h=HEADS)
        s_t = u_flat.rearrange("p (k s) -> p k s", k=4)
        s_gated = qk[:, 0, :, :]
        a_flat = areg[:, :, :].rearrange("p t c -> p (t c)")
        v_flat = vreg[:, :, :].rearrange("p t c -> p (t c)")

        free_at, seen = {}, [0, 0]
        for name, n in TURN.items():
            if name != "par" and name[1:] in AT_ORDER:
                free_at[name] = (at_lo_ready, name[0] * AT_PER_LAYER + AT_ORDER[name[1:]] + 1)
            else:
                seen[n % 2] += 1
                free_at[name] = (tr_free[n % 2], seen[n % 2])
        NAME = {n: name for name, n in TURN.items()}

        def at_count(l, kind, g):
            return l * AT_PER_LAYER + AT_ORDER[(kind, g)] + 1

        def wait_read(eng, name):
            s, v = free_at[name]
            eng.wait_ge(s, v)

        def wait_turn(eng, name):
            eng.wait_ge(tr_full, TURN[name] + 1)
            return TR[TURN[name] % 2]

        def use(l, i):
            return PJ_PER_LAYER * l + i

        def pj_read(l, i):
            return (PJ_PER_LAYER - 2) * l + i + 1


        def piece(start, size):
            return gflat[:, start:start + size]
        cols = piece(256, 48).rearrange("p (a t e) -> p a t e", a=2, t=2)
        column = small[:, 72:76].rearrange("p (a t) -> p a t", a=2)
        r_logit = piece(320, 16).rearrange("p (t e) -> p t e", t=2)
        r_best = piece(336, 16).rearrange("p (t e) -> p t e", t=2)
        r_index = piece(352, 16).rearrange("p (t e) -> p t e", t=2).bitcast(u32)
        r_indexf = piece(368, 4).rearrange("p (t e) -> p t e", t=2)
        r_diff, r_exp, r_g = piece(372, 2), piece(374, 2), piece(376, 2)
        r_hot = piece(384, 32).rearrange("p (i t e) -> p i t e", i=2, t=2)
        sel = piece(416, 16).rearrange("p (t e) -> p t e", t=2)
        r_pos = piece(432, 16).rearrange("p (t e) -> p t e", t=2)
        r_over, r_rank, r_one = piece(448, 8), piece(456, 8), piece(464, 8)
        r_tmp = piece(472, 16).rearrange("p (t e) -> p t e", t=2)
        r_tab = piece(488, 5)
        router = piece(512, 64).rearrange("p (k e) -> p k e", k=KD)
        router_parts = ht_hi[:, 0, 0:KD * 2 * NE].rearrange("p (k c) -> p k c", k=KD)
        place = vreg[:, 1, 0:256].rearrange("p (t s) -> p t s", t=2)
        dskip = small[:, 76:92].rearrange("p (l b) -> p l b", l=2)
        zero_mark = small[:, 92:93]
        dve_rows, sel_early, inv_ready = sem("dve_rows"), sem("sel_early"), sem("inv_ready")
        BC_LOADS = 16 * 8
        place_gate = small[:, 93:94]
        comb_banks = (TR[0], TR[1], PV[0], PV[1])

        def phase_product(tt, dst, l, q, r1, r16):
            return tt(dst.rearrange("p (d a c) -> p d a c", d=2, a=8),
                      w1t[:, r1, q::PAIRS, :].unsqueeze(2).broadcast_to([P, 2, 8, 16]),
                      w16t[:, r16, q::PAIRS, :].unsqueeze(3).broadcast_to([P, 2, 8, 16]), MUL)

        def h_bank(c):
            return TR[1] if c % NCH == NCH - 1 else PJ[c % NCH % 2]

        block = ctx.enter_context(nc.Block())

        @block.sync
        def _(sp):
            sp.dma_start(xres[:, :, :], x[0, :, :].rearrange("(p t) d -> p t d", t=TH)).then_inc(loads, 16)
            sp.dma_start(cst[:, :], consts).then_inc(loads, 16)
            sp.wait_ge(rows_in, 48)

            def load(slot, parts):
                for dst, src in parts:
                    sp.dma_start(dst, src).then_inc(raw_full[slot], 16)

            def split_k(slot, w, k0, c0, n):
                kk = TW // n
                dst = raw[:, slot, :].rearrange("p (k c) -> p k c", c=n)
                src = w[k0 * P:(k0 + kk) * P, c0:c0 + n].rearrange("(k p) c -> p k c", p=P)
                return [(dst[:, h * kk // 2:(h + 1) * kk // 2, :], src[:, h * kk // 2:(h + 1) * kk // 2, :]) for h in range(2)]

            def ffn_parts(slot, kind, c, w1, w3, w2):
                if kind == "c":
                    return split_k(slot, w2, c * FC // P, 0, D)
                k0 = 0 if kind == "a" else KD // 2
                dst = raw[:, slot, :].rearrange("p (k w c) -> p k w c", w=2, c=FC)
                return [(dst[:, :, i, :],
                         w[k0 * P:(k0 + 4) * P, c * FC:(c + 1) * FC].rearrange("(k p) c -> p k c", p=P))
                        for i, w in enumerate((w1, w3))]

            def static_tile(t, parts):
                slot = raw_slot(t)
                if t >= 3:
                    sp.wait_ge(lo_ready, t - 2)
                load(slot, parts(slot))

            def expert_tile(j, here, after):
                kind, c, which = moe_tile(j)
                m1, m3, m2 = [m[0, bass.ds(after if which else here, 1), :, :].rearrange("e a b -> (e a) b")
                              for m in (moe_w1, moe_w3, moe_w2)]
                load(moe_slot(j), ffn_parts(moe_slot(j), kind, c, m1, m3, m2))

            def mixer(l):
                t = T_MIX[l]
                for n in W_IN_ORDER:
                    for kh in range(2):
                        static_tile(t, lambda s: split_k(s, w_in[l, :, :], 4 * kh, 512 * n, 512))
                        t += 1
                for b, n in ((None, 0), (0, 0), (0, 1), (1, 0), (1, 1)):
                    if l == 1 and (b, n) == (1, 1):
                        sp.wait_ge(y_done, 2 * PAIRS)
                    w = w_glu[l, :, :] if b is None else w_branch[l, b, :, :]
                    static_tile(t, lambda s: split_k(s, w, 0, 512 * n, 512))
                    t += 1
                for n in range(2):
                    for kh in range(2):
                        static_tile(t, lambda s: split_k(s, w_out[l, :, :], 4 * kh, 512 * n, 512))
                        t += 1
                        if l == 1:
                            for j in (4 * n + 2 * kh, 4 * n + 2 * kh + 1):
                                expert_tile(j, 0, 0)

            mixer(0)
            f1, f3, f2 = ffn_w1[0, :, :], ffn_w3[0, :, :], ffn_w2[0, :, :]
            for i, kind in enumerate("ab"):
                static_tile(T_FFN0 + i, lambda s: ffn_parts(s, kind, 0, f1, f3, f2))
            with sp.Fori(0, NCH - 1) as c:
                for i, (kind, ahead) in enumerate((("a", 1), ("b", 1), ("c", 0))):
                    slot = raw_slot(T_FFN0 + 2 + i)
                    sp.wait_ge(lo_ready, 3 * c + (T_FFN0 + 2 + i - 2))
                    if kind == "c":
                        dst = raw[:, slot, :].rearrange("p (f c) -> p f c", c=D)
                        for f in range(2):
                            sp.dma_start(dst[:, f, :], f2[bass.ds(c * FC + f * P, P), :]).then_inc(raw_full[slot], 16)
                    else:
                        k0 = 0 if kind == "a" else 4
                        dst = raw[:, slot, :].rearrange("p (k w c) -> p k w c", w=2, c=FC)
                        for j, w in enumerate((f1, f3)):
                            src = w[k0 * P:(k0 + 4) * P, bass.ds(c * FC + FC, FC)].rearrange("(k p) c -> p k c", p=P)
                            sp.dma_start(dst[:, :, j, :], src).then_inc(raw_full[slot], 16)
            static_tile(T_MIX1 - 1, lambda s: ffn_parts(s, "c", NCH - 1, f1, f3, f2))
            mixer(1)

            def expert(turn, here, after):
                for j in range(AHEAD, FFN_TILES + AHEAD):
                    kind, c, which = moe_tile(j)
                    if after is None:
                        if which:
                            continue
                        j = min(j, FFN_TILES - 1)
                    sp.wait_ge(lo_ready, turn * FFN_TILES + (T_MOE + j - RAWS + 1))
                    if after is None and j == FFN_TILES - 1:
                        m2 = moe_w2[0, bass.ds(here, 1), :, :].rearrange("e a b -> (e a) b")
                        load(moe_slot(j), split_k(moe_slot(j), m2, (NCH - 1) * FC // P, 0, D))
                    else:
                        expert_tile(j, here, after)

            with sp.Fori(0, NE - 1) as e:
                expert(e, e, e + 1)
            sp.wait_ge(routed, 1)
            last = sp.value_load(table[0:1, 0:1], min_val=NE - 1, max_val=MAXB - 1)

            def expert_of(b):
                return sp.value_load(table[0:1, bass.ds(b - (NE - 2), 1)], min_val=0, max_val=NE - 1)
            with sp.If(last > NE - 1):
                with sp.Fori(NE - 1, last) as b:
                    expert(b, expert_of(b), expert_of(b + 1))
            expert(last, expert_of(last), None)
            for th in range(TH):
                sp.wait_ge(final_ready, th + 1)
                sp.dma_start(out[0, :, :].rearrange("(p t) d -> p t d", t=TH)[:, th, :], xn[:, th, :]).then_inc(stored, 16)
            sp.wait_ge(stored, 32)
        @block.tensor
        def _(pe):
            def mm(o, a, b, start, stop):
                return pe.matmul(o, a, b, start=start, stop=stop)

            def three(o, a_hi, a_lo, b_hi, b_lo, start, stop):
                mm(o, a_hi, b_hi, start, False)
                mm(o, a_hi, b_lo, False, False)
                return mm(o, a_lo, b_hi, False, stop)

            def open_turn(name):
                n = TURN[name]
                if n >= 2:
                    wait_read(pe, NAME[n - 2])
                return TR[n % 2]

            def transposes(name, sources):
                bank = open_turn(name)
                for i, src in enumerate(sources):
                    rows = src.shape[0]
                    last = pe.transpose(bank[:, i * rows:(i + 1) * rows], src, ident[0:rows, 0:rows])
                last.then_inc(tr_full, 1)

            def proj(t, l, i, k0, first, last, between=None):
                pe.wait_ge(lo_ready, t + 1)
                s = t % SPLITS
                for th in range(TH):
                    if first and i == PJ_PER_LAYER - 1:
                        pe.wait_ge(x_added, 8 * l + th + 1)
                    elif first and i > 0:
                        pe.wait_ge(pj_free[th], pj_read(l, i - 1))
                    for k in range(4):
                        m = three(PJ[th][:, :], at_hi[:, k0 + k, th * P:(th + 1) * P], at_lo[:, k0 + k, th * P:(th + 1) * P],
                                  hi[:, s, k * 512:(k + 1) * 512], lo[:, s, k * 512:(k + 1) * 512],
                                  first and k == 0, last and k == 3)
                    if last and th == 0:
                        m.then_inc(pj0_full, 1)
                    if between is not None and th == 0:
                        between()
                m.then_inc(tile_used, 1)

            def norm_t(l, kind, n):
                for th in range(TH):
                    pe.wait_ge(xn_ready, 8 * l + (0 if kind == "x" else 4) + 2 * n + th + 1)
                    transposes((l, kind, 2 * th + n), [xn[:, th, (4 * n + i) * P:(4 * n + i + 1) * P] for i in range(4)])

            def merged_t(l, n):
                for th in range(TH):
                    pe.wait_ge(m_ready, 4 * l + 2 * n + th + 1)
                    transposes((l, "m", 2 * th + n), [gates[:, th, 0, (4 * n + i) * P:(4 * n + i + 1) * P] for i in range(4)])

            def heads_of(region, th):
                return [region[:, th, h * P:(h + 1) * P] for h in range(HEADS)]

            def s5_in(l, q):
                if 16 * l + q >= 2:
                    pe.wait_ge(pv_free, 16 * l + q - 1)
                b, r0 = q // 2, (q % 2) * 64
                v = PV[q % 2][:, :].rearrange("p (r d c) -> p r d c", r=2, d=2)
                for d in range(2):
                    for r in range(2):
                        rhs = ut2[r0:r0 + 64, b, :] if d == 0 else ut2[r0:r0 + 64, b, ::-1]
                        m = mm(v[:, r, d, :], bbt[r0:r0 + 64, d, r, b, :], rhs, True, True)
                m.then_inc(pv_full, 1)

            def s5_out(l, q):
                pe.wait_ge(states_ready, 16 * l + q + 1)
                xs = xst[q % 2]
                b, k, c0 = q // 2, q // 4, (q % 4) * 32
                for th in range(TH):
                    o = PY[th][c0:c0 + 32, k * P:(k + 1) * P]
                    kinds = ((0, 1), (1, 0)) if th == 0 else ((0, 0), (1, 1))
                    n = 0
                    for d, entering in kinds:
                        for r in range(2):
                            states = xs[:, r, d, 0:P] if entering != d else xs[:, r, d, 1:P + 1]
                            mm(o, cblk[:, entering, r, d, q, :, :].rearrange("p g h -> p (g h)"), states, n == 0, False)
                            n += 1
                    if th == 0 and 16 * l + q > 0:
                        pe.wait_ge(y_done, 16 * l + q)
                    r0 = (q % 2) * 64 + th * 32
                    m = mm(o, cbm[r0:r0 + 32, b, :], ut2[r0:r0 + 32, b, :], False, True)
                m.then_inc(y_done, 1)

            def scores(l, j, c):
                h, th = j // 2, j % 2
                bank = TR[TURN[(l, "sc", j)] % 2]
                if c == 0:
                    open_turn((l, "sc", j))
                else:
                    pe.wait_ge(half_scores, 8 * l + j + 1)
                mm(bank[:, c * SEQ:(c + 1) * SEQ], q_t[c * HD:(c + 1) * HD, h, th * P:(th + 1) * P],
                   k_t[c * HD:(c + 1) * HD, h, :], True, True).then_inc(tr_full if c else half_scores, 1)

            def weights_t(l, j):
                pe.wait_ge(w_ready, 8 * l + j + 1)
                bank = open_turn((l, "o", j))
                for i in range(2):
                    m = pe.transpose(bank[:, i * P:(i + 1) * P], wdiff[:, i * P:(i + 1) * P], ident)
                m.then_inc(wt_tr, 1)

            def head_out(l, j):
                bank, h = TR[TURN[(l, "o", j)] % 2], j // 2
                pe.wait_ge(wt_ready, 8 * l + j + 1)
                for i in range(2):
                    m = mm(bank[:, 2 * P:3 * P], wdiff_t[:, i, :], vreg[:, i, h * P:(h + 1) * P], i == 0, i == 1)
                m.then_inc(tr_full, 1)

            def mixer(l):
                t = T_MIX[l]
                norm_t(l, "x", 0)
                pe.wait_ge(at_lo_ready, at_count(l, "x", 2))
                proj(t, l, 0, 0, True, False, lambda: norm_t(l, "x", 1))
                pe.wait_ge(at_lo_ready, at_count(l, "x", 3))

                def numbers_t():
                    pe.wait_ge(dve_par, 1)
                    transposes("par", [row(PACK + i) for i in range(7)])
                proj(t + 1, l, 0, 4, False, True, numbers_t if l == 0 else None)
                pe.wait_ge(bc_in, BC_LOADS * (l + 1))
                for g in range(4):
                    transposes((l, "ct", g), [craw[g // 2][:, 4 * (g % 2) + i, :, :].rearrange("p a s -> p (a s)") for i in range(4)])
                proj(t + 2, l, 1, 0, True, False)
                proj(t + 3, l, 1, 4, False, True)
                pe.wait_ge(pj_free[1], pj_read(l, 0))
                for g in range(2):
                    transposes((l, "u", g), [u_flat[:, (4 * g + i) * P:(4 * g + i + 1) * P] for i in range(4)])
                proj(t + 4, l, 2, 0, True, False)
                proj(t + 5, l, 2, 4, False, True)
                pe.wait_ge(rot_ready, 4 * l + 2)
                for th in range(TH):
                    transposes((l, "q", th), heads_of(qk[:, 0, :, :], th))
                proj(t + 6, l, 3, 0, True, False)
                proj(t + 7, l, 3, 4, False, True)
                pe.wait_ge(rot_ready, 4 * l + 4)
                for th in range(TH):
                    transposes((l, "k", th), heads_of(qk[:, 1, :, :], th))
                pe.wait_ge(b_laid, 2 * l + 2)
                bp = gflat.rearrange("p (i c) -> p i c", c=P)
                for g in range(8):
                    transposes((l, "b", g), [bp[:, 4 * g + i, :] for i in range(4)])
                pe.wait_ge(blocks_ready, l + 1)
                bank = open_turn((l, "cb", 0))
                for q in range(PAIRS):
                    b, q2 = q // 2, q % 2
                    for d in range(2):
                        r0 = q2 * 64 + d * 32
                        for r in range(2):
                            m = mm(bank[r0:r0 + 32, b * 32:(b + 1) * 32],
                                   bpre[:, d, r, b, q2, 1 - d, :, :].rearrange("p g h -> p (g h)"),
                                   cblk[:, 0, r, d, q, :, :].rearrange("p g h -> p (g h)"), r == 0, r == 1)
                m.then_inc(tr_full, 1)
                wait_read(pe, (l, "b", 6))
                wait_read(pe, (l, "b", 7))
                wait_read(pe, (l, "u", 0))
                wait_read(pe, (l, "u", 1))
                wait_read(pe, (l, "k", 0))
                wait_read(pe, (l, "k", 1))
                wait_read(pe, (l, "q", 1))
                for s in range(8):
                    s5_in(l, 2 * s)
                    scores(l, s, 0)
                    s5_in(l, 2 * s + 1)
                    scores(l, s, 1)
                    if s > 0:
                        weights_t(l, s - 1)
                    proj(t + 8 + s, l, 4 + s // 2, 4 * (s % 2), s % 2 == 0, s % 2 == 1)
                    if s == 0:
                        wait_read(pe, (l, "cb", 0))
                        pe.wait_ge(pj_free[1], pj_read(l, 3))
                    if s > 0:
                        head_out(l, s - 1)
                        s5_out(l, 2 * s - 2)
                        s5_out(l, 2 * s - 1)
                weights_t(l, 7)
                s5_out(l, 14)
                head_out(l, 7)
                s5_out(l, 15)
                pe.wait_ge(at_lo_ready, at_count(l, "sa", 1))

                def attention_t():
                    pe.wait_ge(a_ready, 2 * l + 2)
                    for th in range(TH):
                        transposes((l, "a", th), heads_of(areg, th))

                def gated_s_t():
                    for th in range(TH):
                        wait_read(pe, (l, "s", th))
                    for th in range(TH):
                        transposes((l, "s2", th), heads_of(s_gated, th))
                proj(t + 16, l, 8, 4, True, True, attention_t)
                pe.wait_ge(at_lo_ready, at_count(l, "a", 1))
                for th in range(TH):
                    transposes((l, "s", th), [s_t[:, k, th * P:(th + 1) * P] for k in range(4)])
                proj(t + 17, l, 9, 0, True, True)
                proj(t + 18, l, 10, 0, True, True, gated_s_t)
                pe.wait_ge(at_lo_ready, at_count(l, "s2", 1))
                proj(t + 19, l, 11, 4, True, True)
                proj(t + 20, l, 12, 4, True, True, lambda: merged_t(l, 0))
                pe.wait_ge(at_lo_ready, at_count(l, "m", 2))
                proj(t + 21, l, 13, 0, True, False, lambda: merged_t(l, 1))
                pe.wait_ge(at_lo_ready, at_count(l, "m", 3))
                proj(t + 22, l, 13, 4, False, True)
                proj(t + 23, l, 14, 0, True, False)
                norm_t(l, "h", 0)
                proj(t + 24, l, 14, 4, False, True)

            pe.wait_ge(loads, 32)

            mixer(0)

            def up2(c, a_tile, a_slot, b_tile, b_slot):
                pe.wait_ge(lo_ready, a_tile + 1)
                if c is not None:
                    pe.wait_ge(h_done, c)
                else:
                    pe.wait_ge(at_lo_ready, at_count(0, "h", 2))
                for th in range(TH):
                    if c is None:
                        if th == 1:
                            norm_t(0, "h", 1)
                        pe.wait_ge(x_added, 3 + th)
                    for k in range(4):
                        m = three(PJ[th][:, :], at_hi[:, k, th * P:(th + 1) * P], at_lo[:, k, th * P:(th + 1) * P],
                                  hi[:, a_slot, k * 512:(k + 1) * 512], lo[:, a_slot, k * 512:(k + 1) * 512], k == 0, False)
                m.then_inc(tile_used, 1)
                if c is not None:
                    hidden_t2(c)
                else:
                    pe.wait_ge(at_lo_ready, at_count(0, "h", 3))
                pe.wait_ge(lo_ready, b_tile + 1)
                for th in range(TH):
                    for k in range(4):
                        m = three(PJ[th][:, :], at_hi[:, 4 + k, th * P:(th + 1) * P], at_lo[:, 4 + k, th * P:(th + 1) * P],
                                  hi[:, b_slot, k * 512:(k + 1) * 512], lo[:, b_slot, k * 512:(k + 1) * 512], False, k == 3)
                    if th == 0:
                        m.then_inc(h_full, 1)
                m.then_inc(tile_used, 1)

            def hidden_t2(done):
                pe.wait_ge(h_done, done)
                for th in range(TH):
                    for f in range(2):
                        m = pe.transpose(TR[0][:, f * SEQ + th * P:f * SEQ + (th + 1) * P],
                                         v_flat[:, (2 + th) * FC + f * P:(2 + th) * FC + (f + 1) * P], ident)
                m.then_inc(ht_tr, 1)

            def down2(tile, slot, parts, start, stop):
                pe.wait_ge(lo_ready, tile + 1)
                pe.wait_ge(ht_lo_ready, parts)
                for n in range(2):
                    for th in range(TH):
                        for f in range(2):
                            m = three(banks[2 + 2 * th + n][:, :], ht_hi[:, f, th * P:(th + 1) * P], ht_lo[:, f, th * P:(th + 1) * P],
                                      hi[:, slot, f * D + n * 512:f * D + (n + 1) * 512],
                                      lo[:, slot, f * D + n * 512:f * D + (n + 1) * 512], start and f == 0, stop and f == 1)
                    if stop and n == 0:
                        m.then_inc(y_half, 1)
                m.then_inc(tile_used, 1)

            t = T_FFN0
            up2(None, t, t % 3, t + 1, (t + 1) % 3)
            up2(2, t + 2, (t + 2) % 3, t + 3, t % 3)
            down2(t + 4, (t + 4) % 3, 1, True, False)
            with pe.Fori(1, NCH - 1) as c:
                up2(c * 2 + 2, c * 3 + (t + 2), (t + 2) % 3, c * 3 + (t + 3), t % 3)
                down2(c * 3 + (t + 4), (t + 4) % 3, c + 1, False, False)
            hidden_t2(2 * NCH)
            down2(T_MIX1 - 1, (T_MIX1 - 1) % 3, NCH, False, True)
            mixer(1)

            norm_t(1, "h", 1)
            pe.wait_ge(at_lo_ready, at_count(1, "h", 3))
            pe.wait_ge(router_ready, 1)
            bank = open_turn("router")
            for th in range(TH):
                for k in range(KD):
                    for i, a in enumerate((at_hi, at_lo)):
                        m = mm(bank[:, th * 16:(th + 1) * 16], a[:, k, th * P:(th + 1) * P], router_parts[:, k, :],
                               k == 0 and i == 0, k == KD - 1 and i == 1)
            m.then_inc(tr_full, 1)
            pe.wait_ge(sel_ready, 1)
            bank = open_turn("pos")
            tri, ones = cst[:, C_TRI:C_TRI + P], cst[:, C_ONE:C_ONE + P]
            mm(bank[:, 0:8], tri, sel[:, 0, :], True, True)
            mm(bank[:, 8:16], tri, sel[:, 1, :], True, False)
            mm(bank[:, 8:16], ones, sel[:, 0, :], False, True)
            mm(bank[:, 16:24], ones, sel[:, 0, :], True, False)
            mm(bank[:, 16:24], ones, sel[:, 1, :], False, True).then_inc(tr_full, 1)

            def gather():
                for k in range(KD):
                    for th in range(TH):
                        m = mm(banks[4 + k // 4][:, (k % 4) * P:(k % 4 + 1) * P], xn[:, th, k * P:(k + 1) * P],
                               place[:, th, :], th == 0, th == 1)
                m.then_inc(xe_full, 1)

            def up(b, c, half):
                j = 3 * c - 1 + half if c > 0 else half
                s = (T_MOE + j) % SPLITS
                pe.wait_ge(lo_ready, b * FFN_TILES + (T_MOE + j + 1))
                if half == 0 and c == NCH - 1:
                    pe.wait_ge(gt_ready, b + 1)
                if half == 0 and c == NCH:
                    pe.wait_ge(xe_lo_ready, b + 2)
                for k in range(4):
                    m = three(h_bank(c)[:, :], at_hi[:, 4 * half + k, 0:P], at_lo[:, 4 * half + k, 0:P],
                              hi[:, s, k * 512:(k + 1) * 512], lo[:, s, k * 512:(k + 1) * 512],
                              half == 0 and k == 0, half == 1 and k == 3)
                m.then_inc(tile_used, 1)

            def hidden_t(b, c):
                pe.wait_ge(h_done, b * NCH + (2 * NCH + c + 1))
                if c == 1:
                    pe.wait_ge(x_added, b * 4 + 12)
                for f in range(2):
                    m = pe.transpose(TR[0][:, f * P:(f + 1) * P], v_flat[:, FC + f * P:FC + (f + 1) * P], ident)
                m.then_inc(ht_tr, 1)

            def down(b, c, j):
                s = (T_MOE + j) % SPLITS
                pe.wait_ge(lo_ready, b * FFN_TILES + (T_MOE + j + 1))
                pe.wait_ge(ht_lo_ready, b * NCH + (NCH + c + 1))
                if c == NCH:
                    pe.wait_ge(ye_ready, b + 1)
                for f in range(2):
                    for n in range(2):
                        m = three(banks[2 + n][:, :], ht_hi[:, f, 0:P], ht_lo[:, f, 0:P],
                                  hi[:, s, f * D + n * 512:f * D + (n + 1) * 512],
                                  lo[:, s, f * D + n * 512:f * D + (n + 1) * 512],
                                  c % NCH == 0 and f == 0, c == NCH - 1 and f == 1)
                m.then_inc(tile_used, 1)

            def combine(b):
                pe.wait_ge(gt_ready, b + 1)
                pe.wait_ge(ye_ready, b + 1)
                for i, bank in enumerate(comb_banks):
                    n, th = i // 2, i % 2
                    mm(bank[:, :], ht_hi[:, th, P:2 * P], at_hi[:, 4 * n:4 * n + 4, P:2 * P], True, False)
                    mm(bank[:, :], ht_hi[:, th, P:2 * P], at_lo[:, 4 * n:4 * n + 4, P:2 * P], False, True).then_inc(comb_full, 1)

            def expert_step(b, c, final=False):
                ahead = not (final and c == NCH - 1)
                if ahead:
                    up(b, c + 1, 0)
                hidden_t(b, c)
                if ahead:
                    up(b, c + 1, 1)
                down(b, c, FFN_TILES - 1 if final and c == NCH - 1 else 3 * c + 4)
                if c == 3:
                    for th in range(TH):
                        pe.transpose(TR[1][:, th * P:(th + 1) * P], place[:, th, :], ident)
                    for th in range(TH):
                        m = mm(TR[1][:, TH * P:TH * P + 1], place[:, th, :], column[:, 1, th:th + 1], th == 0, th == 1)
                    m.then_inc(pg_full, 1)
                if c == 8 and not final:
                    pe.wait_ge(place_ready, b + 2)
                    gather()
                if c == NCH:
                    combine(b)

            pe.wait_ge(place_ready, 1)
            gather()
            pe.wait_ge(xe_lo_ready, 1)
            for half in range(2):
                up(0, 0, half)
            expert_step(0, 0)
            last = pe.value_load(table[0:1, 0:1], min_val=NE - 1, max_val=MAXB - 1)
            with pe.Fori(0, last) as b:
                for c in range(1, NCH + 1):
                    expert_step(b, c)
            for c in range(1, NCH):
                expert_step(last, c, True)
            combine(last)

        @block.scalar
        def _(act):
            own = Order(act, act_own)

            def split(t, full_sem, full, src, slot, after=True):
                act.wait_ge(full_sem, full)
                if after:
                    act.wait_ge(tile_used, t - (SPLITS - 1))
                act.activation(hi[:, slot, :], src, ACT.Copy).then_inc(hi_ready, 1)

            def split_moe(b, j):
                slot = moe_slot(j)
                split(b * FFN_TILES + (T_MOE + j), raw_full[slot], moe_full_value(j, b), raw[:, slot, :], (T_MOE + j) % SPLITS)

            def split_static(t):
                s = raw_slot(t)
                split(t, raw_full[s], 32 * (raw_uses(s, t) + 1), raw[:, s, :], t % SPLITS, t >= SPLITS)

            def at_part(l, kind, g, k0, kn, c0, scale=1.0):
                bank = wait_turn(act, (l, kind, g))
                act.activation(at_hi[:, k0:k0 + kn, c0:c0 + P], bank[:, 0:kn * P].rearrange("p (k c) -> p k c", k=kn),
                               ACT.Copy, scale=scale).then_inc(at_hi_ready, 1)

            def squares(n, added=None):
                for th in range(TH):
                    if added is not None:
                        act.wait_ge(x_added, added + th + 1)
                    half = slice(n * 512, (n + 1) * 512)
                    m = act.activation((u_flat, v_flat)[th][:, half], xres[:, th, half], ACT.Square, accum_out=col((SS, SS2)[n] + th))
                if n == 1:
                    m.then_inc(sq_ready, 1)

            def roots(stage):
                act.wait_ge(var_ready, stage + 1)
                act.activation(col(RT, 2), col(VAR, 2), ACT.Sqrt).then_inc(root_ready, 1)

            def inverse(th):
                return col(RI + th)

            def load_gain(src):
                act.dma_start(a_flat, src.partition_broadcast(P)).then_inc(gain_in, 16)

            def evac(name, dst, bank_cols=512):
                bank = wait_turn(act, name)
                act.activation(dst, bank[:, 0:bank_cols], ACT.Copy).then_inc(tr_free[TURN[name] % 2], 1)

            def from_pj(l, i, tile, dst, func, scale=1.0, view=None):
                for th in range(TH):
                    if th == 0:
                        act.wait_ge(pj0_full, use(l, i) + 1)
                    else:
                        act.wait_ge(tile_used, tile + 1)
                    src = PJ[th][:, :] if view is None else view(PJ[th][:, :])
                    factor = scale(th) if callable(scale) else scale
                    act.activation(dst(th), src, func, scale=factor).then_inc(pj_free[th], 1)

            def probs_of(l, j):
                act.wait_ge(max_ready, 8 * l + j + 1)
                for c in range(2):
                    m = act.activation(probs[:, c, :], TR[TURN[(l, "sc", j)] % 2][:, c * SEQ:(c + 1) * SEQ], ACT.Exp, bias=col(NB + c),
                                       scale=HD ** -0.5, accum_out=col(RS + c))
                m.then_inc(exp_ready, 1)

            def scale_second(l, j):
                act.wait_ge(factor_ready, 8 * l + j + 1)
                act.activation(probs[:, 1, :], probs[:, 1, :], ACT.Copy, scale=col(C1)).then_inc(second_scaled, 1)

            def head_back(l, j):
                name = (l, "o", j)
                bank = TR[TURN[name] % 2]
                act.wait_ge(wt_tr, 8 * l + j + 1)
                act.activation(wdiff_t, bank[:, 0:2 * P].rearrange("p (t q) -> p t q", t=2), ACT.Copy).then_inc(wt_ready, 1)
                wait_turn(act, name)
                h, th = j // 2, j % 2
                own.step(act.activation(areg[:, th, h * P:(h + 1) * P], bank[:, 2 * P:3 * P], ACT.Copy))
                act.activation(bank[:, 2 * P:3 * P], bank[:, 2 * P:3 * P], ACT.Square,
                               accum_out=col(AS + j)).then_inc(tr_free[TURN[name] % 2], 1)

            def quarters(l, kind, n, scale=1.0):
                for th in range(TH):
                    at_part(l, kind, 2 * th + n, 4 * n, 4, th * P, scale)

            def lay_b(l, d):
                if l == 0:
                    act.wait_ge(bzero_ready, 2)
                act.wait_ge(mats_ready, 2 * l + 1)
                for kind, src in enumerate((bbar, babar)):
                    t = (1 - d) if kind == 0 else d
                    for g in range(2):
                        for r in range(2):
                            rows = slice(64 * g, 64 * (g + 1))
                            m = act.activation(bpre[rows, d, r, :, :, t, g, :].rearrange("p b q h -> p (b q) h"),
                                               src[rows, r, d * PAIRS:(d + 1) * PAIRS, :], ACT.Copy)
                m.then_inc(b_laid, 1)

            def lay_c(l):
                act.wait_ge(mats_ready, 2 * l + 2)
                for kind, src in enumerate((ctr, cabar)):
                    for r in range(2):
                        for g in range(2):
                            rows = slice(64 * g, 64 * (g + 1))
                            m = act.activation(cblk[rows, kind, r, :, :, g, :].rearrange("p d q h -> p (d q) h"),
                                               src[rows, r, :, :], ACT.Copy, scale=1.0 if r == 0 else -1.0)
                m.then_inc(blocks_ready, 1)

            def mixer(l):
                t = T_MIX[l]
                if l > 0:
                    squares(0, 4)
                quarters(l, "x", 0)
                if l == 0:
                    split_static(0)
                    split_static(1)
                else:
                    squares(1, 6)
                quarters(l, "x", 1)
                if l == 0:
                    squares(0)
                    squares(1)
                split_static(t + 2)
                roots(2 * l)
                split_static(t + 3)
                for g in range(4):
                    bank = wait_turn(act, (l, "ct", g))
                    r, d = g // 2, g % 2
                    for odd in range(2):
                        rows = slice(64 * odd, 64 * (odd + 1))
                        m = act.activation(ctr[rows, r, d * PAIRS:(d + 1) * PAIRS, :],
                                           bank[rows, :].rearrange("p (j g h) -> p j g h", g=2, h=GC)[:, :, odd, :], ACT.Copy)
                    m.then_inc(tr_free[TURN[(l, "ct", g)] % 2], 1)
                act.wait_ge(inv_ready, 2 * l + 1)
                from_pj(l, 0, t + 1, lambda th: u_rows[:, :, th, :], ACT.Copy, inverse,
                        view=lambda b: b.rearrange("p (q c) -> p q c", q=PAIRS))
                split_static(t + 4)
                split_static(t + 5)
                for g in range(2):
                    evac((l, "u", g), ut2[:, 4 * g:4 * g + 4, :].rearrange("p b c -> p (b c)"))
                split_static(t + 6)
                if l == 0:
                    for d in range(2):
                        lay_b(0, d)
                split_static(t + 7)
                for th in range(TH):
                    evac_heads(l, "q", th, q_t)
                split_static(t + 8)
                lay_c(l)
                split_static(t + 9)
                from_pj(l, 3, t + 7, lambda th: vreg[:, th, :], ACT.Copy, inverse)
                for th in range(TH):
                    evac_heads(l, "k", th, k_t)
                bflat = area(0, 4096)
                for g in range(0, 8, 2):
                    evac((l, "b", g), bflat[:, g * 512:(g + 1) * 512])
                for s in range(8):
                    split_static(t + 10 + s)
                    probs_of(l, s)
                    if s % 2 == 1:
                        i = 4 + s // 2
                        g, n = (i - 4) // 2, (i - 4) % 2
                        from_pj(l, i, t + 8 + s, lambda th: gates[:, th, g, n * 512:(n + 1) * 512], ACT.Tanh,
                                lambda th: col(RH + th))
                    if s > 0:
                        head_back(l, s - 1)
                    scale_second(l, s)
                head_back(l, 7)
                act.wait_ge(avar_ready, l + 1)
                act.activation(col(AR, 8), col(AV, 8), ACT.Sqrt).then_inc(aroot_ready, 1)
                act.wait_ge(y_done, PAIRS * (l + 1))
                for th in range(TH):
                    act.activation(s_t[:, :, th * P:(th + 1) * P], PY[th][:, :].rearrange("p (k s) -> p k s", k=4),
                                   ACT.Gelu).then_inc(s_ready, 1)
                for th in range(TH):
                    act.wait_ge(s_ready, 2 * l + th + 1)
                    act.activation(at_hi[:, 4:8, th * P:(th + 1) * P], s_t[:, :, th * P:(th + 1) * P],
                                   ACT.Copy).then_inc(at_hi_ready, 1)
                split_static(t + 18)
                for th in range(TH):
                    at_part(l, "a", th, 0, 4, th * P)
                load_gain(norm_ffn[l, :])
                from_pj(l, 8, t + 16, lambda th: s_gated[:, th, :], ACT.Tanh, scale=0.5)
                split_static(t + 19)
                split_static(t + 20)
                for th in range(TH):
                    at_part(l, "s2", th, 4, 4, th * P, scale=0.5)
                split_static(t + 21)
                quarters(l, "m", 0, 0.5)
                split_static(t + 22)
                quarters(l, "m", 1, 0.5)
                split_static(t + 23)
                split_static(t + 24)
                if l == 1:
                    act.wait_ge(at_lo_ready, at_count(l, "m", 3))
                    act.dma_start(router, moe_router[0, :, :].rearrange("(k p) e -> p k e", p=P)).then_inc(router_in, 16)
                squares(0, 8 * l)

                def ahead(i):
                    if l == 0:
                        split_static(t + 25 + i)
                    else:
                        split_moe(0, i)
                ahead(0)
                quarters(l, "h", 0)
                ahead(1)
                if l == 1:
                    act.wait_ge(router_in, 16)
                    act.activation(router_parts[:, :, 0:NE], router, ACT.Copy).then_inc(router_hi_ready, 1)
                squares(1, 8 * l + 2)
                quarters(l, "h", 1)
                roots(2 * l + 1)
                load_gain(norm_mix[1, :] if l == 0 else norm_final)

            def evac_heads(l, kind, th, dst):
                bank = wait_turn(act, (l, kind, th))
                act.activation(dst[:, :, th * P:(th + 1) * P], bank[:, :].rearrange("p (h s) -> p h s", h=HEADS),
                               ACT.Copy).then_inc(tr_free[TURN[(l, kind, th)] % 2], 1)

            act.dma_start(row(R_LR), ssm_lam_re.rearrange("l d (q g) s -> (l d q) (g s)", g=2)).then_inc(rows_in, 16)
            act.dma_start(row(R_LI), ssm_lam_im.rearrange("l d (q g) s -> (l d q) (g s)", g=2)).then_inc(rows_in, 16)
            act.dma_start(row(R_DT)[:, 0:2], ssm_log_dt.rearrange("l d (q g) -> (l d q) g", g=2)).then_inc(rows_in, 16)
            load_gain(norm_mix[0, :])
            act.dma_start(gflat[:, 4 * P:8 * P], attn_lambda.rearrange("l a c -> (l a c)").partition_broadcast(P)).then_inc(lam_in, 16)
            act.dma_start(subln[:, :, :].rearrange("p l c -> p (l c)"),
                          attn_subln.rearrange("l c -> (l c)").partition_broadcast(P)).then_inc(lam_in, 16)
            act.wait_ge(rows_in, 48)
            act.activation(row(R_EDT)[:, 0:2], row(R_DT)[:, 0:2], ACT.Exp).then_inc(act_par, 1)
            act.wait_ge(dve_rows, 1)
            act.activation(row(R_er), row(R_lr), ACT.Exp)
            act.wait_ge(lam_ready, 1)
            act.activation(col(LEXP, 4), col(LSUM, 4), ACT.Exp).then_inc(lam_exp, 1)
            act.activation(row(R_sn), row(R_red), ACT.Sin)
            act.activation(row(R_sh), row(R_red), ACT.Sin, scale=0.5).then_inc(act_par, 1)
            act.wait_ge(loads, 32)
            mixer(0)

            def silu2(full0, used1):
                for th in range(TH):
                    act.wait_ge(h_full if th == 0 else tile_used, full0 if th == 0 else used1)
                    act.activation(v_flat[:, th * FC:(th + 1) * FC], PJ[th][:, 0:FC], ACT.Silu,
                                   scale=inverse(th)).then_inc(g_ready, 1)

            def hidden_hi(n, cols):
                act.wait_ge(ht_tr, n)
                act.activation(ht_hi[:, :, 0:cols], TR[0][:, 0:2 * cols].rearrange("p (f s) -> p f s", f=2),
                               ACT.Copy).then_inc(ht_hi_ready, 1)

            t = T_FFN0

            def ffn_turn(c, used):
                def split_turn(i):
                    s = raw_slot(t + 2 + i)
                    split(c * 3 + (t + 2 + i), raw_full[s], c * 32 + 32 * (raw_uses(s, t + 2 + i) + 1), raw[:, s, :], (t + 2 + i) % 3)
                split_turn(0)
                silu2(c + 1, used)
                split_turn(1)
                split_turn(2)
                hidden_hi(c + 1, SEQ)
            act.wait_ge(inv_ready, 2)
            ffn_turn(0, t + 2)
            with act.Fori(1, NCH - 1) as c:
                ffn_turn(c, c * 3 + (t + 1))
            lay_b(1, 0)
            silu2(NCH, t + 3 * (NCH - 1) + 1)
            split_static(T_MIX1 - 1)
            lay_b(1, 1)
            hidden_hi(NCH, SEQ)
            split_static(T_MIX1)
            split_static(T_MIX1 + 1)
            mixer(1)

            act.wait_ge(sel_early, 1)
            act.activation(r_exp, r_diff, ACT.Exp).then_inc(gate_exp, 1)

            def gathered(n):
                act.wait_ge(xe_full, n)
                for g in range(2):
                    m = act.activation(at_hi[:, 4 * g:4 * g + 4, 0:P], banks[4 + g][:, :].rearrange("p (k c) -> p k c", k=4), ACT.Copy)
                m.then_inc(xe_hi_ready, 1)

            def silu(b, c):
                act.wait_ge(tile_used, b * FFN_TILES + (T_MOE + (3 * c if c > 0 else 1) + 1))
                act.activation(v_flat[:, 0:FC], h_bank(c)[:, 0:FC], ACT.Silu).then_inc(g_ready, 1)

            def result_hi(b, used):
                act.wait_ge(tile_used, used)
                for n in range(2):
                    m = act.activation(at_hi[:, 4 * n:4 * n + 4, P:2 * P], PY[n][:, :].rearrange("p (k c) -> p k c", k=4),
                                       ACT.Copy, scale=place_gate)
                m.then_inc(ye_hi_ready, 1)

            def expert_step(b, c, final=False):
                if c == NCH:
                    result_hi(b, b * FFN_TILES + (T_MOE + FFN_TILES + 2))
                if c == 4:
                    act.wait_ge(pg_full, b + 1)
                    act.activation(ht_hi[:, :, P:2 * P], TR[1][:, 0:SEQ].rearrange("p (t c) -> p t c", t=TH), ACT.Copy)
                    act.activation(place_gate, TR[1][:, SEQ:SEQ + 1], ACT.Copy).then_inc(gt_ready, 1)
                if c >= 0:
                    split_moe(b, FFN_TILES - 1 if final and c == NCH - 1 else 3 * c + 4)
                    hidden_hi(b * NCH + (NCH + c + 1), P)
                if not (final and c + 2 >= NCH):
                    split_moe(b, 3 * c + 5)
                if not (final and c + 1 >= NCH):
                    silu(b, c + 1)
                if c == NCH - 2 and not final:
                    gathered(b + 2)
                if not (final and c + 2 >= NCH):
                    split_moe(b, 3 * c + 6)

            gathered(1)
            expert_step(0, -1)
            expert_step(0, 0)
            act.wait_ge(routed, 1)
            last = act.value_load(table[0:1, 0:1], min_val=NE - 1, max_val=MAXB - 1)
            with act.Fori(0, last) as b:
                for c in range(1, NCH + 1):
                    expert_step(b, c)
            for c in range(1, NCH):
                expert_step(last, c, True)
            result_hi(last, last * FFN_TILES + (T_MOE + FFN_TILES))
            for n in range(2):
                squares(n, last * 4 + (12 + 2 * n))
            roots(4)

        @block.vector
        def _(dve):
            own = Order(dve, dve_own)
            tt, ts, stt = dve.tensor_tensor, dve.tensor_scalar, dve.scalar_tensor_tensor

            def split(t, slot, src):
                dve.wait_ge(hi_ready, t + 1)
                tt(lo[:, slot, :], src, hi[:, slot, :].bitcast(f32), SUB).then_inc(lo_ready, 1)

            def split_moe(b, j):
                split(b * FFN_TILES + (T_MOE + j), (T_MOE + j) % SPLITS, raw[:, moe_slot(j), :])

            def split_static(t):
                split(t, t % SPLITS, raw[:, raw_slot(t), :])

            def at_part(l, kind, g, k0, kn, c0, scale=None):
                bank = TR[TURN[(l, kind, g)] % 2]
                dve.wait_ge(at_hi_ready, at_count(l, kind, g))
                src = bank[:, 0:kn * P].rearrange("p (k c) -> p k c", k=kn)
                dst, first = at_lo[:, k0:k0 + kn, c0:c0 + P], at_hi[:, k0:k0 + kn, c0:c0 + P].bitcast(f32)
                if scale is None:
                    tt(dst, src, first, SUB).then_inc(at_lo_ready, 1)
                else:
                    stt(dst, src, scale, first, MUL, SUB).then_inc(at_lo_ready, 1)

            def gained(stage, n, th):
                dve.wait_ge(gain_in, 16 * (stage + 1))
                half = slice(n * 512, (n + 1) * 512)
                tt(xn[:, th, half], xres[:, th, half], gain[:, half], MUL).then_inc(xn_ready, 1)

            def inverses(stage):
                dve.wait_ge(sq_ready, stage + 1)
                tt(col(SS, 2), col(SS, 2), col(SS2, 2), ADD).then_inc(sum_ready, 1)
                dve.wait_ge(sum_ready, stage + 1)
                ts(col(VAR, 2), col(SS, 2), 1.0 / D, EPS, MUL, ADD).then_inc(var_ready, 1)
                dve.wait_ge(root_ready, stage + 1)
                dve.reciprocal(col(RI, 2), col(RT, 2)).then_inc(whole_inv, 1)
                dve.wait_ge(whole_inv, stage + 1)
                ts(col(RH, 2), col(RI, 2), 0.5, None, MUL).then_inc(inv_ready, 1)

            def quarters(l, kind, n, scale=None):
                for th in range(TH):
                    at_part(l, kind, 2 * th + n, 4 * n, 4, th * P, scale)

            def rotary(l, i, tile, dst):
                cos_t, sin_t = (cst[:, c:c + 128].rearrange("p (t c) -> p t c", t=2) for c in (C_COS, C_SIN))
                for th in range(TH):
                    if th == 0:
                        dve.wait_ge(pj0_full, use(l, i) + 1)
                    else:
                        dve.wait_ge(tile_used, tile + 1)
                    src = PJ[th][:, :]
                    own.step(stt(a_flat[:, 0:512].rearrange("p (h c) -> p h c", c=HD), src.rearrange("p (h c) -> p h c", c=HD),
                                 col(RI + th), cos_t[:, th, :].unsqueeze(1).broadcast_to([P, 8, HD]), MUL, MUL))
                    for a in range(2):
                        m = stt(a_flat[:, 512:1024].rearrange("p (h a c) -> p h a c", a=2, c=32)[:, :, a, :],
                                src.rearrange("p (h a c) -> p h a c", a=2, c=32)[:, :, 1 - a, :], col(RI + th),
                                sin_t[:, th, 32 * a:32 * (a + 1)].unsqueeze(1).broadcast_to([P, 8, 32]), MUL, MUL)
                    m.then_inc(pj_free[th], 1)
                    dve.wait_ge(pj_free[th], pj_read(l, i))
                    tt(dst[:, th, :], a_flat[:, 0:512], a_flat[:, 512:1024], ADD).then_inc(rot_ready, 1)
                    dve.wait_ge(rot_ready, 4 * l + (0 if i == 1 else 2) + th + 1)

            def phases(l, q):
                n = 16 * l + q
                w = wtab[q % 2]
                dve.wait_ge(php_ready, n + 1)
                tt(w[:, 0, :], w[:, 0, :], php[0], SUB)
                tt(w[:, 1, :], php[1], php[2], ADD).then_inc(wtab_ready, 1)

            def s5_scan(l, q):
                n = 16 * l + q
                v = PV[q % 2][:, :].rearrange("p (r c) -> p r c", r=2)
                w = wtab[q % 2]
                dve.wait_ge(pv_full, n + 1)
                dve.wait_ge(wtab_ready, n + 1)
                tt(rot1, v, w[:, 0:1, :].broadcast_to([P, 2, 256]), MUL)
                tt(rot2, v[:, ::-1, :], w[:, 1:2, :].broadcast_to([P, 2, 256]), MUL).then_inc(pv_free, 1)
                dve.wait_ge(pv_free, n + 1)
                tt(rot1[:, 0, :], rot1[:, 0, :], rot2[:, 0, :], ADD)
                own.step(tt(rot1[:, 1, :], rot1[:, 1, :], rot2[:, 1, :], SUB))
                if n > 0:
                    dve.wait_ge(zs_used, n)
                for r in range(2):
                    for d in range(2):
                        half = slice(d * P, (d + 1) * P)
                        j = 32 * l + d * PAIRS + q
                        m = dve.tensor_tensor_scan(zs[:, r, half], par[:, RAD2, j:j + 1].broadcast_to([P, P]),
                                                   rot1[:, r, half], 0.0, MUL, ADD)
                m.then_inc(zs_ready, 1)

            def row_max(l, j):
                bank = wait_turn(dve, (l, "sc", j))
                own.step(dve.tensor_reduce(col(MX, 2), bank[:, :].rearrange("p (c s) -> p c s", c=2), AX.X, ALU.max))
                ts(col(NB, 2), col(MX, 2), -(HD ** -0.5), None, MUL).then_inc(max_ready, 1)

            def softmax_factors(l, j):
                dve.wait_ge(exp_ready, 8 * l + j + 1)
                dve.reciprocal(col(RR, 2), col(RS, 2)).then_inc(tr_free[TURN[(l, "sc", j)] % 2], 1)
                wait_read(dve, (l, "sc", j))
                tt(col(C1), col(RR + 1), col(NLAM + l), MUL).then_inc(factor_ready, 1)

            def weights(l, j):
                dve.wait_ge(second_scaled, 8 * l + j + 1)
                if 8 * l + j > 0:
                    dve.wait_ge(wt_tr, 8 * l + j)
                stt(wdiff, probs[:, 0, :], col(RR), probs[:, 1, :], MUL, ADD).then_inc(w_ready, 1)

            def gated(l, i, tile, g, n):
                for th in range(TH):
                    if th == 0:
                        dve.wait_ge(pj0_full, use(l, i) + 1)
                    else:
                        dve.wait_ge(tile_used, tile + 1)
                    z = gates[:, th, g, n * 512:(n + 1) * 512]
                    stt(z, z, 1.0, PJ[th][:, :], ADD, MUL).then_inc(pj_free[th], 1)
                    if g == 1:
                        dve.wait_ge(pj_free[th], pj_read(l, i))
                        m = gates[:, th, 0, n * 512:(n + 1) * 512]
                        tt(m, m, z, ADD).then_inc(m_ready, 1)

            def add_out(l, i, tile, n):
                for th in range(TH):
                    if th == 0:
                        dve.wait_ge(pj0_full, use(l, i) + 1)
                    else:
                        dve.wait_ge(tile_used, tile + 1)
                    z = xres[:, th, n * 512:(n + 1) * 512]
                    tt(z, z, PJ[th][:, :], ADD).then_inc(x_added, 1)
                    dve.wait_ge(x_added, 8 * l + 2 * n + th + 1)
                    gained(2 * l + 1, n, th)

            def mixer(l):
                t = T_MIX[l]
                if l > 0:
                    for n in range(2):
                        add_ffn(n)
                        quarters(l, "x", n)
                split_static(t + 2)
                inverses(2 * l)
                for s in range(1, 4):
                    split_static(t + s + 2)
                    if l == 0 and s > 1:
                        if s == 2:
                            wait_read(dve, "par")
                        dve.memset(gflat[:, (s - 2) * 2048:(s - 1) * 2048], 0.0).then_inc(bzero_ready, 1)
                rotary(l, 1, t + 3, qk[:, 0, :, :])
                split_static(t + 6)
                split_static(t + 7)
                rotary(l, 2, t + 5, qk[:, 1, :, :])
                split_static(t + 8)
                split_static(t + 9)
                bflat = area(0, 4096)
                for g in range(1, 8, 2):
                    bank = wait_turn(dve, (l, "b", g))
                    dve.tensor_copy(bflat[:, g * 512:(g + 1) * 512], bank[:, :]).then_inc(tr_free[TURN[(l, "b", g)] % 2], 1)
                dve.wait_ge(dskip_in, 16 * 8)
                own.step(tt(cbm, cst[:, C_PAT:C_PAT + 32].unsqueeze(1).broadcast_to([P, 8, 32]),
                            dskip[:, l, :].unsqueeze(2).broadcast_to([P, 8, 32]), MUL))
                bank = wait_turn(dve, (l, "cb", 0))
                tt(cbm, cbm, bank[:, 0:256].rearrange("p (b c) -> p b c", b=8), ADD).then_inc(tr_free[TURN[(l, "cb", 0)] % 2], 1)
                phases(l, 0)
                for s in range(8):
                    split_static(t + 10 + s)
                    row_max(l, s)
                    s5_scan(l, 2 * s)
                    phases(l, 2 * s + 1)
                    softmax_factors(l, s)
                    s5_scan(l, 2 * s + 1)
                    weights(l, s)
                    if s < 7:
                        phases(l, 2 * s + 2)
                wait_read(dve, (l, "o", 6))
                wait_read(dve, (l, "o", 7))
                ts(col(AV, 8), col(AS, 8), 1.0 / P, EPS, MUL, ADD).then_inc(avar_ready, 1)
                dve.wait_ge(aroot_ready, l + 1)
                own.step(dve.reciprocal(col(AI, 8), col(AR, 8)))
                for th in range(TH):
                    for h in range(HEADS):
                        z = areg[:, th, h * P:(h + 1) * P]
                        m = stt(z, z, col(AI + 2 * h + th), subln[:, l, :], MUL, MUL)
                    m.then_inc(a_ready, 1)
                    if th == 0:
                        for h in range(TH):
                            half = slice(h * P, (h + 1) * P)
                            dve.wait_ge(at_hi_ready, at_count(l, "sa", h))
                            tt(at_lo[:, 4:8, half], s_t[:, :, half], at_hi[:, 4:8, half].bitcast(f32), SUB).then_inc(at_lo_ready, 1)
                split_static(t + 18)
                for th in range(TH):
                    at_part(l, "a", th, 0, 4, th * P)
                for th in range(TH):
                    dve.wait_ge(pj_free[th], pj_read(l, 8))
                    bank = wait_turn(dve, (l, "s", th))
                    stt(s_gated[:, th, :], s_gated[:, th, :], 1.0, bank[:, :], ADD,
                        MUL).then_inc(tr_free[TURN[(l, "s", th)] % 2], 1)
                split_static(t + 19)
                gated(l, 9, t + 17, 0, 0)
                split_static(t + 20)
                for th in range(TH):
                    at_part(l, "s2", th, 4, 4, th * P, scale=0.5)
                gated(l, 10, t + 18, 0, 1)
                split_static(t + 21)
                gated(l, 11, t + 19, 1, 0)
                quarters(l, "m", 0, 0.5)
                gated(l, 12, t + 20, 1, 1)
                split_static(t + 22)
                quarters(l, "m", 1, 0.5)
                split_static(t + 23)
                split_static(t + 24)
                add_out(l, 13, t + 22, 0)

                def ahead(i):
                    if l == 0:
                        split_static(t + 25 + i)
                    else:
                        split_moe(0, i)
                ahead(0)
                quarters(l, "h", 0)
                ahead(1)
                if l == 1:
                    dve.wait_ge(router_hi_ready, 1)
                    tt(router_parts[:, :, NE:2 * NE], router, router_parts[:, :, 0:NE].bitcast(f32), SUB).then_inc(router_ready, 1)
                add_out(l, 14, t + 24, 1)
                quarters(l, "h", 1)
                inverses(2 * l + 1)

            def add_ffn(n):
                dve.wait_ge(y_half if n == 0 else tile_used, 1 if n == 0 else T_MIX1)
                for th in range(TH):
                    z = xres[:, th, n * 512:(n + 1) * 512]
                    tt(z, z, banks[2 + 2 * th + n][:, :], ADD).then_inc(x_added, 1)
                    dve.wait_ge(x_added, 4 + 2 * n + th + 1)
                    gained(2, n, th)

            TWO_PI_A = 6.28125
            TWO_PI_B = round((2 * math.pi - TWO_PI_A) * 2 ** 20) / 2 ** 20
            TWO_PI_C = 2 * math.pi - TWO_PI_A - TWO_PI_B
            MAGIC = 1.5 * 2.0 ** 23
            dve.wait_ge(rows_in, 48)
            dve.wait_ge(act_par, 1)
            dt = row(R_EDT)[:, 0:2].unsqueeze(2).broadcast_to([64, 2, 64])

            def halves(ap):
                return ap.rearrange("p (g s) -> p g s", g=2)
            tt(halves(row(R_lr)), halves(row(R_LR)), dt, MUL).then_inc(dve_rows, 1)
            own.step(tt(halves(row(R_li)), halves(row(R_LI)), dt, MUL))
            own.step(ts(row(R_k), row(R_li), 1.0 / (2 * math.pi), MAGIC, MUL, ADD))
            own.step(ts(row(R_k), row(R_k), -MAGIC, None, ADD))
            own.step(stt(row(R_red), row(R_k), -TWO_PI_A, row(R_li), MUL, ADD))
            own.step(stt(row(R_red), row(R_k), -TWO_PI_B, row(R_red), MUL, ADD))
            own.step(stt(row(R_red), row(R_k), -TWO_PI_C, row(R_red), MUL, ADD))
            own.step(ts(row(R_red), row(R_red), 3.1415925, -3.1415925, ALU.min, ALU.max))
            dve.wait_ge(lam_in, 32)
            own.step(tt(lamp.rearrange("p (l a) c -> p l a c", l=2), lamv[:, :, :, 0, :], lamv[:, :, :, 1, :], MUL))
            dve.tensor_reduce(col(LSUM, 4), lamp, AX.X, ADD).then_inc(lam_ready, 1)
            dve.wait_ge(loads, 32)
            for n in range(2):
                for th in range(TH):
                    gained(0, n, th)
            dve.wait_ge(lam_exp, 1)
            le = col(LEXP, 4).rearrange("p (l a) -> p l a", l=2)
            own.step(tt(col(NLAM, 2), le[:, :, 1], le[:, :, 0], SUB))
            for l in range(2):
                lam_init = 0.8 - 0.6 * math.exp(-0.3 * l)
                own.step(ts(col(NLAM + l), col(NLAM + l), -lam_init, None, ADD))
                own.step(ts(subln[:, l, :], subln[:, l, :], 1.0 - lam_init, None, MUL))
            quarters(0, "x", 0)
            dve.wait_ge(act_par, 2)
            a_re, a_im, co_re, co_im, cos, sin, rad2 = (row(PACK + i) for i in range(7))
            own.step(tt(row(R_t), row(R_sh), row(R_sh), MUL))
            own.step(ts(cos, row(R_t), -2.0, 1.0, MUL, ADD))
            own.step(dve.tensor_copy(sin, row(R_sn)))
            own.step(tt(a_re, row(R_er), cos, MUL))
            own.step(tt(a_im, row(R_er), sin, MUL))
            own.step(tt(rad2, row(R_er), row(R_er), MUL))
            split_static(0)
            own.step(tt(row(R_t), row(R_LR), row(R_LR), MUL))
            own.step(tt(row(R_u), row(R_LI), row(R_LI), MUL))
            own.step(tt(row(R_t), row(R_t), row(R_u), ADD))
            own.step(dve.reciprocal(row(R_den), row(R_t)))
            own.step(ts(row(R_am), a_re, -1.0, None, ADD))
            own.step(tt(row(R_t), row(R_am), row(R_LR), MUL))
            own.step(tt(row(R_u), a_im, row(R_LI), MUL))
            own.step(tt(row(R_t), row(R_t), row(R_u), ADD))
            own.step(tt(co_re, row(R_t), row(R_den), MUL))
            own.step(tt(row(R_t), a_im, row(R_LR), MUL))
            own.step(tt(row(R_u), row(R_am), row(R_LI), MUL))
            own.step(tt(row(R_t), row(R_t), row(R_u), SUB))
            tt(co_im, row(R_t), row(R_den), MUL).then_inc(dve_par, 1)
            quarters(0, "x", 1)
            split_static(1)
            bank = wait_turn(dve, "par")
            dve.tensor_copy(par[:, :, :].rearrange("p i j -> p (i j)"), bank[:, 0:448]).then_inc(tr_free[TURN["par"] % 2], 1)
            mixer(0)

            def hidden2(g, tr, first):
                for th in range(TH):
                    dve.wait_ge(g_ready, g + th)
                    if not first:
                        dve.wait_ge(ht_tr, tr)
                    stt(v_flat[:, (2 + th) * FC:(3 + th) * FC], v_flat[:, th * FC:(th + 1) * FC], col(RI + th),
                        PJ[th][:, FC:2 * FC], MUL, MUL).then_inc(h_done, 1)

            def hidden_lo(n, cols):
                dve.wait_ge(ht_hi_ready, n)
                tt(ht_lo[:, :, 0:cols], TR[0][:, 0:2 * cols].rearrange("p (f s) -> p f s", f=2),
                   ht_hi[:, :, 0:cols].bitcast(f32), SUB).then_inc(ht_lo_ready, 1)

            t = T_FFN0

            def split_turn(i, tile):
                split(tile, (t + 2 + i) % 3, raw[:, raw_slot(t + 2 + i), :])
            split_turn(0, t + 2)
            hidden2(1, 0, True)
            split_turn(1, t + 3)
            split_turn(2, t + 4)
            hidden_lo(1, SEQ)
            with dve.Fori(1, NCH - 1) as c:
                split_turn(0, c * 3 + (t + 2))
                hidden2(c * 2 + 1, c, False)
                split_turn(1, c * 3 + (t + 3))
                split_turn(2, c * 3 + (t + 4))
                hidden_lo(c + 1, SEQ)
            hidden2(2 * NCH - 1, NCH - 1, False)
            split_static(T_MIX1 - 1)
            hidden_lo(NCH, SEQ)
            split_static(T_MIX1)
            split_static(T_MIX1 + 1)
            mixer(1)

            for th in range(TH):
                ts(xn[:, th, :], xn[:, th, :], col(RI + th), None, MUL).then_inc(xn_scaled, 1)
            bank = wait_turn(dve, "router")
            sums = bank[:, 0:32].rearrange("p (t i e) -> p t i e", t=2, i=2)
            own.step(dve.tensor_copy(r_tmp, sums[:, :, 0, :]))
            tt(r_logit, r_tmp, sums[:, :, 1, :], ADD).then_inc(tr_free[TURN["router"] % 2], 1)
            wait_read(dve, "router")
            for th in range(TH):
                own.step(dve.max(r_best[:, th, :], r_logit[:, th, :]))
                own.step(dve.max_index(r_index[:, th, :], r_best[:, th, :], r_logit[:, th, :]))
            own.step(tt(r_diff, r_best[:, :, 1], r_best[:, :, 0], SUB))
            tt(r_diff, r_diff, col(RI, 2), MUL).then_inc(sel_early, 1)
            own.step(dve.tensor_copy(r_indexf, r_index[:, :, 0:2]))
            experts_row = cst[:, C_IOTA:C_IOTA + NE]
            own.step(tt(r_hot, experts_row.unsqueeze(1).unsqueeze(1).broadcast_to([P, 2, 2, NE]),
                        r_indexf.rearrange("p t i -> p i t").unsqueeze(3).broadcast_to([P, 2, 2, NE]), ALU.is_equal))
            tt(sel, r_hot[:, 0, :, :], r_hot[:, 1, :, :], ADD).then_inc(sel_ready, 1)
            own.step(dve.memset(cols, 0.0))
            own.step(dve.memset(cols[:, 0, :, :], -1000.0))
            dve.wait_ge(gate_exp, 1)
            own.step(ts(r_g, r_exp, 1.0, None, ADD))
            own.step(dve.reciprocal(r_g, r_g))
            own.step(tt(r_exp, r_exp, r_g, MUL))
            for i, g in enumerate((r_g, r_exp)):
                own.step(tt(r_hot[:, i, :, :], r_hot[:, i, :, :], g.unsqueeze(2).broadcast_to([P, 2, NE]), MUL))
            own.step(tt(cols[:, 1, :, 0:NE], r_hot[:, 0, :, :], r_hot[:, 1, :, :], ADD))
            bank = wait_turn(dve, "pos")
            pos = bank[:, 0:16].rearrange("p (t e) -> p t e", t=2)
            own.step(stt(r_pos, pos, 1.0, sel, ADD, MUL))
            own.step(ts(cols[:, 0, :, 0:NE], r_pos, -1.0, None, ADD))
            ts(r_over, bank[:, 16:24], float(P), None, ALU.is_gt).then_inc(tr_free[TURN["pos"] % 2], 1)
            wait_read(dve, "pos")
            def places():
                for th in range(TH):
                    m = ts(place[:, th, :], cst[:, C_IOTA:C_IOTA + P], column[:, 0, th:th + 1], None, ALU.is_equal)
                return m

            def gathered(n):
                dve.wait_ge(xe_hi_ready, n)
                for g in range(2):
                    m = tt(at_lo[:, 4 * g:4 * g + 4, 0:P], banks[4 + g][:, :].rearrange("p (k c) -> p k c", k=4),
                           at_hi[:, 4 * g:4 * g + 4, 0:P].bitcast(f32), SUB)
                m.then_inc(xe_lo_ready, 1)

            own.step(dve.tensor_copy(column, cols[:, :, :, 0]))
            places().then_inc(place_ready, 1)
            own.step(dve.tensor_tensor_scan(r_rank, cst[:, C_ONE:C_ONE + NE], r_over, 0.0, MUL, ADD))
            own.step(ts(r_tab[:, 0:1], r_rank[:, NE - 1:NE], float(NE - 1), None, ADD))
            own.step(dve.memset(r_tab[:, 1:2], float(NE - 1)))
            own.step(ts(r_pos, cols[:, 0, :, 0:NE], 1000.0 - P, None, ADD))
            for k in range(MAXB - NE):
                own.step(stt(r_one, r_rank, float(k + 1), r_over, ALU.is_equal, MUL))
                own.step(tt(r_tmp[:, 0, :], r_one, experts_row, MUL))
                own.step(dve.tensor_reduce(r_tab[:, k + 2:k + 3], r_tmp[:, 0, :], AX.X, ADD))
                one = r_one.unsqueeze(1).broadcast_to([P, 2, NE])
                own.step(tt(r_tmp, r_pos, one, MUL))
                own.step(dve.tensor_reduce(cols[:, 0, :, NE + k], r_tmp, AX.X, ADD))
                own.step(ts(cols[:, 0, :, NE + k], cols[:, 0, :, NE + k], -1000.0, None, ADD))
                own.step(tt(r_tmp, cols[:, 1, :, 0:NE], one, MUL))
                own.step(dve.tensor_reduce(cols[:, 1, :, NE + k], r_tmp, AX.X, ADD))
            dve.tensor_copy(table[:, :], r_tab).then_inc(routed, 1)
            gathered(1)

            def hidden(b, c):
                dve.wait_ge(g_ready, b * NCH + (2 * NCH + c + 1))
                dve.wait_ge(ht_tr, b * NCH + (NCH + c))
                tt(v_flat[:, FC:2 * FC], v_flat[:, 0:FC], h_bank(c)[:, FC:2 * FC], MUL).then_inc(h_done, 1)

            def result_lo(b):
                dve.wait_ge(ye_hi_ready, b + 1)
                for n in range(2):
                    m = stt(at_lo[:, 4 * n:4 * n + 4, P:2 * P], PY[n][:, :].rearrange("p (k c) -> p k c", k=4), place_gate,
                            at_hi[:, 4 * n:4 * n + 4, P:2 * P].bitcast(f32), MUL, SUB)
                m.then_inc(ye_ready, 1)

            def add_block(b):
                for i, bank in enumerate(comb_banks):
                    n, th = i // 2, i % 2
                    z = xres[:, th, n * 512:(n + 1) * 512]
                    dve.wait_ge(comb_full, b * 4 + (i + 1))
                    tt(z, z, bank[:, :], ADD).then_inc(x_added, 1)

            def expert_step(b, c, final=False):
                if c == NCH:
                    result_lo(b)
                if c >= 0:
                    split_moe(b, FFN_TILES - 1 if final and c == NCH - 1 else 3 * c + 4)
                    hidden_lo(b * NCH + (NCH + c + 1), P)
                if not (final and c + 2 >= NCH):
                    split_moe(b, 3 * c + 5)
                if not (final and c + 1 >= NCH):
                    hidden(b, c + 1)
                if c == 5 and not final:
                    dve.wait_ge(gt_ready, b + 1)
                    own.step(dve.tensor_copy(column, cols[:, :, :, bass.ds(b + 1, 1)].rearrange("p a t o -> p a (t o)")))
                    places().then_inc(place_ready, 1)
                if c == NCH - 2 and not final:
                    gathered(b + 2)
                if not (final and c + 2 >= NCH):
                    split_moe(b, 3 * c + 6)
                if c == NCH:
                    add_block(b)

            expert_step(0, -1)
            expert_step(0, 0)
            dve.wait_ge(routed, 1)
            last = dve.value_load(table[0:1, 0:1], min_val=NE - 1, max_val=MAXB - 1)
            with dve.Fori(0, last) as b:
                own.loop(b, 1)
                for c in range(1, NCH + 1):
                    expert_step(b, c)
                own.end()
            for c in range(1, NCH):
                expert_step(last, c, True)
            result_lo(last)
            add_block(last)
            inverses(4)
            dve.wait_ge(inv_ready, 5)
            dve.wait_ge(gain_in, 80)
            for th in range(TH):
                stt(xn[:, th, :], xres[:, th, :], col(RI + th), gain, MUL, MUL).then_inc(final_ready, 1)

        @block.gpsimd
        def _(pool):
            own = Order(pool, pool_own)
            tt = pool.tensor_tensor

            def cmul(out_re, out_im, a, a_swapped, b_re, b_im, t1, t2):
                tt(t1, a, b_re, MUL)
                own.step(tt(t2, a_swapped, b_im, MUL))
                tt(out_re, t1[:, 0], t2[:, 0], SUB)
                own.step(tt(out_im, t1[:, 1], t2[:, 1], ADD))

            def load_matrices(l):
                for r, src in enumerate((ssm_b_re, ssm_b_im)):
                    v = src[l, :, :, :, :].rearrange("d g s h -> (d g) s h").rearrange("(j g) s h -> g s j h", g=2)
                    for g in range(2):
                        pool.dma_start(braw[64 * g:64 * (g + 1), r, :, :], v[g, :, :, :]).then_inc(bc_in, 16)
                for r, src in enumerate((ssm_c_re, ssm_c_im)):
                    for a in range(2):
                        pool.dma_start(craw[r][:, :, a, :], src[l, :, :, :, :].rearrange("d g h s -> (d g h) s")
                                       .rearrange("(i p) s -> p i s", p=P)).then_inc(bc_in, 16)

            def load_dskip(l):
                for q2 in range(2):
                    for t in range(2):
                        r0 = q2 * 64 + t * 32
                        pool.dma_start(dskip[r0:r0 + 32, l, :],
                                       ssm_d[l, :].rearrange("(b q c) -> q c b", b=8, q=2)[q2, :, :],
                                       allow_slow_non_contiguous=True).then_inc(dskip_in, 16)

            def signal_mats():
                pool.memset(zero_mark, 0.0).then_inc(mats_ready, 1)

            def phasors(l):
                j0 = 32 * l
                t1, t2 = area(TMP, 512), area(TMP + 512, 512)
                sq = [area(TMP + 1024 + 64 * i, 64).rearrange("p (r j) -> p r j", r=2) for i in range(2)]

                def small_t(t, n):
                    return t[:, 0:64 * n].rearrange("p (r j n) -> p r j n", r=2, j=32)

                def square(dst, src):
                    s1, s2 = (small_t(t, 1)[:, :, :, 0] for t in (t1, t2))
                    cmul(dst[:, 0, :], dst[:, 1, :], src, src[:, ::-1, :], src[:, 0:1, :].broadcast_to([P, 2, 32]),
                         src[:, 1:2, :].broadcast_to([P, 2, 32]), s1, s2)
                square(sq[0], par[:, COS:SIN + 1, j0:j0 + 32])
                power = 0
                for tab, n in ((w1t, 16), (w16t, 8)):
                    pool.memset(tab[:, 0, :, 0:1], 1.0)
                    pool.memset(tab[:, 1, :, 0:1], 0.0)
                    own.step(pool.tensor_copy(tab[:, :, :, 1], sq[power % 2]))
                    k = 2
                    while k < n:
                        square(sq[(power + 1) % 2], sq[power % 2])
                        power += 1
                        p = sq[power % 2]
                        a = tab[:, :, :, 0:k]
                        cmul(tab[:, 0, :, k:2 * k], tab[:, 1, :, k:2 * k], a, a[:, ::-1, :, :],
                             p[:, 0:1, :].unsqueeze(3).broadcast_to([P, 2, 32, k]),
                             p[:, 1:2, :].unsqueeze(3).broadcast_to([P, 2, 32, k]), small_t(t1, k), small_t(t2, k))
                        k *= 2
                    square(sq[(power + 1) % 2], sq[power % 2])
                    power += 1

            def build(l):
                j0 = 32 * l

                def num(i):
                    return par[:, i, j0:j0 + 32]

                def times(dst, src, re, im):
                    cmul(dst[:, 0], dst[:, 1], src, src[:, ::-1, :, :],
                         num(re).unsqueeze(1).unsqueeze(3).broadcast_to([P, 2, 32, GC]),
                         num(im).unsqueeze(1).unsqueeze(3).broadcast_to([P, 2, 32, GC]), bt1, bt2)
                if l == 1:
                    pool.memset(gflat, 0.0)
                pool.wait_ge(bc_in, BC_LOADS * (l + 1))
                times(bbar, braw, CO_RE, CO_IM)
                times(babar, bbar, A_RE, A_IM)
                signal_mats()
                wait_read(pool, (l, "ct", 2))
                wait_read(pool, (l, "ct", 3))
                times(cabar, ctr, A_RE, A_IM)
                signal_mats()

            def phase_products(l, q):
                if 16 * l + q > 0:
                    pool.wait_ge(wtab_ready, 16 * l + q)
                if 16 * l + q >= 2:
                    pool.wait_ge(pv_free, 16 * l + q - 1)
                    pool.wait_ge(zs_used, 16 * l + q - 1)
                for dst, (r1, r16) in zip([wtab[q % 2][:, 0, :]] + php, ((0, 0), (1, 1), (0, 1), (1, 0))):
                    m = phase_product(tt, dst, l, q, r1, r16)
                m.then_inc(php_ready, 1)

            def turn_forward(l, q):
                n = 16 * l + q
                w, xs = wtab[q % 2], xst_flat[q % 2]
                pool.wait_ge(wtab_ready, n + 1)
                pool.wait_ge(zs_ready, n + 1)
                if n > 0:
                    pool.wait_ge(states_ready, n)
                for po, z, r in ((po1, zs, 0), (po2, zs[:, ::-1, :], 1)):
                    for d in range(2):
                        half = slice(d * P, (d + 1) * P)
                        dst = po[:, :, 0:P] if d == 0 else po[:, :, 2 * P - 1:P - 1:-1]
                        m = tt(dst, z[:, :, half], w[:, r:r + 1, half].broadcast_to([P, 2, P]), MUL)
                m.then_inc(zs_used, 1)
                pool.wait_ge(zs_used, n + 1)
                if n >= 2:
                    pool.wait_ge(y_done, n - 1)
                tt(xs[:, 0, 1:2 * P + 1], po1[:, 0, :], po2[:, 0, :], SUB)
                tt(xs[:, 1, 1:2 * P + 1], po1[:, 1, :], po2[:, 1, :], ADD).then_inc(states_ready, 1)

            load_matrices(0)
            load_dskip(0)
            load_dskip(1)
            pool.memset(area(4096, 4096), 0.0)
            wait_read(pool, "par")
            for l in range(2):
                if l == 1:
                    pool.wait_ge(y_done, PAIRS)
                    load_matrices(1)
                    pool.wait_ge(at_lo_ready, at_count(0, "m", 3))
                    phasors(1)
                build(l)
                if l == 0:
                    pool.wait_ge(b_laid, 2)
                    phasors(0)
                pool.wait_ge(blocks_ready, l + 1)
                pool.wait_ge(mats_ready, 2 * l + 2)
                for xs in xst:
                    pool.memset(xs[:, :, 0, 0:1], 0.0)
                    pool.memset(xs[:, :, 1, P:P + 1], 0.0)
                phase_products(l, 0)
                for q in range(PAIRS):
                    if q + 1 < PAIRS:
                        phase_products(l, q + 1)
                    turn_forward(l, q)


_INS = ["x", "norm_mix", "w_in", "attn_lambda", "attn_subln", "ssm_lam_re", "ssm_lam_im", "ssm_log_dt", "ssm_b_re",
        "ssm_b_im", "ssm_c_re", "ssm_c_im", "ssm_d", "w_glu", "w_branch", "w_out", "norm_ffn", "ffn_w1", "ffn_w3",
        "ffn_w2", "moe_router", "moe_w1", "moe_w3", "moe_w2", "norm_final"]


def shape_constants():
    import numpy as np
    c = np.zeros((P, C_END), np.float32)
    c[:, C_ID:C_ID + P] = np.eye(P)
    c[:, C_TRI:C_TRI + P] = np.triu(np.ones((P, P)), 1)
    c[:, C_ONE:C_ONE + P] = 1.0
    c[:, C_IOTA:C_IOTA + P] = np.arange(P)
    c[:, C_MASK:C_MASK + P] = np.arange(P) > 0
    c[:, C_PAT:C_PAT + 32] = (np.arange(P)[:, None] % 32) == np.arange(32)
    half = HD // 2
    freq = (1.0 / (np.float32(10000.0) ** (np.arange(half, dtype=np.float32) / np.float32(half)))).astype(np.float32)
    pos = (2 * np.arange(P)[:, None] + np.arange(TH)).astype(np.float32)
    ang = (pos[:, :, None] * freq).astype(np.float32).astype(np.float64)
    c[:, C_COS:C_COS + P] = np.concatenate([np.cos(ang), np.cos(ang)], -1).reshape(P, P)
    c[:, C_SIN:C_SIN + P] = np.concatenate([-np.sin(ang), np.sin(ang)], -1).reshape(P, P)
    return c


def kernel(**inputs):
    import numpy as _np
    import concourse.bacc as _bacc
    from concourse import mybir as _mybir
    from concourse.bass_utils import run_bass_kernel_spmd as _run

    nc = _bacc.Bacc("TRN2", target_bir_lowering=False, num_devices=1)
    arrays, args = {}, []
    for name in _INS + ["consts"]:
        a = shape_constants() if name == "consts" else _np.ascontiguousarray(inputs[name])
        arrays[f"in_{name}_dram"] = a
        args.append(nc.dram_tensor(f"in_{name}_dram", a.shape, _mybir.dt.from_np(a.dtype), kind="ExternalInput").ap())
    args.append(nc.dram_tensor("out_0_dram", (1, SEQ, D), _mybir.dt.float32, kind="ExternalOutput").ap())
    build(nc, *args)
    r = _run(nc, [arrays], core_ids=[0])
    return r.results[0]["out_0_dram"]
```
